# Optimizing a Trainium2 kernel written in Bass

```python
import jax, jax.numpy as jnp
from jax import lax
import numpy as np
import math

D_MODEL = 1024
BATCH = 1
SEQ = 256
DEPTH = 2

CONV_WIDTH = D_MODEL // 2
CONV_HEADS = 8
CONV_K = 3
POOL_WIDTH = D_MODEL // 2
POOL_WINDOWS = (2, 4, 8, 16)
POOL_GROUPS = len(POOL_WINDOWS)
POOL_GROUP_DIM = POOL_WIDTH // POOL_GROUPS
MIX_WIDTH = CONV_WIDTH + POOL_WIDTH
IN_COLS = 4 * CONV_WIDTH + 2 * POOL_WIDTH
NORM_EPS = 1e-6


def rms_norm(x, g):
    xf = x.astype(jnp.float32)
    y = xf * lax.rsqrt(jnp.mean(xf * xf, axis=-1, keepdims=True) + NORM_EPS)
    return (y * g.astype(jnp.float32)).astype(x.dtype)

def causal_depthwise_conv(z, w):
    C = z.shape[-1]
    return lax.conv_general_dilated(
        z, w[:, None, :].astype(z.dtype),
        window_strides=(1,), padding=[(CONV_K - 1, 0)],
        dimension_numbers=("NWC", "WIO", "NWC"),
        feature_group_count=C)

def causal_multiscale_pool(p, w_pool, pool_scale):
    B, T, _ = p.shape
    pf = p.astype(jnp.float32)
    pos = jnp.arange(1, T + 1, dtype=jnp.float32)[None, :, None]
    outs = []
    for g, w in enumerate(POOL_WINDOWS):
        pg = pf[..., g * POOL_GROUP_DIM:(g + 1) * POOL_GROUP_DIM]
        s = jnp.cumsum(pg, axis=1)
        lag = jnp.pad(s, ((0, 0), (w, 0), (0, 0)))[:, :T]
        mean = (s - lag) / jnp.minimum(pos, float(w))
        outs.append(mean - pg)
    pooled = jnp.stack(outs, axis=2).astype(p.dtype)
    mixed = jnp.einsum("btgc,gcd->btgd", pooled, w_pool)
    return mixed.reshape(B, T, POOL_WIDTH) * pool_scale

def first_inputs(seed: int = 0) -> dict:
    key = jax.random.key(seed)
    ks = jax.random.split(key, 12)
    f32 = jnp.float32
    x = jax.random.normal(ks[0], (BATCH, SEQ, D_MODEL), f32)
    c = jax.random.normal(ks[1], (BATCH, D_MODEL), f32)
    w_ada = jax.random.normal(ks[2], (DEPTH, D_MODEL, 3 * D_MODEL), f32) * D_MODEL ** -0.5
    b_ada = 0.01 * jax.random.normal(ks[3], (DEPTH, 3 * D_MODEL), f32)
    g_pre = 1.0 + 0.02 * jax.random.normal(ks[4], (DEPTH, D_MODEL), f32)
    w_in = jax.random.normal(ks[5], (DEPTH, D_MODEL, IN_COLS), f32) * D_MODEL ** -0.5
    w_conv = jax.random.normal(ks[6], (DEPTH, CONV_K, CONV_WIDTH), f32) * CONV_K ** -0.5
    w_pool = jax.random.normal(ks[7], (DEPTH, POOL_GROUPS, POOL_GROUP_DIM, POOL_GROUP_DIM), f32) * POOL_GROUP_DIM ** -0.5
    pool_scale = 1.0 + 0.1 * jax.random.normal(ks[8], (DEPTH, POOL_WIDTH), f32)
    w_out = jax.random.normal(ks[9], (DEPTH, MIX_WIDTH, D_MODEL), f32) * MIX_WIDTH ** -0.5
    g_post = 1.0 + 0.02 * jax.random.normal(ks[10], (DEPTH, D_MODEL), f32)
    return {"x": x, "c": c, "w_ada": w_ada, "b_ada": b_ada, "g_pre": g_pre, "w_in": w_in,
            "w_conv": w_conv, "w_pool": w_pool, "pool_scale": pool_scale,
            "w_out": w_out, "g_post": g_post}

def first_block(x, c, w_ada, b_ada, g_pre, w_in, w_conv, w_pool, pool_scale, w_out, g_post):
    B, T, D = x.shape
    c_act = jax.nn.silu(c)
    cw = CONV_WIDTH
    for l in range(DEPTH):
        mod = c_act @ w_ada[l] + b_ada[l]
        shift, scale, gate = jnp.split(mod, 3, axis=-1)
        h = rms_norm(x, g_pre[l]) * (1.0 + scale[:, None, :]) + shift[:, None, :]
        proj = h @ w_in[l]
        u_a = proj[..., 0 * cw:1 * cw]
        b_a = proj[..., 1 * cw:2 * cw]
        c_a = proj[..., 2 * cw:3 * cw]
        gate_a = proj[..., 3 * cw:4 * cw]
        o = 4 * cw
        u_p = proj[..., o:o + POOL_WIDTH]
        gate_p = proj[..., o + POOL_WIDTH:o + 2 * POOL_WIDTH]
        y_a = b_a * causal_depthwise_conv(c_a * u_a, w_conv[l]) * jax.nn.silu(gate_a)
        y_p = causal_multiscale_pool(u_p, w_pool[l], pool_scale[l]) * jax.nn.silu(gate_p)
        y = jnp.concatenate([y_a, y_p], axis=-1) @ w_out[l]
        x = x + gate[:, None, :] * rms_norm(y, g_post[l])
    return x


N_MIXERS = 4
HEAD_DIM = 64
Q_BLOCK = 128
D_FF = 2816
EPS = 1e-6
NEG = -1e30
FORCE = 1e9

NSA_HQ = 16
NSA_HKV = 4
CMP_BLOCK = 32
CMP_STRIDE = 16
CMP_HIDDEN = 256
SEL_BLOCK = 64
SEL_TOPK = 16
NSA_WINDOW = 512
NSA_IN = NSA_HQ * HEAD_DIM + 6 * NSA_HKV * HEAD_DIM + 3 * NSA_HQ

DIFF_H = 8
DIFF_IN = 3 * DIFF_H * 2 * HEAD_DIM

GDN_H = 8
GDN_DK = 128
GDN_DV = 128
GDN_CONV = 4
GDN_CHUNK = 64
GDN_QKV = GDN_H * (2 * GDN_DK + GDN_DV)
GDN_IN = GDN_QKV + 2 * GDN_H + GDN_H * GDN_DV

SWA_HQ = 16
SWA_HKV = 4
SWA_WINDOW = 128
SWA_IN = (SWA_HQ + 2 * SWA_HKV) * HEAD_DIM


f32 = jnp.float32

def rmsnorm(x, g):
    xf = x.astype(f32)
    y = xf * lax.rsqrt(jnp.mean(xf * xf, axis=-1, keepdims=True) + EPS)
    return (y * g.astype(f32)).astype(x.dtype)

def l2norm(x):
    xf = x.astype(f32)
    return xf * lax.rsqrt(jnp.sum(xf * xf, axis=-1, keepdims=True) + EPS)

def swiglu(x, w_in, w_out):
    a, b = jnp.split(x @ w_in, 2, axis=-1)
    return (jax.nn.silu(a) * b) @ w_out

def alibi_slopes(n):
    return 2.0 ** (-8.0 * jnp.arange(1, n + 1, dtype=f32) / n)

def masked_softmax(s, mask):
    return jax.nn.softmax(jnp.where(mask, s, NEG), axis=-1) * mask

def banded_attention(q, k, v, slopes, window, sinks=None):
    B, Hkv, G, S, dh = q.shape
    nb = S // Q_BLOCK
    span = window + Q_BLOCK
    pad = ((0, 0), (0, 0), (window, 0), (0, 0))
    kp, vp = jnp.pad(k, pad), jnp.pad(v, pad)
    qb = q.reshape(B, Hkv, G, nb, Q_BLOCK, dh).transpose(3, 0, 1, 2, 4, 5)
    scale = dh ** -0.5

    def block(args):
        qi, i = args
        start = i * Q_BLOCK
        ki = lax.dynamic_slice_in_dim(kp, start, span, axis=2)
        vi = lax.dynamic_slice_in_dim(vp, start, span, axis=2)
        t = start + jnp.arange(Q_BLOCK)
        s_pos = start - window + jnp.arange(span)
        dist = t[:, None] - s_pos[None, :]
        mask = (dist >= 0) & (dist < window) & (s_pos[None, :] >= 0)
        sc = jnp.einsum('bhgtd,bhsd->bhgts', qi, ki).astype(f32) * scale \
            - slopes[:, :, None, None] * dist
        if sinks is None:
            p = masked_softmax(sc, mask)
        else:
            sink = jnp.broadcast_to(sinks.astype(f32)[:, :, None, None], sc.shape[:-1] + (1,))
            p = jax.nn.softmax(jnp.concatenate([jnp.where(mask, sc, NEG), sink], axis=-1), axis=-1)[..., :-1]
        return jnp.einsum('bhgts,bhsd->bhgtd', p.astype(v.dtype), vi)

    o = lax.map(block, (qb, jnp.arange(nb)))
    return o.transpose(1, 2, 3, 0, 4, 5).reshape(B, Hkv, G, S, dh)

def compress_blocks(t, pos, w1, w2):
    B, H, S, dh = t.shape
    ratio = CMP_BLOCK // CMP_STRIDE
    n_sub = S // CMP_STRIDE
    n_cmp = n_sub - ratio + 1
    sub = t.reshape(B, H, n_sub, CMP_STRIDE, dh)
    blocks = jnp.concatenate([sub[:, :, r:r + n_cmp] for r in range(ratio)], axis=3)
    blocks = (blocks + pos).reshape(B, H, n_cmp, CMP_BLOCK * dh)
    return jax.nn.gelu(blocks @ w1) @ w2

def nsa_compressed_selected(q, kc, vc, ks, vs, slopes):
    B, Hkv, G, S, dh = q.shape
    nb = S // Q_BLOCK
    n_cmp = kc.shape[2]
    n_sel = S // SEL_BLOCK
    n_top = min(SEL_TOPK, n_sel)
    scale = dh ** -0.5
    cmp_start = jnp.arange(n_cmp) * CMP_STRIDE
    cmp_end = cmp_start + CMP_BLOCK - 1
    sel_start = jnp.arange(n_sel) * SEL_BLOCK
    overlap = ((cmp_start[:, None] < sel_start[None, :] + SEL_BLOCK)
               & (cmp_start[:, None] + CMP_BLOCK > sel_start[None, :])).astype(f32)
    ksb = ks.reshape(B, Hkv, n_sel, SEL_BLOCK, dh)
    vsb = vs.reshape(B, Hkv, n_sel, SEL_BLOCK, dh)
    gather = jax.vmap(jax.vmap(lambda tb, idx: tb[idx]))
    qb = q.reshape(B, Hkv, G, nb, Q_BLOCK, dh).transpose(3, 0, 1, 2, 4, 5)
    jsel = jnp.arange(n_sel)

    def block(args):
        qi, i = args
        t = i * Q_BLOCK + jnp.arange(Q_BLOCK)
        dist_c = t[:, None] - cmp_end[None, :]
        sc = jnp.einsum('bhgtd,bhnd->bhgtn', qi, kc).astype(f32) * scale \
            - slopes[:, :, None, None] * dist_c
        p_c = masked_softmax(sc, dist_c >= 0)
        o_cmp = jnp.einsum('bhgtn,bhnd->bhgtd', p_c.astype(vc.dtype), vc)
        imp = jnp.einsum('bhgtn,ns->bhts', p_c, overlap)
        cur = t // SEL_BLOCK
        forced = (jsel[None, :] == 0) | (jsel[None, :] == cur[:, None]) | (jsel[None, :] == cur[:, None] - 1)
        causal = jsel[None, :] <= cur[:, None]
        imp = jnp.where(forced, FORCE, jnp.where(causal, imp, -jnp.inf))
        _, idx = lax.top_k(imp, n_top)
        kg = gather(ksb, idx).reshape(B, Hkv, Q_BLOCK, n_top * SEL_BLOCK, dh)
        vg = gather(vsb, idx).reshape(B, Hkv, Q_BLOCK, n_top * SEL_BLOCK, dh)
        kpos = (idx[..., None] * SEL_BLOCK + jnp.arange(SEL_BLOCK)).reshape(B, Hkv, Q_BLOCK, n_top * SEL_BLOCK)
        dist_s = (t[None, None, :, None] - kpos)[:, :, None]
        ss = jnp.einsum('bhgtd,bhtkd->bhgtk', qi, kg).astype(f32) * scale \
            - slopes[:, :, None, None] * dist_s
        p_s = masked_softmax(ss, dist_s >= 0)
        o_sel = jnp.einsum('bhgtk,bhtkd->bhgtd', p_s.astype(vs.dtype), vg)
        return o_cmp, o_sel

    o_cmp, o_sel = lax.map(block, (qb, jnp.arange(nb)))
    back = lambda o: o.transpose(1, 2, 3, 0, 4, 5).reshape(B, Hkv, G, S, dh)
    return back(o_cmp), back(o_sel)

def nsa_mixer(h, w_in, w_out, q_norm, k_norm, cmp_pos, cmp_w1, cmp_w2):
    B, S, _ = h.shape
    G = NSA_HQ // NSA_HKV
    dh = HEAD_DIM
    splits = np.cumsum([NSA_HQ * dh] + [NSA_HKV * dh] * 6).tolist()
    q, kc, vc, ks, vs, kw, vw, gates = jnp.split(h @ w_in, splits, axis=-1)
    q = rmsnorm(q.reshape(B, S, NSA_HKV, G, dh), q_norm).transpose(0, 2, 3, 1, 4)
    heads = lambda t: t.reshape(B, S, NSA_HKV, dh).transpose(0, 2, 1, 3)
    kc = rmsnorm(compress_blocks(heads(kc), cmp_pos[0], cmp_w1[0], cmp_w2[0]), k_norm[0])
    vc = compress_blocks(heads(vc), cmp_pos[1], cmp_w1[1], cmp_w2[1])
    ks, vs = rmsnorm(heads(ks), k_norm[1]), heads(vs)
    kw, vw = rmsnorm(heads(kw), k_norm[2]), heads(vw)
    slopes = alibi_slopes(NSA_HQ).reshape(NSA_HKV, G)
    o_cmp, o_sel = nsa_compressed_selected(q, kc, vc, ks, vs, slopes)
    o_win = banded_attention(q, kw, vw, slopes, NSA_WINDOW)
    g = jax.nn.sigmoid(gates.reshape(B, S, NSA_HKV, G, 3).transpose(0, 2, 3, 1, 4))
    o = g[..., 0:1] * o_cmp + g[..., 1:2] * o_sel + g[..., 2:3] * o_win
    return o.transpose(0, 3, 1, 2, 4).reshape(B, S, NSA_HQ * dh) @ w_out

def dense_diff_attention(q, k, v, slopes, lmbda):
    B, H, _, S, dh = q.shape
    nb = S // Q_BLOCK
    scale = dh ** -0.5
    qb = q.reshape(B, H, 2, nb, Q_BLOCK, dh).transpose(3, 0, 1, 2, 4, 5)
    s_pos = jnp.arange(S)

    def block(args):
        qi, i = args
        t = i * Q_BLOCK + jnp.arange(Q_BLOCK)
        dist = t[:, None] - s_pos[None, :]
        sc = jnp.einsum('bhctd,bhcsd->bhcts', qi, k).astype(f32) * scale \
            - slopes[:, None, None, None] * dist
        p = masked_softmax(sc, dist >= 0)
        a = p[:, :, 0] - lmbda * p[:, :, 1]
        return jnp.einsum('bhts,bhsd->bhtd', a.astype(v.dtype), v)

    o = lax.map(block, (qb, jnp.arange(nb)))
    return o.transpose(1, 2, 0, 3, 4).reshape(B, H, S, 2 * dh)

def diff_mixer(h, w_in, w_out, q_norm, k_norm, lam, subln, lam_init):
    B, S, _ = h.shape
    H, dh = DIFF_H, HEAD_DIM
    q, k, v = jnp.split(h @ w_in, 3, axis=-1)
    q = rmsnorm(q.reshape(B, S, H, 2, dh), q_norm).transpose(0, 2, 3, 1, 4)
    k = rmsnorm(k.reshape(B, S, H, 2, dh), k_norm).transpose(0, 2, 3, 1, 4)
    v = v.reshape(B, S, H, 2 * dh).transpose(0, 2, 1, 3)
    lf = lam.astype(f32)
    lmbda = jnp.exp(jnp.sum(lf[0] * lf[1])) - jnp.exp(jnp.sum(lf[2] * lf[3])) + lam_init
    o = dense_diff_attention(q, k, v, alibi_slopes(H), lmbda)
    o = rmsnorm(o, subln) * (1.0 - lam_init)
    return o.transpose(0, 2, 1, 3).reshape(B, S, H * 2 * dh) @ w_out

def causal_conv(x, w):
    K, C = w.shape
    return lax.conv_general_dilated(x, w[:, None, :], window_strides=(1,), padding=[(K - 1, 0)],
                                    dimension_numbers=('NWC', 'WIO', 'NWC'), feature_group_count=C)

def chunked_gated_delta(q, k, v, beta, g):
    B, S, H, dk = q.shape
    dv = v.shape[-1]
    C = GDN_CHUNK
    n = S // C
    ch = lambda t: jnp.moveaxis(t.astype(f32).reshape((B, n, C, H) + t.shape[3:]), 3, 1)
    q, k, v, beta, g = ch(q), ch(k), ch(v), ch(beta), ch(g)
    gc = jnp.cumsum(g, axis=-1)
    tril = jnp.tril(jnp.ones((C, C), bool))
    strict = jnp.tril(jnp.ones((C, C), bool), -1)
    decay = jnp.exp(jnp.where(tril, gc[..., :, None] - gc[..., None, :], -jnp.inf))
    kb = k * beta[..., None]
    A = jnp.where(strict, jnp.einsum('bhnid,bhnjd->bhnij', kb, k) * decay, 0.0)
    eye = jnp.eye(C, dtype=f32)
    T = lax.linalg.triangular_solve(eye + A, jnp.broadcast_to(eye, A.shape), left_side=True, lower=True)
    u = T @ (v * beta[..., None])
    w = T @ (kb * jnp.exp(gc)[..., None])
    attn = jnp.einsum('bhnid,bhnjd->bhnij', q, k) * decay
    qg = q * jnp.exp(gc)[..., None]
    kd = k * jnp.exp(gc[..., -1:] - gc)[..., None]
    glast = jnp.exp(gc[..., -1])

    def step(state, xs):
        qg_i, w_i, u_i, attn_i, kd_i, gl_i = xs
        v_new = u_i - w_i @ state
        o = qg_i @ state + attn_i @ v_new
        state = state * gl_i[..., None, None] + jnp.swapaxes(kd_i, -1, -2) @ v_new
        return state, o

    xs = tuple(jnp.moveaxis(t, 2, 0) for t in (qg, w, u, attn, kd, glast))
    _, o = lax.scan(step, jnp.zeros((B, H, dk, dv), f32), xs)
    return o.transpose(1, 0, 3, 2, 4).reshape(B, S, H, dv)

def gdn_mixer(h, w_in, w_out, conv_w, a_log, dt_bias, o_norm):
    B, S, _ = h.shape
    H, dk, dv = GDN_H, GDN_DK, GDN_DV
    qkv, b, a, gate = jnp.split(h @ w_in, [GDN_QKV, GDN_QKV + H, GDN_QKV + 2 * H], axis=-1)
    qkv = jax.nn.silu(causal_conv(qkv, conv_w))
    q, k, v = jnp.split(qkv, [H * dk, 2 * H * dk], axis=-1)
    q = l2norm(q.reshape(B, S, H, dk)) * dk ** -0.5
    k = l2norm(k.reshape(B, S, H, dk))
    v = v.reshape(B, S, H, dv)
    beta = jax.nn.sigmoid(b.astype(f32))
    log_alpha = -jnp.exp(a_log.astype(f32)) * jax.nn.softplus(a.astype(f32) + dt_bias.astype(f32))
    o = chunked_gated_delta(q, k, v, beta, log_alpha).astype(h.dtype)
    o = rmsnorm(o, o_norm) * jax.nn.silu(gate.reshape(B, S, H, dv))
    return o.reshape(B, S, H * dv) @ w_out

def swa_mixer(h, w_in, w_out, q_norm, k_norm, sinks):
    B, S, _ = h.shape
    G = SWA_HQ // SWA_HKV
    dh = HEAD_DIM
    q, k, v = jnp.split(h @ w_in, [SWA_HQ * dh, (SWA_HQ + SWA_HKV) * dh], axis=-1)
    q = rmsnorm(q.reshape(B, S, SWA_HKV, G, dh), q_norm).transpose(0, 2, 3, 1, 4)
    k = rmsnorm(k.reshape(B, S, SWA_HKV, dh), k_norm).transpose(0, 2, 1, 3)
    v = v.reshape(B, S, SWA_HKV, dh).transpose(0, 2, 1, 3)
    slopes = alibi_slopes(SWA_HQ).reshape(SWA_HKV, G)
    o = banded_attention(q, k, v, slopes, SWA_WINDOW, sinks.reshape(SWA_HKV, G))
    return o.transpose(0, 3, 1, 2, 4).reshape(B, S, SWA_HQ * dh) @ w_out

def second_inputs(seed: int = 0) -> dict:
    key = jax.random.key(seed)
    ks = iter(jax.random.split(key, 40))
    nrm = lambda shape, scale: jax.random.normal(next(ks), shape, f32) * scale
    gain = lambda shape: 1.0 + 0.02 * jax.random.normal(next(ks), shape, f32)
    n_of = lambda m: len(range(m, DEPTH, N_MIXERS))
    nA, nB, nC, nD = n_of(0), n_of(1), n_of(2), n_of(3)
    D, dh = D_MODEL, HEAD_DIM
    dt = jnp.exp(jax.random.uniform(next(ks), (nC, GDN_H), f32, math.log(1e-3), math.log(1e-1)))
    return {
        "x": jax.random.normal(next(ks), (BATCH, SEQ, D), f32),
        "ffn1_norm": gain((DEPTH, D)),
        "ffn1_w_in": nrm((DEPTH, D, 2 * D_FF), D ** -0.5),
        "ffn1_w_out": nrm((DEPTH, D_FF, D), D_FF ** -0.5),
        "mix_norm": gain((DEPTH, D)),
        "ffn2_norm": gain((DEPTH, D)),
        "ffn2_w_in": nrm((DEPTH, D, 2 * D_FF), D ** -0.5),
        "ffn2_w_out": nrm((DEPTH, D_FF, D), D_FF ** -0.5),
        "nsa_w_in": nrm((nA, D, NSA_IN), D ** -0.5),
        "nsa_w_out": nrm((nA, NSA_HQ * dh, D), (NSA_HQ * dh) ** -0.5),
        "nsa_q_norm": gain((nA, dh)),
        "nsa_k_norm": gain((nA, 3, dh)),
        "nsa_cmp_pos": nrm((nA, 2, CMP_BLOCK, dh), 0.02),
        "nsa_cmp_w1": nrm((nA, 2, CMP_BLOCK * dh, CMP_HIDDEN), (CMP_BLOCK * dh) ** -0.5),
        "nsa_cmp_w2": nrm((nA, 2, CMP_HIDDEN, dh), CMP_HIDDEN ** -0.5),
        "diff_w_in": nrm((nB, D, DIFF_IN), D ** -0.5),
        "diff_w_out": nrm((nB, DIFF_H * 2 * dh, D), (DIFF_H * 2 * dh) ** -0.5),
        "diff_q_norm": gain((nB, dh)),
        "diff_k_norm": gain((nB, dh)),
        "diff_lambda": nrm((nB, 4, dh), 0.1),
        "diff_subln": gain((nB, 2 * dh)),
        "gdn_w_in": nrm((nC, D, GDN_IN), D ** -0.5),
        "gdn_w_out": nrm((nC, GDN_H * GDN_DV, D), (GDN_H * GDN_DV) ** -0.5),
        "gdn_conv_w": nrm((nC, GDN_CONV, GDN_QKV), GDN_CONV ** -0.5),
        "gdn_a_log": jnp.log(jax.random.uniform(next(ks), (nC, GDN_H), f32, 1.0, 16.0)),
        "gdn_dt_bias": dt + jnp.log(-jnp.expm1(-dt)),
        "gdn_o_norm": gain((nC, GDN_DV)),
        "swa_w_in": nrm((nD, D, SWA_IN), D ** -0.5),
        "swa_w_out": nrm((nD, SWA_HQ * dh, D), (SWA_HQ * dh) ** -0.5),
        "swa_q_norm": gain((nD, dh)),
        "swa_k_norm": gain((nD, dh)),
        "swa_sinks": nrm((nD, SWA_HQ), 1.0),
    }

def second_block(x, ffn1_norm, ffn1_w_in, ffn1_w_out, mix_norm, ffn2_norm, ffn2_w_in, ffn2_w_out,
              nsa_w_in, nsa_w_out, nsa_q_norm, nsa_k_norm, nsa_cmp_pos, nsa_cmp_w1, nsa_cmp_w2,
              diff_w_in, diff_w_out, diff_q_norm, diff_k_norm, diff_lambda, diff_subln,
              gdn_w_in, gdn_w_out, gdn_conv_w, gdn_a_log, gdn_dt_bias, gdn_o_norm,
              swa_w_in, swa_w_out, swa_q_norm, swa_k_norm, swa_sinks):
    for layer in range(DEPTH):
        kind, j = layer % N_MIXERS, layer // N_MIXERS
        x = x + 0.5 * swiglu(rmsnorm(x, ffn1_norm[layer]), ffn1_w_in[layer], ffn1_w_out[layer])
        hn = rmsnorm(x, mix_norm[layer])
        if kind == 0:
            y = nsa_mixer(hn, nsa_w_in[j], nsa_w_out[j], nsa_q_norm[j], nsa_k_norm[j],
                          nsa_cmp_pos[j], nsa_cmp_w1[j], nsa_cmp_w2[j])
        elif kind == 1:
            lam_init = 0.8 - 0.6 * math.exp(-0.3 * layer)
            y = diff_mixer(hn, diff_w_in[j], diff_w_out[j], diff_q_norm[j], diff_k_norm[j],
                           diff_lambda[j], diff_subln[j], lam_init)
        elif kind == 2:
            y = gdn_mixer(hn, gdn_w_in[j], gdn_w_out[j], gdn_conv_w[j], gdn_a_log[j],
                          gdn_dt_bias[j], gdn_o_norm[j])
        else:
            y = swa_mixer(hn, swa_w_in[j], swa_w_out[j], swa_q_norm[j], swa_k_norm[j], swa_sinks[j])
        x = x + y
        x = x + 0.5 * swiglu(rmsnorm(x, ffn2_norm[layer]), ffn2_w_in[layer], ffn2_w_out[layer])
    return x


def setup_inputs(seed=0):
    out = dict(first_inputs(seed))
    for name, value in second_inputs(seed + 1).items():
        if name != "x":
            out[name + "_2"] = value
    return out


def reference(
    x, c, w_ada, b_ada, g_pre, w_in, w_conv, w_pool, pool_scale, w_out, g_post, ffn1_norm_2,
    ffn1_w_in_2, ffn1_w_out_2, mix_norm_2, ffn2_norm_2, ffn2_w_in_2, ffn2_w_out_2, nsa_w_in_2,
    nsa_w_out_2, nsa_q_norm_2, nsa_k_norm_2, nsa_cmp_pos_2, nsa_cmp_w1_2, nsa_cmp_w2_2,
    diff_w_in_2, diff_w_out_2, diff_q_norm_2, diff_k_norm_2, diff_lambda_2, diff_subln_2,
    gdn_w_in_2, gdn_w_out_2, gdn_conv_w_2, gdn_a_log_2, gdn_dt_bias_2, gdn_o_norm_2, swa_w_in_2,
    swa_w_out_2, swa_q_norm_2, swa_k_norm_2, swa_sinks_2,
):
    x = first_block(
        x, c, w_ada, b_ada, g_pre, w_in, w_conv, w_pool, pool_scale, w_out, g_post,
    )
    return second_block(
        x, ffn1_norm_2, ffn1_w_in_2, ffn1_w_out_2, mix_norm_2, ffn2_norm_2, ffn2_w_in_2,
        ffn2_w_out_2, nsa_w_in_2, nsa_w_out_2, nsa_q_norm_2, nsa_k_norm_2, nsa_cmp_pos_2,
        nsa_cmp_w1_2, nsa_cmp_w2_2, diff_w_in_2, diff_w_out_2, diff_q_norm_2, diff_k_norm_2,
        diff_lambda_2, diff_subln_2, gdn_w_in_2, gdn_w_out_2, gdn_conv_w_2, gdn_a_log_2,
        gdn_dt_bias_2, gdn_o_norm_2, swa_w_in_2, swa_w_out_2, swa_q_norm_2, swa_k_norm_2,
        swa_sinks_2,
    )


_drawn_inputs = setup_inputs


def setup_inputs(seed=0):
    import zlib

    import numpy as np

    out = dict(_drawn_inputs(seed))
    spreads = {}
    factors = {'g_post': 2.785,
     'ffn1_norm_2': 5.364,
     'mix_norm_2': 3.338,
     'ffn2_norm_2': 6.351,
     'nsa_q_norm_2': 8.0,
     'nsa_k_norm_2': 8.0,
     'nsa_cmp_pos_2': 8.0,
     'diff_q_norm_2': 5.885,
     'diff_k_norm_2': 7.162,
     'diff_subln_2': 7.621}
    for name, (base, spread) in spreads.items():
        noise = np.random.default_rng([zlib.crc32(name.encode()), seed]).standard_normal(out[name].shape)
        drawn = base * np.exp(spread * noise) if base else spread * noise
        out[name] = __import__('jax').numpy.asarray(drawn.astype(out[name].dtype))
    for name, factor in factors.items():
        out[name] = (out[name] * factor).astype(out[name].dtype)
    return out
```

```python
import math
from contextlib import ExitStack

import concourse.bass as bass
from concourse import mybir
from concourse.alu_op_type import AluOpType as ALU

F32 = mybir.dt.float32
BF16 = mybir.dt.bfloat16
I32 = mybir.dt.int32
ACT = mybir.ActivationFunctionType
AX = mybir.AxisListType

P = 128
T = 256
TT = T // P
D = 1024
KD = D // P
EPS = 1e-6
NEG = -1e30

CW = 512
IN1 = 6 * CW
WINDOWS = (2, 4, 8, 16)
DFF = 2816
NPAIR = DFF // 256
DH = 64
HQ = 16
HKV = 4
G = HQ // HKV
CMP_HIDDEN = 256
CMP_TILES = 32 * DH // P
NCMP = T // 16 - 1
NSA_IN = HQ * DH + 6 * HKV * DH + 3 * HQ
NGATE = 3 * HQ
DIFF_H = 8
LAM_INIT = 0.8 - 0.6 * math.exp(-0.3)

RAW = 4
SPL = 4
LEAD = SPL - 1
CH = 2048
CC = 256

A_GPRE, A_GPOST, A_F1, A_MIX, A_F2, A_POOL, A_CONV, A_C, A_N = 0, 16, 32, 48, 64, 80, 88, 112, 120
B_BADA, B_POS, B_NQ, B_NK, B_DQ, B_DK, B_SUB, B_N = 0, 48, 80, 81, 84, 85, 86, 87

IN1_ORDER = [8, 9, 0, 1, 4, 5, 10, 11, 6, 7, 2, 3]
OUT1_ORDER = [2, 3, 0, 1]
NSA_ORDER = [4, 5, 0, 1, 2, 3, 6, 8, 7, 9, 10]

CONV_BLK = (0, 1)
CONV_FFN = {0: 2, 1: 5, 2: 6, 3: 9}
CONV_NSA, CONV_NSA_O, CONV_DIFF, CONV_DIFF_O = 3, 4, 7, 8
OUT_BLK, OUT_NSA, OUT_DIFF = (0, 1), 3, 6
OUT_FFN = {0: 2, 1: 4, 2: 5, 3: 7}


class Tally:

    def __init__(self, sem):
        self.sem, self.n, self.it, self.per = sem, 0, None, 0

    def add(self, ins):
        ins.then_inc(self.sem, 1)
        self.n += 1
        return self.n

    def value(self, n):
        return n if self.it is None else n + self.it * self.per


def stream_items():
    items = [("ada", 0, c) for c in range(8)]
    side = [("ada", 0, c) for c in range(8, 12)] + [("ada", 1, c) for c in range(8)]
    for c in IN1_ORDER:
        items.append(("w", "in1", 0, c))
        items.append(side.pop(0))
    items += [("w", "out1", 0, c) for c in OUT1_ORDER]
    side = [("ada", 1, c) for c in range(8, 12)]
    for c in IN1_ORDER:
        items.append(("w", "in1", 1, c))
        if side:
            items.append(side.pop(0))
    items += [("w", "out1", 1, c) for c in OUT1_ORDER]

    def ffn(q):
        got = []
        for j in range(NPAIR):
            got += [("w", "fin", q, j, 0), ("w", "fin", q, j, 1)]
        return got + [("w", "fout", q, j) for j in range(NPAIR)]

    items += ffn(0)
    items += [("w", "nsa", c) for c in NSA_ORDER]
    items += [("w", "cmp", kv, half) for kv in range(2) for half in range(2)]
    items += [("w", "nsao", c) for c in range(4)]
    items += ffn(1) + ffn(2)
    items += [("w", "diff", c) for c in range(12)]
    items += [("w", "diffo", c) for c in range(4)]
    items += ffn(3)
    return items


def two_blocks_kernel(nc, a, out):
    ctx = ExitStack()
    with ctx:
        def sb(name, shape, dt=F32):
            return ctx.enter_context(nc.sbuf_tensor(name, shape, dt))

        def sem(name):
            return ctx.enter_context(nc.semaphore(name))

        x = sb("x", [P, TT, D])
        xn = sb("xn", [P, TT, D])
        proj = sb("proj", [P, 2 * 3072])
        raw = sb("raw", [P, RAW, CH])
        whi = sb("whi", [P, SPL, CH], BF16)
        wlo = sb("wlo", [P, SPL, CH], BF16)
        hT_hi = sb("hT_hi", [P, KD, T], BF16)
        hT_lo = sb("hT_lo", [P, KD, T], BF16)
        sT_hi = sb("sT_hi", [P, 2 * NPAIR, T], BF16)
        sT_lo = sb("sT_lo", [P, 2 * NPAIR, T], BF16)
        bias = sb("bias", [P, HQ, T])
        bias_c = sb("bias_c", [P, TT, HQ, NCMP])
        dist = sb("dist", [P, T])
        dist_c = sb("dist_c", [P, TT, NCMP])
        ident = sb("ident", [P, P])
        ones = sb("ones", [P, P])
        rowsA = xn[:, 1, 0:P]
        rowsB = xn[:, 1, P:2 * P]
        colA = sb("colA", [P, A_N])
        colB = sb("colB", [P, B_N])
        wpool = sb("wpool", [P, 2, 4, P])
        w2 = sb("w2", [P, 2, 2, DH])
        lam = sb("lam", [P, 4, DH])
        lam_s = sb("lam_s", [P, 8])
        count_fix = sb("count_fix", [P, 4, 16])
        pos1 = sb("pos1", [P, 16])
        cact = sb("cact", [P, KD])
        mod = sb("mod", [P, 24])
        gain1 = sb("gain1", [P, 2, KD])
        shift1 = sb("shift1", [P, 2, KD])
        gate_col = sb("gate_col", [P, KD])
        gate_row = sb("gate_row", [P, D])
        gq = sb("gq", [P, 2])
        gsub = sb("gsub", [P, 1])
        stat = sb("stat", [P, 64])
        rs = sb("rs", [P, 64])
        nt0 = sb("nt0", [P, 64])
        nt1 = sb("nt1", [P, 64])
        nt2 = sb("nt2", [P, 64])
        scratch = sb("scratch", [P, 2048])
        region = sb("region", [P, 7 * 1024])
        acc_ada = region[:, 0:3072]
        diag = xn[:, 0, :]
        y1 = region[:, 3072:5120].rearrange("p (k t) -> p k t", t=T)
        pool_a = region[:, 5120:6144].rearrange("p (g t) -> p g t", t=T)
        pool_b = region[:, 6144:7168].rearrange("p (g t) -> p g t", t=T)
        z1 = pool_a
        v1 = scratch[:, 0:1024].rearrange("p (g t) -> p g t", t=T)
        silu_a = region[:, 4096:5120].rearrange("p (b n) -> p b n", b=2)
        sact = region[:, 5120:5632]
        h1 = region[:, 5120:7168].rearrange("p (k t) -> p k t", t=T)
        qT = region[:, 0:2048].rearrange("p (h t) -> p h t", t=T)
        kT = region[:, 2048:4096].rearrange("p (h t) -> p h t", t=T)
        sc = region[:, 4096:6144].rearrange("p (b n) -> p b n", b=2)
        pT = scratch.rearrange("p (b n) -> p b n", b=2)
        kcT = region[:, 0:2048].rearrange("p (k h t) -> p k h t", k=2, h=HKV)
        cmpR = scratch[:, 0:1920].rearrange("p (k m n) -> p k m n", k=2, m=CMP_TILES)
        cmp_hi, cmp_lo = (v.rearrange("p k t -> p (k t)")[:, 0:1920]
                          .rearrange("p (k m n) -> p k m n", k=2, m=CMP_TILES) for v in (sT_hi, sT_lo))
        cmp_g = gate_row[:, 0:240].rearrange("p (k c n) -> p k c n", k=2, c=2)
        vcmp = gate_row[0:NCMP, 256:512].rearrange("p (h d) -> p h d", h=HKV)
        kcn = gate_row[0:HKV * NCMP, 512:640].rearrange("p (c d) -> p c d", c=2)
        kcmpT = gate_row[:, 640:640 + HKV * NCMP]
        gates = sb("gates", [P, TT, NGATE])
        nmax = sb("nmax", [P, 2, 8])
        psums = sb("psums", [P, 4, 8])
        rw = sb("rw", [P, 8])
        otmp = sb("otmp", [P, 512])

        acc = ctx.enter_context(nc.psum_tensor("acc", [P, 8, 512], F32))

        raw_landed = [sem(f"raw_landed{i}") for i in range(RAW)]
        params_landed = sem("params_landed")
        x_landed = sem("x_landed")
        wsmall_landed = sem("wsmall_landed")
        out_stored = sem("out_stored")
        consts_ready = sem("consts_ready")
        pool_step = sem("pool_step")
        bias_ready = sem("bias_ready")
        hi_ready = sem("hi_ready")
        raw_done = sem("raw_done")
        chunk_used = sem("chunk_used")
        cols_ready = sem("cols_ready")
        colsd_ready = sem("colsd_ready")
        cact_ready = sem("cact_ready")
        ada_ready = sem("ada_ready")
        mod_ps = sem("mod_ps")
        diag_ready = sem("diag_ready")
        gate_ps = sem("gate_ps")
        gate_sb = sem("gate_sb")
        x_ready = sem("x_ready")
        ss_ready = sem("ss_ready")
        xn_ready = sem("xn_ready")
        turned = sem("turned")
        feat_hi = sem("feat_hi")
        feat_ready = sem("feat_ready")
        proj_ready = sem("proj_ready")
        pooled_ready = sem("pooled_ready")
        mixed_ps = sem("mixed_ps")
        y_ps = sem("y_ps")
        silu_ready = sem("silu_ready")
        gated = sem("gated")
        s_ready = sem("s_ready")
        dve_step = sem("dve_step")
        act_step = sem("act_step")
        kc_ps = sem("kc_ps")
        kc_act = sem("kc_act")
        cmpr_ready = sem("cmpr_ready")
        cmph_ps = sem("cmph_ps")
        gelu_ready = sem("gelu_ready")
        cmpk_ps = sem("cmpk_ps")
        cmpv_ps = sem("cmpv_ps")
        cmpk_sq = sem("cmpk_sq")
        kcn_ready = sem("kcn_ready")
        kcn_ps = sem("kcn_ps")
        cmp_sb = sem("cmp_sb")
        qsq_ready = sem("qsq_ready")
        sq_free = sem("sq_free")
        qn_ready = sem("qn_ready")
        qk_turned = sem("qk_turned")
        qk_act = sem("qk_act")
        qk_dve = sem("qk_dve")
        gexp_ready = sem("gexp_ready")
        qk_ps = sem("qk_ps")
        scored = sem("scored")
        probs = sem("probs")
        mixed = sem("mixed")
        probs_turned = sem("probs_turned")
        pT_act = sem("pT_act")
        pT_dve = sem("pT_dve")
        pv_ps = sem("pv_ps")
        combined = sem("combined")
        osq_ready = sem("osq_ready")

        items = stream_items()
        w_raw = [r for r, it in enumerate(items) if it[0] == "w"]
        w_at = {items[r][1:]: w for w, r in enumerate(w_raw)}
        NW = len(w_raw)

        def col_chunk(ap, c0, n=CC):
            return ap.rearrange("(k p) n -> p k n", p=P)[:, :, c0:c0 + n]

        def row_chunk(ap, c):
            return ap.rearrange("(c k p) n -> p c k n", p=P, k=2)[:, c, :, :]

        ffn_in = [a["ffn1_w_in_2"][0], a["ffn2_w_in_2"][0], a["ffn1_w_in_2"][1], a["ffn2_w_in_2"][1]]
        ffn_out = [a["ffn1_w_out_2"][0], a["ffn2_w_out_2"][0], a["ffn1_w_out_2"][1], a["ffn2_w_out_2"][1]]

        def source(item):
            if item[0] == "ada":
                return col_chunk(a["w_ada"][item[1]], item[2] * CC)
            kind, *at = item[1:]
            if kind == "in1":
                return col_chunk(a["w_in"][at[0]], at[1] * CC)
            if kind == "out1":
                return row_chunk(a["w_out"][at[0]], at[1])
            if kind == "fin":
                return col_chunk(ffn_in[at[0]], at[2] * DFF + at[1] * CC)
            if kind == "fout":
                return row_chunk(ffn_out[at[0]], at[1])
            if kind == "nsa":
                return col_chunk(a["nsa_w_in_2"][0], at[0] * CC, NGATE if at[0] == 10 else CC)
            if kind == "cmp":
                return a["nsa_cmp_w1_2"][0, at[0]].rearrange("(k p) n -> p k n", p=P)[:, at[1] * 8:at[1] * 8 + 8, :]
            if kind == "nsao":
                return row_chunk(a["nsa_w_out_2"][0], at[0])
            if kind == "diff":
                return col_chunk(a["diff_w_in_2"][0], at[0] * CC)
            return row_chunk(a["diff_w_out_2"][0], at[0])

        def size(item):
            return 8 * NGATE if item[1:] == ("nsa", 10) else CH

        def raw_view(slot, ap):
            k, n = ap.shape[1], ap.shape[2]
            return raw[:, slot, 0:k * n].rearrange("p (k n) -> p k n", k=k)

        out_last = [w_at[k] for k in (("out1", 0, 1), ("out1", 1, 1), ("fout", 0, 10), ("nsao", 3), ("fout", 1, 10),
                                      ("fout", 2, 10), ("diffo", 3), ("fout", 3, 10))]

        def bank_complete(eng, o, k):
            if k < 3:
                eng.wait_ge(y_ps, 3 * o + k + 1)
            else:
                eng.wait_ge(chunk_used, out_last[o] + 1)

        def landed_value(r, it=0):
            return 16 * (r // RAW + 1) + 16 * it

        block = ctx.enter_context(nc.Block())

        @block.sync
        def _(sp):
            sp.dma_start(x[:, :, :], a["x"][0].rearrange("(t p) n -> p t n", p=P)).then_inc(x_landed, 16)

            def load(r):
                if r >= RAW:
                    sp.wait_ge(raw_done, r - RAW + 1)
                src = source(items[r])
                sp.dma_start(raw_view(r % RAW, src), src).then_inc(raw_landed[r % RAW], 16)

            def ffn_loads(q, r0):
                w_in_v = ffn_in[q].rearrange("(k p) n -> p k n", p=P)
                with sp.Fori(0, 5) as it:
                    for c in range(4):
                        sp.wait_ge(raw_done, it * 4 + (r0 + c - RAW + 1))
                        col = it * (2 * CC) + ((c % 2) * DFF + (c // 2) * CC)
                        sp.dma_start(raw_view((r0 + c) % RAW, w_in_v[:, :, 0:CC]),
                                     w_in_v[:, :, bass.ds(col, CC)]).then_inc(raw_landed[(r0 + c) % RAW], 16)
                for r in range(r0 + 20, r0 + 23):
                    load(r)
                w_out_v = ffn_out[q].rearrange("(c k p) n -> p c k n", p=P, k=2)
                with sp.Fori(0, 2) as it:
                    for c in range(4):
                        r = r0 + 23 + c
                        sp.wait_ge(raw_done, it * 4 + (r - RAW + 1))
                        sp.dma_start(raw_view(r % RAW, w_out_v[:, 0]),
                                     w_out_v[:, bass.ds(it * 4 + (1 + c), 1)].rearrange("p c k n -> p (c k) n"))\
                            .then_inc(raw_landed[r % RAW], 16)
                for r in range(r0 + 31, r0 + 33):
                    load(r)

            r = 0
            while r < len(items):
                if items[r][1] == "fin":
                    ffn_loads(items[r][2], r)
                    r += 3 * NPAIR
                else:
                    load(r)
                    r += 1
            for tt in range(TT):
                sp.wait_ge(x_ready, 2 * 7 + tt + 1)
                sp.dma_start(out[0].rearrange("(t p) n -> p t n", p=P)[:, tt], x[:, tt, :]).then_inc(out_stored, 16)
            sp.wait_ge(out_stored, 16 * TT)

        @block.gpsimd
        def _(pool):
            steps = Tally(pool_step)

            def step(ins):
                pool.wait_ge(pool_step, steps.add(ins))

            step(nc.gpsimd.memset(ident[:, :], 0.0))
            step(nc.gpsimd.affine_select(out=ident[:, :], in_=ident[:, :], compare_op=ALU.not_equal, fill=1.0,
                                         base=0, pattern=[[-1, P]], channel_multiplier=1))
            nc.gpsimd.iota(pos1[:, :], pattern=[[1, 16]], base=1, channel_multiplier=0,
                           allow_small_or_imprecise_dtypes=True).then_inc(consts_ready, 1)
            nc.gpsimd.memset(ones[:, :], 1.0).then_inc(consts_ready, 1)
            step(nc.gpsimd.iota(dist[:, :], pattern=[[-1, T]], base=P, channel_multiplier=1,
                                allow_small_or_imprecise_dtypes=True))
            step(nc.gpsimd.iota(dist_c[:, :, :], pattern=[[P, TT], [-16, NCMP]], base=-31, channel_multiplier=1,
                                allow_small_or_imprecise_dtypes=True))
            for h in range(HQ):
                slope = 2.0 ** (-0.5 * (h + 1))
                step(nc.gpsimd.tensor_scalar(bias[:, h, :], dist[:, :], -slope, None, ALU.mult))
                step(nc.gpsimd.affine_select(out=bias[:, h, :], in_=bias[:, h, :], compare_op=ALU.is_ge,
                                             fill=NEG, base=P, pattern=[[-1, T]], channel_multiplier=1))
                step(nc.gpsimd.tensor_scalar(bias_c[:, :, h, :], dist_c[:, :, :], -slope, None, ALU.mult))
                step(nc.gpsimd.affine_select(out=bias_c[:, :, h, :], in_=bias_c[:, :, h, :], compare_op=ALU.is_ge,
                                             fill=NEG, base=-31, pattern=[[P, TT], [-16, NCMP]],
                                             channel_multiplier=1))
            step(nc.gpsimd.memset(dist_c[:, :, :], 1.0))
            nc.gpsimd.affine_select(out=dist_c[:, :, :], in_=dist_c[:, :, :], compare_op=ALU.is_ge, fill=0.0,
                                    base=-31, pattern=[[P, TT], [-16, NCMP]],
                                    channel_multiplier=1).then_inc(bias_ready, 1)

        nsa_steps = [(b, hkv, tt) for b in ("sel", "win") for hkv in range(HKV) for tt in range(TT)]
        nsa_steps += [("cmp", tt, half) for tt in range(TT) for half in range(2)]
        diff_steps = [("diff", hp, tt) for hp in range(DIFF_H // 2) for tt in range(TT)]
        NS = len(nsa_steps)
        att_steps = nsa_steps + diff_steps
        NA = len(att_steps)
        pj = proj[:, 0:TT * NSA_IN].rearrange("p (t n) -> p t n", t=TT)
        pd = proj[:, :].rearrange("p (t n) -> p t n", t=TT)
        pf = proj[:, :].rearrange("p (k t) -> p k t", t=T)
        twice = xn.rearrange("p t (b h c d) -> p t b h c d", b=2, h=HKV, c=2)
        mapsA = []
        na = nd = 0
        for s in att_steps:
            mapsA.append((na, nd))
            na += 1
            nd += 1 if (s[0] == "cmp" or (s[0] != "diff" and s[2] == 1)) else 0

        def nk(step):
            return NCMP if step[0] == "cmp" else P * (step[2] + 1)

        @block.scalar
        def _(act):
            steps = Tally(act_step)

            def step(ins):
                act.wait_ge(act_step, steps.value(steps.add(ins)))

            act.dma_start(rowsA[A_C:A_N, :], a["c"].rearrange("b (k p) -> (b k) p", p=P)).then_inc(params_landed, 16)
            for at, name in ((A_GPRE, "g_pre"), (A_GPOST, "g_post"), (A_F1, "ffn1_norm_2"), (A_MIX, "mix_norm_2"),
                             (A_F2, "ffn2_norm_2")):
                act.dma_start(rowsA[at:at + 16, :], a[name].rearrange("l (k p) -> (l k) p", p=P))\
                   .then_inc(params_landed, 16)
            act.dma_start(rowsA[A_POOL:A_CONV, :], a["pool_scale"].rearrange("l (k p) -> (l k) p", p=P))\
               .then_inc(params_landed, 16)
            act.dma_start(rowsA[A_CONV:A_C, :], a["w_conv"].rearrange("l j (k p) -> (l j k) p", p=P))\
               .then_inc(params_landed, 16)
            act.dma_start(rowsB[B_BADA:B_POS, :], a["b_ada"].rearrange("l (k p) -> (l k) p", p=P))\
               .then_inc(params_landed, 16)
            act.dma_start(rowsB[B_POS:B_NQ, :], a["nsa_cmp_pos_2"][0].rearrange("v (m j) d -> (v m) (j d)", j=2))\
               .then_inc(params_landed, 16)
            n_params = 10
            for c in range(2):
                for at, name, n in ((B_NQ, "nsa_q_norm_2", 1), (B_NK, "nsa_k_norm_2", 3), (B_DQ, "diff_q_norm_2", 1),
                                    (B_DK, "diff_k_norm_2", 1)):
                    src = a[name][0] if n == 3 else a[name]
                    act.dma_start(rowsB[at:at + n, c * DH:(c + 1) * DH], src).then_inc(params_landed, 16)
                    n_params += 1
            act.dma_start(rowsB[B_SUB:B_N, :], a["diff_subln_2"]).then_inc(params_landed, 16)
            n_params += 1
            act.dma_start(wpool[:, :, :, :], a["w_pool"].rearrange("l g c d -> c l g d")).then_inc(wsmall_landed, 16)
            act.dma_start(w2[:, :, :, :], a["nsa_cmp_w2_2"][0].rearrange("v (k p) d -> p v k d", p=P))\
               .then_inc(wsmall_landed, 16)
            act.dma_start(lam[:, :, :], a["diff_lambda_2"][0].partition_broadcast(P)).then_inc(wsmall_landed, 16)
            assert n_params == N_PARAMS

            split_at = [0]

            def split_hi(w, it=0, n=CH):
                r = w_raw[w]
                act.wait_ge(raw_landed[r % RAW], landed_value(r, it))
                if w >= SPL:
                    act.wait_ge(chunk_used, it * 4 + (w - SPL + 1))
                nc.scalar.activation(whi[:, w % SPL, 0:n], raw[:, r % RAW, 0:n], ACT.Copy).then_inc(hi_ready, 1)

            def split_to(w):
                while split_at[0] <= min(w, NW - 1):
                    split_hi(split_at[0], n=size(items[w_raw[split_at[0]]]))
                    split_at[0] += 1

            def sumsq(n_x, n_ss):
                for tt in range(TT):
                    act.wait_ge(x_ready, 2 * n_x + tt + 1)
                    step(nc.scalar.activation(scratch[:, tt * D:(tt + 1) * D], x[:, tt, :], ACT.Square,
                                              accum_out=stat[:, tt:tt + 1]))
                    act.sem_inc(ss_ready, 1)

            def to_features(f, dst, scale=None, shift=None):
                for kt in range(KD):
                    if kt % 2 == 0:
                        act.wait_ge(turned, 4 * f + kt // 2 + 1)
                    src = acc[:, kt // 2, (kt % 2) * T:(kt % 2) * T + T]
                    if shift is not None:
                        nc.scalar.activation(h1[:, kt, :], src, ACT.Identity, bias=shift(kt), scale=scale(kt))\
                          .then_inc(feat_hi, 1)
                    elif scale is not None:
                        nc.scalar.activation(dst[:, kt, :], src, ACT.Copy, scale=scale(kt)).then_inc(feat_hi, 1)
                    else:
                        nc.scalar.activation(dst[:, kt, :], src, ACT.Copy).then_inc(feat_hi, 1)

            def ffn(q):
                w0 = w_at[("fin", q, 0, 0)]

                def silu_pair(j, w, it=0):
                    act.wait_ge(chunk_used, it * 4 + (w + 1))
                    act.wait_ge(gated, it * 2 + (NPAIR * q + j))
                    b = (2 * j) % 4
                    nc.scalar.activation(silu_a[:, j % 2, :], acc[:, b, :], ACT.Silu).then_inc(silu_ready, 1)

                with act.Fori(0, 5) as it:
                    for c in range(4):
                        split_hi(w0 + c + LEAD, it)
                        if c % 2 == 0:
                            silu_pair(c // 2, w0 + c, it)
                split_at[0] = w0 + 20 + LEAD
                split_to(w0 + 20 + LEAD)
                silu_pair(10, w0 + 20)
                split_to(w0 + 21 + LEAD)
                w1 = w0 + 22
                split_to(w1 + LEAD)
                if q < 3:
                    with act.Fori(0, 2) as it:
                        for c in range(4):
                            split_hi(w1 + 1 + c + LEAD, it)
                    split_at[0] = w1 + 9 + LEAD
                split_to(w1 + 10 + LEAD)

            def evict(n, w, dst, func=ACT.Copy, width=None):
                act.wait_ge(chunk_used, w + 1)
                src = acc[:, n % 4, :]
                if width is not None:
                    src = src.rearrange("p (t n) -> p t n", t=TT)[:, :, 0:width]
                nc.scalar.activation(dst, src, func).then_inc(proj_ready, 1)

            act.wait_ge(colsd_ready, 1)
            nc.scalar.activation(cact[:, :], colA[:, A_C:A_N], ACT.Silu).then_inc(cact_ready, 1)
            nc.scalar.activation(lam_s[:, 7:8], colA[:, A_C:A_C + 1], ACT.Copy).then_inc(silu_ready, 1)
            for l in range(2):
                if l == 0:
                    act.wait_ge(x_landed, 16)
                    for tt in range(TT):
                        step(nc.scalar.activation(scratch[:, tt * D:(tt + 1) * D], x[:, tt, :], ACT.Square,
                                                  accum_out=stat[:, tt:tt + 1]))
                        act.sem_inc(ss_ready, 1)
                else:
                    sumsq(1 - 1, None)
                split_to(w_at[("in1", l, IN1_ORDER[0])] + LEAD - 1)
                act.wait_ge(diag_ready, 1 if l == 0 else 4)
                to_features(l, hT_hi, scale=lambda kt: gain1[:, l, kt:kt + 1], shift=lambda kt: shift1[:, l, kt:kt + 1])
                for n, c in enumerate(IN1_ORDER):
                    w = w_at[("in1", l, c)]
                    split_to(w + LEAD)
                    func = ACT.Silu if c in (6, 7, 10, 11) else ACT.Copy
                    evict(n, w, proj[:, c * 512:(c + 1) * 512], func)
                act.wait_ge(gate_ps, l + 1)
                nc.scalar.activation(gate_row[:, :], acc[:, 4:6, :].rearrange("p b n -> p (b n)"), ACT.Copy)\
                  .then_inc(gate_sb, 1)
                for c in OUT1_ORDER:
                    split_to(w_at[("out1", l, c)] + LEAD)
                for tt in range(TT):
                    bank_complete(act, l, 2 * tt + 1)
                    step(nc.scalar.activation(scratch[:, tt * D:(tt + 1) * D],
                                              acc[:, 4 + 2 * tt:6 + 2 * tt, :].rearrange("p b n -> p (b n)"),
                                              ACT.Square, accum_out=stat[:, 2 + tt:3 + tt]))
                    act.sem_inc(ss_ready, 1)
            ffn_x = {0: 1, 1: 3, 2: 4, 3: 6}
            gain_of = {0: A_F1, 1: A_F2, 2: A_F1 + KD, 3: A_F2 + KD}

            def ffn_all(q):
                sumsq(ffn_x[q], None)
                g0 = gain_of[q]
                to_features(CONV_FFN[q], hT_hi, scale=lambda kt: colA[:, g0 + kt:g0 + kt + 1])
                ffn(q)

            def turn_out(n, dst, gain, who):
                for b in range(n):
                    yield b

            def attention(first, last):
                for i in range(first, last + 1):
                    if i < last:
                        s = att_steps[i]
                        act.wait_ge(scored, i + 1)
                        b = i % 2
                        if s[0] == "cmp":
                            nc.scalar.activation(sc[:, b, 0:8 * NCMP], sc[:, b, 0:8 * NCMP], ACT.Exp)\
                              .then_inc(probs, 1)
                        else:
                            for m in range(4):
                                v = sc[:, b, m * nk(s):(m + 1) * nk(s)]
                                ins = nc.scalar.activation(v, v, ACT.Exp, bias=nmax[:, b, m:m + 1],
                                                           accum_out=psums[:, i % 4, m:m + 1])
                            ins.then_inc(probs, 1)
                    if i > first:
                        j = i - 1
                        s = att_steps[j]
                        act.wait_ge(probs_turned, j + 1)
                        if j >= first + 2:
                            act.wait_ge(pv_ps, j - 1)
                        if s[0] == "cmp":
                            nc.scalar.activation(pT[0:NCMP, j % 2, 0:512], acc[0:NCMP, 4, :], ACT.Copy)\
                              .then_inc(pT_act, 1)
                        else:
                            n = 4 * P if s[0] != "diff" else 2 * nk(s)
                            nc.scalar.activation(pT[:, j % 2, 0:n], acc[:, 4, 0:n], ACT.Copy).then_inc(pT_act, 1)

            ffn_all(0)
            sumsq(2, None)
            to_features(CONV_NSA, hT_hi, scale=lambda kt: colA[:, A_MIX + kt:A_MIX + kt + 1])
            for n, c in enumerate(NSA_ORDER):
                w = w_at[("nsa", c)]
                split_to(w + LEAD)
                if c in (4, 5):
                    act.wait_ge(chunk_used, w + 1)
                    for tt in range(TT):
                        ins = nc.scalar.activation(
                            twice[:, tt, c - 4], acc[:, n % 4, tt * T:(tt + 1) * T].rearrange("p (h d) -> p h d", d=DH)
                            .unsqueeze(2).to_broadcast([P, HKV, 2, DH]), ACT.Copy)
                    ins.then_inc(proj_ready, 1)
                else:
                    wd = NGATE if c == 10 else CC
                    evict(n, w, pj[:, :, c * CC:c * CC + wd], width=wd)
                if n == 4:
                    for kv in range(2):
                        for hb in range(2):
                            act.wait_ge(kc_ps, 2 * kv + hb + 1)
                            nc.scalar.activation(
                                kcT[0:DH, kv, 2 * hb:2 * hb + 2, :],
                                acc[0:DH, 4 + 2 * kv + hb, :].rearrange("p (h t) -> p h t", h=2),
                                ACT.Copy).then_inc(kc_act, 1)
            nc_proj = 24 + 11
            split_to(w_at[("cmp", 0, 0)] + LEAD)
            act.wait_ge(proj_ready, nc_proj)
            nc.scalar.activation(gates[:, :, :], pj[:, :, NSA_IN - NGATE:NSA_IN], ACT.Exp, scale=-1.0)\
              .then_inc(gexp_ready, 1)
            act.wait_ge(cmpr_ready, 2)
            for tt in range(TT):
                if tt:
                    act.wait_ge(sq_free, 1)
                nc.scalar.activation(scratch[:, 0:D], pj[:, tt, 0:D], ACT.Square).then_inc(qsq_ready, 1)
                ksw = pj[:, tt, 1536:2560].rearrange("p (b n) -> p b n", b=2)[:, :, 0:256]
                nc.scalar.activation(scratch[:, D:D + 512].rearrange("p (b n) -> p b n", b=2), ksw,
                                     ACT.Square).then_inc(qsq_ready, 1)
            for kv in range(2):
                for half in range(2):
                    split_to(w_at[("cmp", kv, half)] + LEAD)
            for kv in range(2):
                act.wait_ge(cmph_ps, kv + 1)
                nc.scalar.activation(cmp_g[:, kv, :, :], acc[:, 4 + 2 * kv:6 + 2 * kv, 0:HKV * NCMP],
                                     ACT.Gelu_apprx_tanh).then_inc(gelu_ready, 1)
            for rnd in range(2):
                for b in (0, 2):
                    act.wait_ge(qk_turned, 4 * rnd + b + 1)
                    dst = (qT if rnd == 0 else kT)[:, 2 * b:2 * b + 2, :]
                    gcol = gq[:, 0:1] if rnd == 0 else colB[:, B_NK + 1 + b // 2:B_NK + 2 + b // 2]
                    nc.scalar.activation(dst, acc[:, b, :].rearrange("p (h t) -> p h t", h=2), ACT.Copy,
                                         scale=gcol).then_inc(qk_act, 1)
            act.wait_ge(cmpk_ps, 1)
            step(nc.scalar.activation(otmp[0:HKV * NCMP, 0:DH], acc[0:HKV * NCMP, 4, 0:DH], ACT.Square,
                                      accum_out=stat[0:HKV * NCMP, 4:5]))
            act.sem_inc(cmpk_sq, 1)
            act.wait_ge(cmpv_ps, 1)
            nc.scalar.activation(vcmp[:, :, :], acc[0:NCMP, 6, 0:256].rearrange("p (h d) -> p h d", h=HKV),
                                 ACT.Copy).then_inc(cmp_sb, 1)
            act.wait_ge(kcn_ps, 1)
            nc.scalar.activation(kcmpT[:, :], acc[:, 5, 0:HKV * NCMP], ACT.Copy, scale=colB[:, B_NK:B_NK + 1])\
              .then_inc(cmp_sb, 1)
            attention(0, NS)
            to_features(CONV_NSA_O, sT_hi)
            for c in range(4):
                split_to(w_at[("nsao", c)] + LEAD)
            ffn_all(1)
            ffn_all(2)
            sumsq(5, None)
            to_features(CONV_DIFF, hT_hi, scale=lambda kt: colA[:, A_MIX + KD + kt:A_MIX + KD + kt + 1])
            for n in range(12):
                w = w_at[("diff", n)]
                split_to(w + LEAD)
                evict(n, w, pd[:, :, n * CC:(n + 1) * CC], width=CC)
            act.wait_ge(proj_ready, 35 + 8)
            nq = 4
            for tt in range(TT):
                if tt:
                    act.wait_ge(sq_free, 2 + tt)
                nc.scalar.activation(scratch[:, 0:2 * D], pd[:, tt, 0:2 * D], ACT.Square).then_inc(qsq_ready, 1)
            for b in (0, 2, 4, 6):
                act.wait_ge(qk_turned, 8 + b + 1)
                dst = (qT if b < 4 else kT)[:, 2 * (b % 4):2 * (b % 4) + 2, :]
                gcol = gq[:, 1:2] if b < 4 else colB[:, B_DK:B_DK + 1]
                nc.scalar.activation(dst, acc[:, b, :].rearrange("p (h t) -> p h t", h=2), ACT.Copy,
                                     scale=gcol).then_inc(qk_act, 1)
            act.wait_ge(gexp_ready, 2)
            nc.scalar.activation(lam_s[:, 2:4], lam_s[:, 0:2], ACT.Exp).then_inc(gexp_ready, 1)
            attention(NS, NA)
            for tt in range(TT):
                act.wait_ge(combined, NA)
                nc.scalar.activation(scratch[:, tt * D:(tt + 1) * D], xn[:, tt, :], ACT.Square).then_inc(osq_ready, 1)
            to_features(CONV_DIFF_O, sT_hi, scale=lambda kt: gsub[:, 0:1])
            for c in range(4):
                split_to(w_at[("diffo", c)] + LEAD)
            ffn_all(3)

        @block.vector
        def _(dve):
            steps = Tally(dve_step)

            def step(ins):
                dve.wait_ge(dve_step, steps.value(steps.add(ins)))

            raw_at = [0]

            def split_lo(r, n, w, it=0):
                dve.wait_ge(hi_ready, it * 4 + (w + 1))
                nc.vector.tensor_tensor(wlo[:, w % SPL, 0:n], raw[:, r % RAW, 0:n], whi[:, w % SPL, 0:n],
                                        ALU.subtract).then_inc(raw_done, 1)

            def accumulate_ada(r, l, c):
                dve.wait_ge(raw_landed[r % RAW], landed_value(r))
                if l == 1 and c in (0, 8):
                    dve.wait_ge(mod_ps, 1 + c // 8)
                dst = acc_ada[:, c * CC:(c + 1) * CC]
                v = raw[:, r % RAW, :].rearrange("p (k n) -> p k n", k=8)
                step(nc.vector.tensor_scalar(dst, v[:, 0, :], cact[:, 0:1], None, ALU.mult))
                for k in range(1, 8):
                    ins = nc.vector.scalar_tensor_tensor(out=dst, in0=v[:, k, :], scalar=cact[:, k:k + 1], in1=dst,
                                                         op0=ALU.mult, op1=ALU.add)
                    if k < 7:
                        step(ins)
                ins.then_inc(raw_done, 1)
                if c in (7, 11):
                    dve.wait_ge(raw_done, r + 1)
                    dve.sem_inc(ada_ready, 1)

            def stream_to(w):
                end = w_raw[min(w, NW - 1)] + 1
                while raw_at[0] < end:
                    r = raw_at[0]
                    if items[r][0] == "ada":
                        accumulate_ada(r, items[r][1], items[r][2])
                    else:
                        split_lo(r, size(items[r]), w_raw.index(r))
                    raw_at[0] += 1

            def rsqrt(dst, src, n, inv_n, parts=P):
                m, u, v = nt0[0:parts, 0:n], nt1[0:parts, 0:n], nt2[0:parts, 0:n]
                step(nc.vector.tensor_scalar(m, src, inv_n, EPS, ALU.mult, ALU.add))
                step(nc.vector.tensor_scalar(u.bitcast(I32), m.bitcast(I32), 1, None, ALU.logical_shift_right))
                step(nc.vector.tensor_scalar(v.bitcast(I32), u.bitcast(I32), -1.0, float(0x5F3759DF), ALU.mult,
                                             ALU.add))
                step(nc.vector.tensor_scalar(m, m, -0.5, None, ALU.mult))
                for i in range(3):
                    step(nc.vector.tensor_tensor(u, v, v, ALU.mult))
                    step(nc.vector.tensor_tensor(u, u, m, ALU.mult))
                    step(nc.vector.scalar_tensor_tensor(out=dst if i == 2 else v, in0=u, scalar=1.5, in1=v,
                                                        op0=ALU.add, op1=ALU.mult))

            def normalise(n_ss):
                for tt in range(TT):
                    dve.wait_ge(ss_ready, n_ss + tt + 1)
                    rsqrt(rs[:, tt:tt + 1], stat[:, tt:tt + 1], 1, 1.0 / D)
                    nc.vector.tensor_scalar(xn[:, tt, :], x[:, tt, :], rs[:, tt:tt + 1], None, ALU.mult)\
                      .then_inc(xn_ready, 1)

            def to_features(f, dst_hi, dst_lo, scale=None):
                for kt in range(KD):
                    if kt % 2 == 0:
                        dve.wait_ge(feat_hi, 8 * f + kt + 2)
                    src = acc[:, kt // 2, (kt % 2) * T:(kt % 2) * T + T]
                    if scale is not None:
                        nc.vector.scalar_tensor_tensor(out=dst_lo[:, kt, :], in0=src, scalar=scale(kt),
                                                       in1=dst_hi[:, kt, :], op0=ALU.mult, op1=ALU.subtract)\
                          .then_inc(feat_ready, 1)
                    else:
                        nc.vector.tensor_tensor(dst_lo[:, kt, :], src, dst_hi[:, kt, :], ALU.subtract)\
                          .then_inc(feat_ready, 1)

            def residual(o, factor):
                for tt in range(TT):
                    for nh in range(2):
                        bank_complete(dve, o, 2 * tt + nh)
                        xv = x[:, tt, nh * 512:(nh + 1) * 512]
                        ins = nc.vector.scalar_tensor_tensor(out=xv, in0=acc[:, 4 + 2 * tt + nh, :], scalar=factor,
                                                             in1=xv, op0=ALU.mult, op1=ALU.add)
                        if nh == 0:
                            step(ins)
                    ins.then_inc(x_ready, 1)
                dve.wait_ge(x_ready, 2 * (o + 1))

            def ffn(q):
                w0, r0 = w_at[("fin", q, 0, 0)], w_raw[w_at[("fin", q, 0, 0)]]

                def gate_pair(j, w, it=0, pair=None):
                    dve.wait_ge(silu_ready, it * 2 + (NPAIR * q + j + 2))
                    dve.wait_ge(chunk_used, it * 4 + (w + 1))
                    dve.wait_ge(s_ready, it * 2 + (8 + NPAIR * q + j))
                    nc.vector.tensor_tensor(sact[:, :], silu_a[:, j % 2, :], acc[:, (2 * j + 1) % 4, :],
                                            ALU.mult).then_inc(gated, 1)
                    dve.wait_ge(gated, it * 2 + (NPAIR * q + j + 2))
                    at = bass.ds(pair, 2) if pair is not None else slice(2 * j, 2 * j + 2)
                    hi = sT_hi[:, at, :]
                    lo = sT_lo[:, at, :]
                    sv = sact.rearrange("p (k t) -> p k t", t=T)
                    step(nc.vector.tensor_copy(hi, sv))
                    nc.vector.tensor_tensor(lo, sv, hi, ALU.subtract).then_inc(s_ready, 1)

                n0 = steps.n
                with dve.Fori(0, 5) as it:
                    steps.it, steps.per = it, 2
                    for c in range(4):
                        split_lo(r0 + c + LEAD, CH, w0 + c + LEAD, it)
                        if c % 2 == 1:
                            gate_pair(c // 2, w0 + c, it, it * 4 + 2 * (c // 2))
                    steps.it = None
                steps.n = n0 + 10
                raw_at[0] = r0 + 20 + LEAD
                stream_to(w0 + 21 + LEAD)
                gate_pair(10, w0 + 21)
                w1, r1 = w0 + 22, r0 + 22
                stream_to(w1 + LEAD)
                if q < 3:
                    with dve.Fori(0, 2) as it:
                        for c in range(4):
                            split_lo(r1 + 1 + c + LEAD, CH, w1 + 1 + c + LEAD, it)
                    raw_at[0] = r1 + 9 + LEAD
                stream_to(w1 + 10 + LEAD)

            dve.wait_ge(cols_ready, 1)
            step(nc.vector.tensor_copy(colA[:, :], acc[:, 0, 0:A_N]))
            step(nc.vector.tensor_copy(colB[:, :], acc[:, 1, 0:B_N]))
            dve.sem_inc(colsd_ready, 1)
            dve.wait_ge(consts_ready, 1)
            step(nc.vector.reciprocal(pos1[:, :], pos1[:, :]))
            for g, w in enumerate(WINDOWS):
                step(nc.vector.tensor_scalar(count_fix[:, g, :], pos1[:, :], float(w), 1.0, ALU.mult, ALU.max))
            step(nc.vector.tensor_scalar(gq[:, 0:1], colB[:, B_NQ:B_NQ + 1], DH ** -0.5, None, ALU.mult))
            step(nc.vector.tensor_scalar(gq[:, 1:2], colB[:, B_DQ:B_DQ + 1], DH ** -0.5, None, ALU.mult))
            step(nc.vector.tensor_scalar(gsub[:, :], colB[:, B_SUB:B_SUB + 1], 1.0 - LAM_INIT, None, ALU.mult))
            dve.wait_ge(wsmall_landed, 48)
            lp = otmp[:, 0:2 * DH].rearrange("p (a d) -> p a d", a=2)
            lv = lam.rearrange("p (a b) d -> p a b d", b=2)
            step(nc.vector.tensor_tensor(lp, lv[:, :, 0, :], lv[:, :, 1, :], ALU.mult))
            step(nc.vector.tensor_reduce(out=lam_s[:, 0:2], in_=lp, axis=AX.X, op=ALU.add))
            nc.vector.memset(otmp[:, 0:1], 0.0).then_inc(gated, 1)
            dve.wait_ge(cact_ready, 1)

            def modulation(l, part):
                dve.wait_ge(mod_ps, 2 * l + part + 1)
                if part == 0:
                    step(nc.vector.tensor_tensor(mod[:, 0:16], acc[:, 6, 0:16], colB[:, 24 * l:24 * l + 16], ALU.add))
                    step(nc.vector.tensor_copy(shift1[:, l, :], mod[:, 0:8]))
                    step(nc.vector.scalar_tensor_tensor(out=gain1[:, l, :], in0=mod[:, 8:16], scalar=1.0,
                                                        in1=colA[:, A_GPRE + 8 * l:A_GPRE + 8 * l + 8], op0=ALU.add,
                                                        op1=ALU.mult))
                    dve.sem_inc(diag_ready, 1)
                else:
                    step(nc.vector.tensor_tensor(mod[:, 16:24], acc[:, 6, 16:24],
                                                 colB[:, 24 * l + 16:24 * l + 24], ALU.add))
                    step(nc.vector.tensor_tensor(gate_col[:, :], mod[:, 16:24],
                                                 colA[:, A_GPOST + 8 * l:A_GPOST + 8 * l + 8], ALU.mult))
                    for kt in range(KD):
                        ins = nc.vector.tensor_scalar(diag[:, kt * P:(kt + 1) * P], ident[:, :],
                                                      gate_col[:, kt:kt + 1], None, ALU.mult)
                        step(ins)
                    dve.sem_inc(diag_ready, 2)

            def pooling(l):
                p0 = pf[:, 16:20, :]
                src, dst = p0, pool_a
                for g, d in enumerate((1, 2, 4, 8)):
                    step(nc.vector.tensor_copy(dst[:, g:4, 0:d], src[:, g:4, 0:d]))
                    step(nc.vector.tensor_tensor(dst[:, g:4, d:T], src[:, g:4, d:T], src[:, g:4, 0:T - d], ALU.add))
                    src, dst = dst, (pool_b if dst is pool_a else pool_a)
                for g, w in enumerate(WINDOWS):
                    sv = (pool_a if g % 2 == 0 else pool_b)[:, g, :]
                    step(nc.vector.tensor_tensor(sv[:, 0:16], sv[:, 0:16], count_fix[:, g, :], ALU.mult))
                    step(nc.vector.scalar_tensor_tensor(out=pool_b[:, g, :], in0=sv, scalar=1.0 / w, in1=p0[:, g, :],
                                                        op0=ALU.mult, op1=ALU.subtract))
                dve.sem_inc(pooled_ready, 1)

            def conv(l):
                step(nc.vector.tensor_tensor(z1[:, :, :], pf[:, 8:12, :], pf[:, 0:4, :], ALU.mult))
                tap = lambda j, i: colA[:, A_CONV + 12 * l + 4 * j + i:A_CONV + 12 * l + 4 * j + i + 1]
                for i in range(4):
                    step(nc.vector.tensor_scalar(v1[:, i, :], z1[:, i, :], tap(2, i), None, ALU.mult))
                    for j, d in ((1, 1), (0, 2)):
                        step(nc.vector.scalar_tensor_tensor(out=v1[:, i, d:T], in0=z1[:, i, 0:T - d],
                                                            scalar=tap(j, i), in1=v1[:, i, d:T], op0=ALU.mult,
                                                            op1=ALU.add))

            def y_split(k0, n):
                for k in range(k0, k0 + n, 2):
                    step(nc.vector.tensor_copy(sT_hi[:, k:k + 2, :], y1[:, k:k + 2, :]))
                    nc.vector.tensor_tensor(sT_lo[:, k:k + 2, :], y1[:, k:k + 2, :], sT_hi[:, k:k + 2, :],
                                            ALU.subtract).then_inc(s_ready, 1)

            n_ss = 0
            x_updates = 0
            n_proj = 0
            for l in range(2):
                if l == 0:
                    stream_to(-1) if False else None
                    while items[raw_at[0]][0] == "ada":
                        accumulate_ada(raw_at[0], items[raw_at[0]][1], items[raw_at[0]][2])
                        raw_at[0] += 1
                    normalise(n_ss)
                    modulation(0, 0)
                    stream_to(LEAD - 1)
                else:
                    normalise(n_ss)
                n_ss += 2
                for kt in range(KD):
                    dve.wait_ge(feat_hi, 8 * l + kt + 1)
                    step(nc.vector.tensor_copy(hT_hi[:, kt, :], h1[:, kt, :]))
                    nc.vector.tensor_tensor(hT_lo[:, kt, :], h1[:, kt, :], hT_hi[:, kt, :], ALU.subtract)\
                      .then_inc(feat_ready, 1)
                for n, c in enumerate(IN1_ORDER):
                    stream_to(w_at[("in1", l, c)] + LEAD)
                    if n == 2:
                        dve.wait_ge(proj_ready, n_proj + 2)
                        pooling(l)
                    if n == 6:
                        dve.wait_ge(proj_ready, n_proj + 6)
                        conv(l)
                    if n == 8:
                        dve.wait_ge(proj_ready, n_proj + 8)
                        dve.wait_ge(mixed_ps, l + 1)
                        for g in range(4):
                            step(nc.vector.scalar_tensor_tensor(
                                out=y1[:, 4 + g, :], in0=acc[:, 6 + g // 2, (g % 2) * T:(g % 2) * T + T],
                                scalar=colA[:, A_POOL + 4 * l + g:A_POOL + 4 * l + g + 1], in1=pf[:, 20 + g, :],
                                op0=ALU.mult, op1=ALU.mult))
                        y_split(4, 4)
                    if n == 9:
                        modulation(l, 1)
                    if n == 10:
                        dve.wait_ge(proj_ready, n_proj + 10)
                        step(nc.vector.tensor_tensor(v1[:, :, :], v1[:, :, :], pf[:, 12:16, :], ALU.mult))
                for hf in range(2):
                    dve.wait_ge(proj_ready, n_proj + 11 + hf)
                    step(nc.vector.tensor_tensor(y1[:, 2 * hf:2 * hf + 2, :], v1[:, 2 * hf:2 * hf + 2, :],
                                                 pf[:, 4 + 2 * hf:6 + 2 * hf, :], ALU.mult))
                    y_split(2 * hf, 2)
                n_proj += 12
                if l == 0:
                    modulation(1, 0)
                for c in OUT1_ORDER:
                    stream_to(w_at[("out1", l, c)] + LEAD)
                dve.wait_ge(gate_sb, l + 1)
                for tt in range(TT):
                    dve.wait_ge(ss_ready, n_ss + tt + 1)
                    rsqrt(rs[:, 2 + tt:3 + tt], stat[:, 2 + tt:3 + tt], 1, 1.0 / D)
                    step(nc.vector.scalar_tensor_tensor(
                        out=xn[:, tt, :], in0=acc[:, 4 + 2 * tt:6 + 2 * tt, :].rearrange("p b n -> p (b n)"),
                        scalar=rs[:, 2 + tt:3 + tt], in1=gate_row[:, :], op0=ALU.mult, op1=ALU.mult))
                    nc.vector.tensor_tensor(x[:, tt, :], x[:, tt, :], xn[:, tt, :], ALU.add).then_inc(x_ready, 1)
                n_ss += 2
                dve.wait_ge(x_ready, 2 * (l + 1))

            gain_of = {0: A_F1, 1: A_F2, 2: A_F1 + KD, 3: A_F2 + KD}

            def ffn_all(q, n_ss):
                normalise(n_ss)
                g0 = gain_of[q]
                to_features(CONV_FFN[q], hT_hi, hT_lo, scale=lambda kt: colA[:, g0 + kt:g0 + kt + 1])
                ffn(q)
                residual(OUT_FFN[q], 0.5)

            def attention(first, last):
                for i in range(first, last + 2):
                    if i < last:
                        s = att_steps[i]
                        b = i % 2
                        dve.wait_ge(qk_ps, i + 1)
                        if i >= first + 2:
                            dve.wait_ge(probs_turned, i - 1)
                        n = nk(s)
                        S = acc[:, 2 * b:2 * b + 2, :]
                        if s[0] == "cmp":
                            half = s[2]
                            scv = sc[:, b, 0:8 * n].rearrange("p (e h n) -> p e h n", e=2, h=4)
                            bv = bias_c[:, s[1], 8 * half:8 * half + 8, :].rearrange("p (h e) n -> p e h n", e=2)
                            step(nc.vector.tensor_tensor(scv, S[:, :, 0:4 * n].rearrange("p e (h n) -> p e h n", h=4),
                                                         bv, ALU.add))
                            flat = sc[:, b, 0:8 * n].rearrange("p (m n) -> p m n", m=8)
                            step(nc.vector.tensor_reduce(out=nmax[:, b, :], in_=flat, axis=AX.X, op=ALU.max))
                            nc.vector.tensor_tensor(flat, flat, nmax[:, b, :].unsqueeze(2).to_broadcast([P, 8, n]),
                                                    ALU.subtract).then_inc(scored, 1)
                        else:
                            off = P if s[2] == 0 else 0
                            scv = sc[:, b, 0:4 * n].rearrange("p (e h n) -> p e h n", e=2, h=2)
                            if s[0] == "diff":
                                bv = bias.rearrange("p (h e) s -> p h e s", e=2)[:, 2 * s[1]:2 * s[1] + 2, 1,
                                                                                off:off + n]
                                for e in range(2):
                                    ins = nc.vector.tensor_tensor(
                                        scv[:, e], S[:, e, :].rearrange("p (h s) -> p h s", h=2)[:, :, 0:n], bv,
                                        ALU.add)
                                    step(ins)
                            else:
                                bv = bias[:, 4 * s[1]:4 * s[1] + 4, off:off + n].rearrange(
                                    "p (h e) s -> p e h s", e=2)
                                step(nc.vector.tensor_tensor(
                                    scv, S.rearrange("p e (h s) -> p e h s", h=2)[:, :, :, 0:n], bv, ALU.add))
                            flat = sc[:, b, 0:4 * n].rearrange("p (m n) -> p m n", m=4)
                            nc.vector.tensor_reduce(out=nmax[:, b, 0:4], in_=flat, axis=AX.X, op=ALU.max,
                                                    negate=True).then_inc(scored, 1)
                    if first < i <= last:
                        j = i - 1
                        s = att_steps[j]
                        n = nk(s)
                        if s[0] == "cmp":
                            dve.wait_ge(probs, j + 1)
                            flat = sc[:, j % 2, 0:8 * n].rearrange("p (m n) -> p m n", m=8)
                            step(nc.vector.tensor_reduce(out=psums[:, j % 4, :], in_=flat, axis=AX.X, op=ALU.add))
                            nc.vector.tensor_tensor(flat, flat,
                                                    dist_c[:, s[1], :].unsqueeze(1).to_broadcast([P, 8, n]),
                                                    ALU.mult).then_inc(mixed, 1)
                        elif s[0] == "diff":
                            dve.wait_ge(probs, j + 1)
                            pv = sc[:, j % 2, 0:4 * n].rearrange("p (m n) -> p m n", m=4)
                            ps = psums[:, j % 4, :]
                            step(nc.vector.reciprocal(ps[:, 0:4], ps[:, 0:4]))
                            step(nc.vector.tensor_scalar(ps[:, 2:4], ps[:, 2:4], lam_s[:, 5:6], None, ALU.mult))
                            for h in range(2):
                                step(nc.vector.tensor_scalar(pv[:, 2 + h, :], pv[:, 2 + h, :], ps[:, 2 + h:3 + h],
                                                             None, ALU.mult))
                                ins = nc.vector.scalar_tensor_tensor(out=pv[:, h, :], in0=pv[:, h, :],
                                                                     scalar=ps[:, h:h + 1], in1=pv[:, 2 + h, :],
                                                                     op0=ALU.mult, op1=ALU.add)
                                if h == 0:
                                    step(ins)
                            ins.then_inc(mixed, 1)
                        if mapsA[j][1] != (mapsA[j + 1][1] if j + 1 < NA else nd):
                            dve.wait_ge(probs_turned, j + 1)
                            if j >= first + 2:
                                dve.wait_ge(pv_ps, j - 1)
                            m = NCMP if s[0] == "cmp" else P
                            nc.vector.tensor_copy(pT[0:m, j % 2, 512:1024], acc[0:m, 5, :]).then_inc(pT_dve, 1)
                    if i >= first + 2:
                        j = i - 2
                        s = att_steps[j]
                        dve.wait_ge(pv_ps, j + 1)
                        O = acc[:, 6 + j % 2, :]
                        if s[0] == "diff":
                            nc.vector.tensor_copy(xn[:, s[2], s[1] * 256:(s[1] + 1) * 256], O[:, 0:256])\
                              .then_inc(combined, 1)
                            continue
                        br = {"cmp": 0, "sel": 1, "win": 2}[s[0]]
                        tt = s[1] if s[0] == "cmp" else s[2]
                        nh = 8 if s[0] == "cmp" else 4
                        h0 = 8 * s[2] if s[0] == "cmp" else 4 * s[1]
                        ps = psums[:, j % 4, 0:nh]
                        gv = gates[:, tt, 3 * h0:3 * (h0 + nh)].rearrange("p (h e b) -> p e h b", e=2, b=3)[:, :, :, br]
                        step(nc.vector.reciprocal(rw[:, 0:nh], ps))
                        rv = rw[:, 0:nh].rearrange("p (e h) -> p e h", e=2)
                        step(nc.vector.tensor_tensor(rv, rv, gv, ALU.mult))
                        Ov = O[:, 0:nh * DH].rearrange("p (m d) -> p m d", d=DH)
                        tv = otmp[:, 0:nh * DH].rearrange("p (m d) -> p m d", d=DH)
                        ov = xn[:, tt, h0 * DH:(h0 + nh) * DH].rearrange("p (h e d) -> p e h d", e=2, d=DH)
                        rb = rw[:, 0:nh].unsqueeze(2).to_broadcast([P, nh, DH])
                        step(nc.vector.tensor_tensor(tv, Ov, rb, ALU.mult))
                        tv4 = otmp[:, 0:nh * DH].rearrange("p (e h d) -> p e h d", e=2, d=DH)
                        if s[0] == "sel":
                            nc.vector.tensor_copy(ov, tv4).then_inc(combined, 1)
                        else:
                            nc.vector.tensor_tensor(ov, ov, tv4, ALU.add).then_inc(combined, 1)
                        dve.wait_ge(combined, j + 1)

            ffn_all(0, n_ss)
            n_ss += 2
            normalise(n_ss)
            n_ss += 2
            to_features(CONV_NSA, hT_hi, hT_lo, scale=lambda kt: colA[:, A_MIX + kt:A_MIX + kt + 1])
            for n, c in enumerate(NSA_ORDER):
                stream_to(w_at[("nsa", c)] + LEAD)
                if n == 4:
                    for kv in range(2):
                        for hb in range(2):
                            dve.wait_ge(kc_ps, 2 * kv + hb + 1)
                            step(nc.vector.tensor_copy(
                                kcT[DH:P, kv, 2 * hb:2 * hb + 2, 0:T - 1],
                                acc[DH:P, 4 + 2 * kv + hb, :].rearrange("p (h t) -> p h t", h=2)[:, :, 1:T]))
                    dve.wait_ge(kc_act, 4)
                    for kv in range(2):
                        kv_v = kcT[:, kv].rearrange("p h (n m r) -> p m h n r", m=8, r=2)
                        for mh in range(2):
                            src = kv_v[:, :, :, mh:mh + NCMP, 0]
                            dst = cmpR[:, kv, 8 * mh:8 * mh + 8, :].rearrange("p m (h n) -> p m h n", h=HKV)
                            pos = colB[:, B_POS + 16 * kv + 8 * mh:B_POS + 16 * kv + 8 * mh + 8]
                            step(nc.vector.tensor_tensor(
                                dst, src, pos.unsqueeze(2).unsqueeze(3).to_broadcast([P, 8, HKV, NCMP]), ALU.add))
                        step(nc.vector.tensor_copy(cmp_hi[:, kv], cmpR[:, kv]))
                        nc.vector.tensor_tensor(cmp_lo[:, kv], cmpR[:, kv], cmp_hi[:, kv], ALU.subtract)\
                          .then_inc(cmpr_ready, 1)
            stream_to(w_at[("cmp", 0, 0)] + LEAD)
            dve.wait_ge(gexp_ready, 1)
            step(nc.vector.tensor_scalar(gates[:, :, :], gates[:, :, :], 1.0, None, ALU.add))
            step(nc.vector.reciprocal(gates[:, :, :], gates[:, :, :]))
            dve.sem_inc(gexp_ready, 1)
            for tt in range(TT):
                dve.wait_ge(qsq_ready, 2 * tt + 2)
                step(nc.vector.tensor_reduce(out=stat[:, 8 + 24 * tt:32 + 24 * tt],
                                             in_=scratch[:, 0:24 * DH].rearrange("p (g d) -> p g d", d=DH),
                                             axis=AX.X, op=ALU.add))
                dve.sem_inc(sq_free, 1)
            stream_to(w_at[("cmp", 0, 1)] + LEAD)
            rsqrt(rs[:, 8:56], stat[:, 8:56], 48, 1.0 / DH)
            for tt in range(TT):
                qv = pj[:, tt, 0:D].rearrange("p (h d) -> p h d", d=DH)
                rq = rs[:, 8 + 24 * tt:24 + 24 * tt].unsqueeze(2).to_broadcast([P, HQ, DH])
                nc.vector.tensor_tensor(qv, qv, rq, ALU.mult).then_inc(qn_ready, 1)
                for b in range(2):
                    kv_ = pj[:, tt, 1536 + 512 * b:1792 + 512 * b].rearrange("p (h d) -> p h d", d=DH)
                    rk = rs[:, 24 + 24 * tt + 4 * b:28 + 24 * tt + 4 * b]
                    shape = [P, HKV, 2, DH]
                    nc.vector.tensor_tensor(twice[:, tt, b], kv_.unsqueeze(2).to_broadcast(shape),
                                            rk.unsqueeze(2).unsqueeze(3).to_broadcast(shape),
                                            ALU.mult).then_inc(qn_ready, 1)
            stream_to(w_at[("cmp", 1, 0)] + LEAD)
            for rnd in range(2):
                for b in (1, 3):
                    dve.wait_ge(qk_turned, 4 * rnd + b + 1)
                    dst = (qT if rnd == 0 else kT)[:, 2 * b:2 * b + 2, :]
                    gcol = gq[:, 0:1] if rnd == 0 else colB[:, B_NK + 1 + b // 2:B_NK + 2 + b // 2]
                    nc.vector.tensor_scalar(dst, acc[:, b, :].rearrange("p (h t) -> p h t", h=2), gcol, None,
                                            ALU.mult).then_inc(qk_dve, 1)
            stream_to(w_at[("cmp", 1, 1)] + LEAD)
            dve.wait_ge(cmpk_sq, 1)
            nk_rows = HKV * NCMP
            rsqrt(rs[0:nk_rows, 4:5], stat[0:nk_rows, 4:5], 1, 1.0 / DH, parts=nk_rows)
            for c in range(2):
                ins = nc.vector.tensor_scalar(kcn[:, c, :], acc[0:nk_rows, 4, 0:DH], rs[0:nk_rows, 4:5], None, ALU.mult)
                ins.then_inc(kcn_ready, 1)
            dve.wait_ge(bias_ready, 1)
            attention(0, NS)
            for tt in range(TT):
                dve.sem_inc(xn_ready, 1)
            to_features(CONV_NSA_O, sT_hi, sT_lo)
            for c in range(4):
                stream_to(w_at[("nsao", c)] + LEAD)
            residual(OUT_NSA, 1.0)
            ffn_all(1, n_ss)
            n_ss += 2
            ffn_all(2, n_ss)
            n_ss += 2
            normalise(n_ss)
            n_ss += 2
            to_features(CONV_DIFF, hT_hi, hT_lo, scale=lambda kt: colA[:, A_MIX + KD + kt:A_MIX + KD + kt + 1])
            for n in range(12):
                stream_to(w_at[("diff", n)] + LEAD)
            for tt in range(TT):
                dve.wait_ge(qsq_ready, 4 + tt + 1)
                step(nc.vector.tensor_reduce(out=stat[:, 32 * tt:32 * tt + 32],
                                             in_=scratch[:, 0:2 * D].rearrange("p (g d) -> p g d", d=DH), axis=AX.X,
                                             op=ALU.add))
                dve.sem_inc(sq_free, 1)
            rsqrt(rs[:, 0:64], stat[:, 0:64], 64, 1.0 / DH)
            for tt in range(TT):
                qv = pd[:, tt, 0:2 * D].rearrange("p (h d) -> p h d", d=DH)
                rq = rs[:, 32 * tt:32 * tt + 32].unsqueeze(2).to_broadcast([P, 32, DH])
                nc.vector.tensor_tensor(qv, qv, rq, ALU.mult).then_inc(qn_ready, 1)
            for b in (1, 3, 5, 7):
                dve.wait_ge(qk_turned, 8 + b + 1)
                dst = (qT if b < 4 else kT)[:, 2 * (b % 4):2 * (b % 4) + 2, :]
                gcol = gq[:, 1:2] if b < 4 else colB[:, B_DK:B_DK + 1]
                nc.vector.tensor_scalar(dst, acc[:, b, :].rearrange("p (h t) -> p h t", h=2), gcol, None,
                                        ALU.mult).then_inc(qk_dve, 1)
            dve.wait_ge(gexp_ready, 3)
            step(nc.vector.tensor_tensor(lam_s[:, 4:5], lam_s[:, 3:4], lam_s[:, 2:3], ALU.subtract))
            step(nc.vector.tensor_scalar(lam_s[:, 5:6], lam_s[:, 4:5], LAM_INIT, None, ALU.subtract))
            attention(NS, NA)
            for tt in range(TT):
                dve.wait_ge(osq_ready, tt + 1)
                step(nc.vector.tensor_reduce(out=stat[:, 8 * tt:8 * tt + 8],
                                             in_=scratch[:, tt * D:(tt + 1) * D].rearrange("p (g d) -> p g d", d=P),
                                             axis=AX.X, op=ALU.add))
            rsqrt(rs[:, 0:16], stat[:, 0:16], 16, 1.0 / P)
            for tt in range(TT):
                ov = xn[:, tt, :].rearrange("p (h d) -> p h d", d=P)
                ro = rs[:, 8 * tt:8 * tt + 8].unsqueeze(2).to_broadcast([P, DIFF_H, P])
                nc.vector.tensor_tensor(ov, ov, ro, ALU.mult).then_inc(xn_ready, 1)
            to_features(CONV_DIFF_O, sT_hi, sT_lo, scale=lambda kt: gsub[:, 0:1])
            for c in range(4):
                stream_to(w_at[("diffo", c)] + LEAD)
            residual(OUT_DIFF, 1.0)
            ffn_all(3, n_ss)

        @block.tensor
        def _(pe):
            def turn(f):
                for tt in range(TT):
                    pe.wait_ge(xn_ready, 2 * f + tt + 1)
                    for kt in range(KD):
                        ins = nc.tensor.transpose(acc[:, kt // 2, (kt % 2) * T + tt * P:(kt % 2) * T + tt * P + P],
                                                  xn[:, tt, kt * P:(kt + 1) * P], ident[:, :])
                        if tt == 1 and kt % 2 == 1:
                            ins.then_inc(turned, 1)

            def chunk_ready(w, it=0):
                pe.wait_ge(raw_done, it * 4 + (w_raw[w] + 1))

            def cols_by_tokens(w, bank, it=0, first=None):
                s = w % SPL
                hi = whi[:, s, :].rearrange("p (k n) -> p k n", k=8)
                lo = wlo[:, s, :].rearrange("p (k n) -> p k n", k=8)
                for ft in range(2):
                    o = acc[:, bank, ft * T:(ft + 1) * T]
                    cs = slice(ft * P, (ft + 1) * P)
                    for kt in range(KD):
                        if first is not None and ft == 0 and kt % 2 == 0:
                            pe.wait_ge(feat_ready, 8 * first + kt + 2)
                        nc.tensor.matmul(o, hi[:, kt, cs], hT_hi[:, kt, :], start=kt == 0, stop=False)
                        nc.tensor.matmul(o, hi[:, kt, cs], hT_lo[:, kt, :], start=False, stop=False)
                        ins = nc.tensor.matmul(o, lo[:, kt, cs], hT_hi[:, kt, :], start=False, stop=kt == KD - 1)
                ins.then_inc(chunk_used, 1)

            def tokens_by_cols(w, bank, n=CC, first=None):
                s = w % SPL
                hi = whi[:, s, 0:8 * n].rearrange("p (k n) -> p k n", k=8)
                lo = wlo[:, s, 0:8 * n].rearrange("p (k n) -> p k n", k=8)
                for tt in range(TT):
                    o = acc[:, bank, tt * T:tt * T + n]
                    ts = slice(tt * P, (tt + 1) * P)
                    for kt in range(KD):
                        if first is not None and tt == 0 and kt % 2 == 0:
                            pe.wait_ge(feat_ready, 8 * first + kt + 2)
                        nc.tensor.matmul(o, hT_hi[:, kt, ts], hi[:, kt, :], start=kt == 0, stop=False)
                        nc.tensor.matmul(o, hT_hi[:, kt, ts], lo[:, kt, :], start=False, stop=False)
                        ins = nc.tensor.matmul(o, hT_lo[:, kt, ts], hi[:, kt, :], start=False, stop=kt == KD - 1)
                ins.then_inc(chunk_used, 1)

            def out_chunk(w, kts, start, stop):
                s = w % SPL
                hi = whi[:, s, :].rearrange("p (k n) -> p k n", k=2)
                lo = wlo[:, s, :].rearrange("p (k n) -> p k n", k=2)
                for tt in range(TT):
                    ts = slice(tt * P, (tt + 1) * P)
                    for nh in range(2):
                        o = acc[:, 4 + 2 * tt + nh, :]
                        ns = slice(nh * 512, (nh + 1) * 512)
                        for k in range(2):
                            sh, sl = (v[:, kts[k], ts] if isinstance(kts[k], int) else
                                      v[:, bass.ds(kts[k], 1), ts].rearrange("p k t -> p (k t)")
                                      for v in (sT_hi, sT_lo))
                            nc.tensor.matmul(o, sh, hi[:, k, ns], start=start and k == 0, stop=False)
                            nc.tensor.matmul(o, sh, lo[:, k, ns], start=False, stop=False)
                            ins = nc.tensor.matmul(o, sl, hi[:, k, ns], start=False, stop=stop and k == 1)
                        if stop and tt + nh < 2:
                            ins.then_inc(y_ps, 1)
                ins.then_inc(chunk_used, 1)

            pe.wait_ge(consts_ready, 2)
            pe.wait_ge(params_landed, 16 * N_PARAMS)
            nc.tensor.transpose(acc[:, 0, 0:A_N], rowsA[0:A_N, :], ident[0:A_N, 0:A_N])
            nc.tensor.transpose(acc[:, 1, 0:B_N], rowsB[0:B_N, :], ident[0:B_N, 0:B_N]).then_inc(cols_ready, 1)

            def sum_modulation(l, part):
                pe.wait_ge(ada_ready, 2 * l + part + 1)
                for j in (range(0, 16) if part == 0 else range(16, 24)):
                    ins = nc.tensor.matmul(acc[:, 6, j:j + 1], acc_ada[:, j * P:(j + 1) * P], ones[:, 0:1],
                                           start=True, stop=True)
                ins.then_inc(mod_ps, 1)

            sum_modulation(0, 0)
            n_s = n_proj = 0
            for l in range(2):
                turn(l)
                for n, c in enumerate(IN1_ORDER):
                    w = w_at[("in1", l, c)]
                    chunk_ready(w)
                    if n >= 4:
                        pe.wait_ge(proj_ready, n_proj + n - 3)
                    elif n == 0:
                        pe.wait_ge(feat_ready, 8 * l + 8)
                    cols_by_tokens(w, n % 4)
                    if n == 6:
                        pe.wait_ge(wsmall_landed, 48)
                        pe.wait_ge(pooled_ready, l + 1)
                        for g in range(4):
                            ins = nc.tensor.matmul(acc[:, 6 + g // 2, (g % 2) * T:(g % 2) * T + T], wpool[:, l, g, :],
                                                   pool_b[:, g, :], start=True, stop=True)
                        ins.then_inc(mixed_ps, 1)
                    if n == 8:
                        pe.wait_ge(s_ready, n_s + 2)
                        sum_modulation(l, 1)
                    if n == 10:
                        pe.wait_ge(diag_ready, 3 * (l + 1) if l == 0 else 6)
                        for nh in range(2):
                            ins = nc.tensor.matmul(acc[:, 4 + nh, :], ones[:, :], diag[:, nh * 512:(nh + 1) * 512],
                                                   start=True, stop=True)
                        ins.then_inc(gate_ps, 1)
                n_proj += 12
                if l == 0:
                    sum_modulation(1, 0)
                    pe.wait_ge(diag_ready, 4)
                pe.wait_ge(gate_sb, l + 1)
                for n, c in enumerate(OUT1_ORDER):
                    w = w_at[("out1", l, c)]
                    chunk_ready(w)
                    pe.wait_ge(s_ready, n_s + n + 1)
                    out_chunk(w, [2 * c, 2 * c + 1], n == 0, n == 3)
                n_s += 4

            def ffn(q, n_s):
                f = CONV_FFN[q]
                turn(f)
                w0 = w_at[("fin", q, 0, 0)]

                def in_chunk(c, it=0, half=None):
                    chunk_ready(w0 + c, it)
                    j = c // 2
                    pe.wait_ge(silu_ready if c % 2 == 0 else gated, it * 2 + (NPAIR * q + j))
                    cols_by_tokens(w0 + c, c % 4)

                pe.wait_ge(feat_ready, 8 * f + 8)
                with pe.Fori(0, 5) as it:
                    for c in range(4):
                        in_chunk(c, it)
                in_chunk(20)
                in_chunk(21)
                w1 = w0 + 22

                chunk_ready(w1)
                pe.wait_ge(s_ready, n_s + 1)
                out_chunk(w1, [0, 1], True, False)
                with pe.Fori(0, 2) as it:
                    for c in range(4):
                        chunk_ready(w1 + 1 + c, it)
                        pe.wait_ge(s_ready, it * 4 + (n_s + 2 + c))
                        out_chunk(w1 + 1 + c, [it * 8 + (2 + 2 * c), it * 8 + (3 + 2 * c)], False, False)
                for c in (9, 10):
                    chunk_ready(w1 + c)
                    pe.wait_ge(s_ready, n_s + c + 1)
                    out_chunk(w1 + c, [2 * c, 2 * c + 1], False, c == 10)

            def scores(i):
                s = att_steps[i]
                b = 2 * (i % 2)
                n = nk(s)
                for m in range(8 if s[0] == "cmp" else 4):
                    if s[0] == "cmp":
                        tt, h = s[1], 8 * s[2] + m
                        e, slot = m % 2, m // 2
                        q, k = qT[e * DH:(e + 1) * DH, h // 2, tt * P:(tt + 1) * P], \
                            kcmpT[e * DH:(e + 1) * DH, (h // G) * NCMP:(h // G + 1) * NCMP]
                        o = acc[:, b + e, slot * n:slot * n + n]
                    elif s[0] == "diff":
                        tt = s[2]
                        e, slot = m % 2, m // 2
                        h = 2 * s[1] + slot
                        q, k = qT[e * DH:(e + 1) * DH, h, tt * P:(tt + 1) * P], kT[e * DH:(e + 1) * DH, h, 0:n]
                        o = acc[:, b + e, slot * T:slot * T + n]
                    else:
                        tt, h = s[2], 4 * s[1] + m
                        e, slot = m % 2, m // 2
                        br = 0 if s[0] == "sel" else 4
                        q, k = qT[e * DH:(e + 1) * DH, h // 2, tt * P:(tt + 1) * P], \
                            kT[e * DH:(e + 1) * DH, br + s[1], 0:n] if False else \
                            kT[e * DH:(e + 1) * DH, br + s[1], 0:n]
                        o = acc[:, b + e, slot * T:slot * T + n]
                    ins = nc.tensor.matmul(o, q, k, start=True, stop=True)
                ins.then_inc(qk_ps, 1)

            def turn_probs(i):
                s = att_steps[i]
                b = i % 2
                n = nk(s)
                if s[0] == "cmp":
                    for m in range(8):
                        ins = nc.tensor.transpose(acc[0:NCMP, 4 + m // 4, (m % 4) * P:(m % 4 + 1) * P],
                                                  sc[:, b, m * n:(m + 1) * n], ident[:, :])
                else:
                    blocks = s[2] + 1
                    for m in range(2 if s[0] == "diff" else 4):
                        for kt in range(blocks):
                            at = (m + 2 * kt if s[0] == "diff" else m + 4 * kt) * P
                            ins = nc.tensor.transpose(acc[:, 4 + at // 512, at % 512:at % 512 + P],
                                                      sc[:, b, m * n + kt * P:m * n + (kt + 1) * P], ident[:, :])
                ins.then_inc(probs_turned, 1)

            def values(i):
                s = att_steps[i]
                b = i % 2
                O = acc[:, 6 + i % 2, :]
                if s[0] == "cmp":
                    for m in range(8):
                        h = 8 * s[2] + 2 * (m % 4) + m // 4
                        ins = nc.tensor.matmul(O[:, m * DH:(m + 1) * DH], pT[0:NCMP, b, m * P:(m + 1) * P],
                                               vcmp[:, h // G, :], start=True, stop=True)
                else:
                    blocks = s[2] + 1
                    diff = s[0] == "diff"
                    for m in range(2 if diff else 4):
                        for kt in range(blocks):
                            at = (m + 2 * kt if diff else m + 4 * kt) * P
                            if diff:
                                v = pd[:, kt, 2 * D + (2 * s[1] + m) * P:2 * D + (2 * s[1] + m + 1) * P]
                                o = O[:, m * P:(m + 1) * P]
                            else:
                                c0 = (1792 if s[0] == "sel" else 2304) + s[1] * DH
                                v = pj[:, kt, c0:c0 + DH]
                                o = O[:, m * DH:(m + 1) * DH]
                            ins = nc.tensor.matmul(o, pT[:, b, at:at + P], v, start=kt == 0, stop=kt == blocks - 1)
                ins.then_inc(pv_ps, 1)

            def attention(first, last):
                n_mixed = 0 if first == 0 else NS - 16
                for i in range(first, last + 2):
                    if i < last:
                        if i >= first + 2:
                            pe.wait_ge(scored, i - 1)
                        scores(i)
                    if first < i <= last:
                        j = i - 1
                        s = att_steps[j]
                        pe.wait_ge(probs, j + 1)
                        if s[0] in ("cmp", "diff"):
                            n_mixed += 1
                            pe.wait_ge(mixed, n_mixed)
                        if j > first:
                            pe.wait_ge(pT_act, mapsA[j][0])
                            if mapsA[j][1]:
                                pe.wait_ge(pT_dve, mapsA[j][1])
                        turn_probs(j)
                    if i >= first + 2:
                        j = i - 2
                        pe.wait_ge(pT_act, mapsA[j][0] + 1)
                        n_dve = mapsA[j + 1][1] if j + 1 < NA else nd
                        if n_dve:
                            pe.wait_ge(pT_dve, n_dve)
                        if j >= first + 2:
                            pe.wait_ge(combined, j - 1)
                        values(j)

            ffn(0, n_s)
            n_s += NPAIR
            turn(CONV_NSA)
            for n, c in enumerate(NSA_ORDER):
                w = w_at[("nsa", c)]
                chunk_ready(w)
                if n >= 4:
                    pe.wait_ge(proj_ready, n_proj + n - 3)
                tokens_by_cols(w, n % 4, NGATE if c == 10 else CC, first=CONV_NSA if n == 0 else None)
                if n == 3:
                    for kv in range(2):
                        pe.wait_ge(proj_ready, n_proj + kv + 1)
                        for h in range(HKV):
                            for tt in range(TT):
                                src = xn[:, tt, (4 * kv + h) * P:(4 * kv + h + 1) * P]
                                ins = nc.tensor.transpose(
                                    acc[:, 4 + 2 * kv + h // 2, (h % 2) * T + tt * P:(h % 2) * T + tt * P + P],
                                    src, ident[:, :])
                            if h % 2 == 1:
                                ins.then_inc(kc_ps, 1)
            n_proj += 11

            for kv in range(2):
                pe.wait_ge(cmpr_ready, kv + 1)
                for half in range(2):
                    w = w_at[("cmp", kv, half)]
                    chunk_ready(w)
                    hi = whi[:, w % SPL, :].rearrange("p (k n) -> p k n", k=8)
                    lo = wlo[:, w % SPL, :].rearrange("p (k n) -> p k n", k=8)
                    for ct in range(2):
                        o = acc[:, 4 + 2 * kv + ct, 0:HKV * NCMP]
                        cs = slice(ct * P, (ct + 1) * P)
                        for k in range(8):
                            m = 8 * half + k
                            nc.tensor.matmul(o, hi[:, k, cs], cmp_hi[:, kv, m, :], start=m == 0, stop=False)
                            nc.tensor.matmul(o, hi[:, k, cs], cmp_lo[:, kv, m, :], start=False, stop=False)
                            ins = nc.tensor.matmul(o, lo[:, k, cs], cmp_hi[:, kv, m, :], start=False, stop=m == 15)
                    if half == 0:
                        ins.then_inc(chunk_used, 1)
                    else:
                        ins.then_inc(cmph_ps, 1)
                        pe.sem_inc(chunk_used, 1) if False else None
                        pe.wait_ge(cmph_ps, kv + 1)
                        pe.sem_inc(chunk_used, 1)

            def turn_heads(src, bank, pair, tt):
                return nc.tensor.transpose(acc[:, bank, (pair % 2) * T + tt * P:(pair % 2) * T + tt * P + P], src,
                                           ident[:, :])

            pe.wait_ge(qn_ready, 6)
            pe.wait_ge(proj_ready, n_proj)
            for pair in range(8):
                for tt in range(TT):
                    ins = turn_heads(pj[:, tt, pair * P:(pair + 1) * P], pair // 2, pair, tt)
                if pair % 2 == 1:
                    ins.then_inc(qk_turned, 1)
            for b in range(2):
                for h in range(HKV):
                    k = 4 * b + h
                    if h % 2 == 0:
                        if (k // 2) % 2 == 0:
                            pe.wait_ge(qk_act, k // 4 + 1)
                        else:
                            pe.wait_ge(qk_dve, k // 4 + 1)
                    for tt in range(TT):
                        ins = turn_heads(xn[:, tt, k * P:(k + 1) * P], k // 2, k, tt)
                    if h % 2 == 1:
                        ins.then_inc(qk_turned, 1)
            pe.wait_ge(gelu_ready, 1)
            pe.wait_ge(wsmall_landed, 48)
            for ct in range(2):
                ins = nc.tensor.matmul(acc[0:HKV * NCMP, 4, 0:DH], cmp_g[:, 0, ct, :], w2[:, 0, ct, :],
                                       start=ct == 0, stop=ct == 1)
            ins.then_inc(cmpk_ps, 1)
            pe.wait_ge(gelu_ready, 2)
            for h in range(HKV):
                for ct in range(2):
                    ins = nc.tensor.matmul(acc[0:NCMP, 6, h * DH:(h + 1) * DH],
                                           cmp_g[:, 1, ct, h * NCMP:(h + 1) * NCMP], w2[:, 1, ct, :],
                                           start=ct == 0, stop=ct == 1)
            ins.then_inc(cmpv_ps, 1)
            pe.wait_ge(kcn_ready, 2)
            nc.tensor.transpose(acc[:, 5, 0:HKV * NCMP], kcn.rearrange("p c d -> p (c d)"),
                                ident[0:HKV * NCMP, 0:HKV * NCMP]).then_inc(kcn_ps, 1)
            pe.wait_ge(qk_act, 4)
            pe.wait_ge(qk_dve, 4)
            pe.wait_ge(cmp_sb, 2)
            attention(0, NS)
            turn(CONV_NSA_O)
            for n in range(4):
                w = w_at[("nsao", n)]
                chunk_ready(w)
                pe.wait_ge(feat_ready, 8 * CONV_NSA_O + 2 * n + 2)
                out_chunk(w, [2 * n, 2 * n + 1], n == 0, n == 3)
            ffn(1, n_s)
            n_s += NPAIR
            ffn(2, n_s)
            n_s += NPAIR
            turn(CONV_DIFF)
            for n in range(12):
                w = w_at[("diff", n)]
                chunk_ready(w)
                if n >= 4:
                    pe.wait_ge(proj_ready, n_proj + n - 3)
                tokens_by_cols(w, n % 4, first=CONV_DIFF if n == 0 else None)
            n_proj += 12
            pe.wait_ge(qn_ready, 8)
            pe.wait_ge(proj_ready, n_proj)
            for pair in range(16):
                for tt in range(TT):
                    ins = turn_heads(pd[:, tt, pair * P:(pair + 1) * P], pair // 2, pair, tt)
                if pair % 2 == 1:
                    ins.then_inc(qk_turned, 1)
            pe.wait_ge(qk_act, 8)
            pe.wait_ge(qk_dve, 8)
            attention(NS, NA)
            turn(CONV_DIFF_O)
            for n in range(4):
                w = w_at[("diffo", n)]
                chunk_ready(w)
                pe.wait_ge(feat_ready, 8 * CONV_DIFF_O + 2 * n + 2)
                out_chunk(w, [2 * n, 2 * n + 1], n == 0, n == 3)
            ffn(3, n_s)


N_PARAMS = 19


_USED = ["x", "c", "w_ada", "b_ada", "g_pre", "w_in", "w_conv", "w_pool", "pool_scale", "w_out", "g_post",
         "ffn1_norm_2", "ffn1_w_in_2", "ffn1_w_out_2", "mix_norm_2", "ffn2_norm_2", "ffn2_w_in_2", "ffn2_w_out_2",
         "nsa_w_in_2", "nsa_w_out_2", "nsa_q_norm_2", "nsa_k_norm_2", "nsa_cmp_pos_2", "nsa_cmp_w1_2",
         "nsa_cmp_w2_2", "diff_w_in_2", "diff_w_out_2", "diff_q_norm_2", "diff_k_norm_2", "diff_lambda_2",
         "diff_subln_2"]


def kernel(**inputs):
    import numpy as _np
    import concourse.bacc as _bacc
    from concourse import mybir as _mybir
    from concourse.bass_utils import run_bass_kernel_spmd as _run

    nc = _bacc.Bacc("TRN2", target_bir_lowering=False, num_devices=1)
    arrays, args = {}, {}
    for name in _USED:
        arr = _np.ascontiguousarray(inputs[name])
        arrays[f"in_{name}_dram"] = arr
        args[name] = nc.dram_tensor(f"in_{name}_dram", arr.shape, _mybir.dt.from_np(arr.dtype),
                                    kind="ExternalInput").ap()
    out = nc.dram_tensor("out_dram", (1, T, D), F32, kind="ExternalOutput").ap()
    two_blocks_kernel(nc, args, out)
    r = _run(nc, [arrays], core_ids=[0])
    return r.results[0]["out_dram"]
```

```python
import math
from contextlib import ExitStack

import concourse.bass as bass
from concourse import mybir
from concourse.alu_op_type import AluOpType as ALU

F32 = mybir.dt.float32
F32R = mybir.dt.float32r
I32 = mybir.dt.int32
ACT = mybir.ActivationFunctionType
AX = mybir.AxisListType

P = 128
T = 256
TT = T // P
D = 1024
KD = D // P
EPS = 1e-6
NEG = -1e30

CW = 512
IN1 = 6 * CW
WINDOWS = (2, 4, 8, 16)
DFF = 2816
NPAIR = DFF // 256
DH = 64
HQ = 16
HKV = 4
G = HQ // HKV
CMP_HIDDEN = 256
CMP_TILES = 32 * DH // P
NCMP = T // 16 - 1
NSA_IN = HQ * DH + 6 * HKV * DH + 3 * HQ
NGATE = 3 * HQ
DIFF_H = 8
LAM_INIT = 0.8 - 0.6 * math.exp(-0.3)

RAW = 3
SPL = 3
LEAD = SPL - 1
CH = 2048
CC = 256

A_GPRE, A_GPOST, A_F1, A_MIX, A_F2, A_POOL, A_CONV, A_N = 0, 16, 32, 48, 64, 80, 88, 112
B_BADA, B_POS, B_NQ, B_NK, B_DQ, B_DK, B_SUB, B_N = 0, 48, 80, 81, 84, 85, 86, 87

IN1_ORDER = [8, 9, 0, 1, 4, 5, 10, 11, 6, 7, 2, 3]
OUT1_ORDER = [2, 3, 0, 1]
NSA_ORDER = [4, 5, 0, 1, 2, 3, 6, 8, 7, 9, 10]

CONV_BLK = (0, 1)
CONV_FFN = {0: 2, 1: 5, 2: 6, 3: 9}
CONV_NSA, CONV_NSA_O, CONV_DIFF, CONV_DIFF_O = 3, 4, 7, 8
OUT_BLK, OUT_NSA, OUT_DIFF = (0, 1), 3, 6
OUT_FFN = {0: 2, 1: 4, 2: 5, 3: 7}


class Tally:

    def __init__(self, sem):
        self.sem, self.n, self.it, self.per = sem, 0, None, 0

    def add(self, ins):
        ins.then_inc(self.sem, 1)
        self.n += 1
        return self.n

    def value(self, n):
        return n if self.it is None else n + self.it * self.per


def stream_items():
    items = [("ada", 0, c) for c in range(8)]
    side = [("ada", 0, c) for c in range(8, 12)] + [("ada", 1, c) for c in range(8)]
    for c in IN1_ORDER:
        items.append(("w", "in1", 0, c))
        items.append(side.pop(0))
    items += [("w", "out1", 0, c) for c in OUT1_ORDER]
    side = [("ada", 1, c) for c in range(8, 12)]
    for c in IN1_ORDER:
        items.append(("w", "in1", 1, c))
        if side:
            items.append(side.pop(0))
    items += [("w", "out1", 1, c) for c in OUT1_ORDER]

    def ffn(q):
        got = []
        for j in range(NPAIR):
            got += [("w", "fin", q, j, 0), ("w", "fin", q, j, 1)]
            if j:
                got.append(("w", "fout", q, j - 1))
        return got + [("w", "fout", q, NPAIR - 1)]

    items += ffn(0)
    items += [("w", "nsa", c) for c in NSA_ORDER]
    items += [("w", "cmp", kv, half) for kv in range(2) for half in range(2)]
    items += [("w", "nsao", c) for c in range(4)]
    items += ffn(1) + ffn(2)
    items += [("w", "diff", c) for c in range(12)]
    items += [("w", "diffo", c) for c in range(4)]
    items += ffn(3)
    return items


def two_blocks_kernel(nc, a, out):
    ctx = ExitStack()
    with ctx:
        def sb(name, shape, dt=F32):
            return ctx.enter_context(nc.sbuf_tensor(name, shape, dt))

        def sem(name):
            return ctx.enter_context(nc.semaphore(name))

        x = sb("x", [P, TT, D])
        xn = sb("xn", [P, TT, D])
        proj = sb("proj", [P, 2 * 3072])
        raw = sb("raw", [P, RAW, CH])
        whi = sb("whi", [P, SPL, CH], F32R)
        wlo = sb("wlo", [P, SPL, CH], F32R)
        hT_hi = sb("hT_hi", [P, KD, T], F32R)
        hT_lo = sb("hT_lo", [P, KD, T], F32R)
        sT_hi = sb("sT_hi", [P, KD, T], F32R)
        sT_lo = sb("sT_lo", [P, KD, T], F32R)
        bias = sb("bias", [P, HQ, T])
        wpool = bias[:, 0:4, :].rearrange("p (l g) n -> p l (g n)", l=2).rearrange("p l (g n) -> p l g n", g=4)
        gate_row = bias[:, 4:8, :].rearrange("p h n -> p (h n)")
        bias_c = sb("bias_c", [P, TT, HQ, NCMP])
        dist = sb("dist", [P, T])
        dist_c = sb("dist_c", [P, TT, NCMP])
        ident = sb("ident", [P, P])
        ones = sb("ones", [P, P])
        rowsA = xn[:, 1, 0:P]
        rowsB = xn[:, 1, P:2 * P]
        colA = sb("colA", [P, A_N])
        colB = sb("colB", [P, B_N])
        w2 = sb("w2", [P, 2, 2, DH])
        lam = sb("lam", [P, 4, DH])
        lam_s = sb("lam_s", [P, 8])
        count_fix = sb("count_fix", [P, 4, 16])
        pos1 = sb("pos1", [P, 16])
        cact = sb("cact", [P, KD])
        mod = sb("mod", [P, 24])
        gain1 = sb("gain1", [P, 2, KD])
        shift1 = sb("shift1", [P, 2, KD])
        gate_col = sb("gate_col", [P, KD])
        gq = sb("gq", [P, 2])
        gsub = sb("gsub", [P, 1])
        stat = sb("stat", [P, 64])
        rs = sb("rs", [P, 64])
        nt0 = sb("nt0", [P, 64])
        nt1 = sb("nt1", [P, 64])
        nt2 = sb("nt2", [P, 64])
        nt3 = sb("nt3", [P, 64])
        scratch = sb("scratch", [P, 2048])
        region = sb("region", [P, 7 * 1024])
        acc_ada = region[:, 0:3072]
        diag = xn[:, 0, :]
        y1 = region[:, 3072:5120].rearrange("p (k t) -> p k t", t=T)
        pool_a = region[:, 5120:6144].rearrange("p (g t) -> p g t", t=T)
        pool_b = region[:, 6144:7168].rearrange("p (g t) -> p g t", t=T)
        z1 = pool_a
        v1 = scratch[:, 0:1024].rearrange("p (g t) -> p g t", t=T)
        silu_a = region[:, 4096:5120].rearrange("p (b n) -> p b n", b=2)
        sact = region[:, 5120:5632]
        h1 = region[:, 5120:7168].rearrange("p (k t) -> p k t", t=T)
        qT = region[:, 0:2048].rearrange("p (h t) -> p h t", t=T)
        kT = region[:, 2048:4096].rearrange("p (h t) -> p h t", t=T)
        sc = region[:, 4096:6144].rearrange("p (b n) -> p b n", b=2)
        pT = scratch.rearrange("p (b n) -> p b n", b=2)
        kcT = region[:, 0:2048].rearrange("p (k h t) -> p k h t", k=2, h=HKV)
        cmpR = scratch[:, 0:1920].rearrange("p (k m n) -> p k m n", k=2, m=CMP_TILES)
        cmp_hi, cmp_lo = (v.rearrange("p k t -> p (k t)")[:, 0:1920]
                          .rearrange("p (k m n) -> p k m n", k=2, m=CMP_TILES) for v in (sT_hi, sT_lo))
        cmp_flat = [v.rearrange("p k t -> p (k t)") for v in (sT_hi, sT_lo)]
        cmp_g = region[:, 6656:6896].rearrange("p (k c n) -> p k c n", k=2, c=2)
        v60 = region[0:HKV * NCMP, 6896:6896 + DH]
        cmp_gt = region[0:HKV * NCMP, 4096:4608].rearrange("p (k n) -> p k n", k=2)
        cmp_small = sb("cmp_small", [P, 2 * DH + 2 * HKV * NCMP])
        kcn = cmp_small[0:HKV * NCMP, 0:2 * DH].rearrange("p (c d) -> p c d", c=2)
        kblk = cmp_small[:, 2 * DH:2 * DH + 2 * HKV * NCMP].rearrange("p (h m) -> p h m", h=HKV)
        sel = dist[0:HKV * NCMP, 0:240].rearrange("p (f m) -> p f m", f=2)
        vmask = sb("vmask", [8 * NCMP, 8])
        gates = sb("gates", [P, TT, NGATE])
        nmax = sb("nmax", [P, 2, HQ])
        psums = sb("psums", [P, 4, HQ])
        rw = sb("rw", [P, HQ])
        ada2 = sb("ada2", [P, CC])
        rowsC = cmp_small[0:KD, 0:P]
        otmp = region[:, 6144:6656]

        whi_f, hT_hi_f, sT_hi_f, cmp_hi_f = (v.bitcast(F32) for v in (whi[:, :, :], hT_hi[:, :, :], sT_hi[:, :, :], cmp_hi))

        acc = ctx.enter_context(nc.psum_tensor("acc", [P, 8, 512], F32))

        raw_landed = [sem(f"raw_landed{i}") for i in range(RAW)]
        params_landed = sem("params_landed")
        x_landed = sem("x_landed")
        wsmall_landed = sem("wsmall_landed")
        out_stored = sem("out_stored")
        consts_ready = sem("consts_ready")
        pool_step = sem("pool_step")
        bias_ready = sem("bias_ready")
        hi_ready = sem("hi_ready")
        raw_done = sem("raw_done")
        chunk_used = sem("chunk_used")
        cols_ready = sem("cols_ready")
        colsd_ready = sem("colsd_ready")
        cact_ready = sem("cact_ready")
        ada_ready = sem("ada_ready")
        mod_ps = sem("mod_ps")
        diag_ready = sem("diag_ready")
        gate_ps = sem("gate_ps")
        gate_sb = sem("gate_sb")
        x_ready = sem("x_ready")
        ss_ready = sem("ss_ready")
        xn_ready = sem("xn_ready")
        turned = sem("turned")
        feat_hi = sem("feat_hi")
        feat_ready = sem("feat_ready")
        proj_ready = sem("proj_ready")
        pooled_ready = sem("pooled_ready")
        mixed_ps = sem("mixed_ps")
        y_ps = sem("y_ps")
        silu_ready = sem("silu_ready")
        gated = sem("gated")
        s_ready = sem("s_ready")
        dve_step = sem("dve_step")
        act_step = sem("act_step")
        kc_ps = sem("kc_ps")
        kc_act = sem("kc_act")
        cmpr_ready = sem("cmpr_ready")
        g_turned = sem("g_turned")
        g_sb = sem("g_sb")
        vsel_ps = sem("vsel_ps")
        vblk_ready = sem("vblk_ready")
        c_landed = sem("c_landed")
        c_ps = sem("c_ps")
        gelu_ready = sem("gelu_ready")
        cmpk_ps = sem("cmpk_ps")
        cmpv_ps = sem("cmpv_ps")
        cmpk_sq = sem("cmpk_sq")
        kcn_ready = sem("kcn_ready")
        kcn_ps = sem("kcn_ps")
        cmp_sb = sem("cmp_sb")
        qsq_ready = sem("qsq_ready")
        sq_free = sem("sq_free")
        qn_ready = sem("qn_ready")
        qk_turned = sem("qk_turned")
        qk_act = sem("qk_act")
        qk_dve = sem("qk_dve")
        gexp_ready = sem("gexp_ready")
        qk_ps = sem("qk_ps")
        scored = sem("scored")
        probs = sem("probs")
        mixed = sem("mixed")
        probs_turned = sem("probs_turned")
        pT_act = sem("pT_act")
        pT_dve = sem("pT_dve")
        pv_ps = sem("pv_ps")
        combined = sem("combined")
        osq_ready = sem("osq_ready")

        items = stream_items()
        w_raw = [r for r, it in enumerate(items) if it[0] == "w"]
        w_at = {items[r][1:]: w for w, r in enumerate(w_raw)}
        NW = len(w_raw)

        def col_chunk(ap, c0, n=CC):
            return ap.rearrange("(k p) n -> p k n", p=P)[:, :, c0:c0 + n]

        def row_chunk(ap, c):
            return ap.rearrange("(c k p) n -> p c k n", p=P, k=2)[:, c, :, :]

        ffn_in = [a["ffn1_w_in_2"][0], a["ffn2_w_in_2"][0], a["ffn1_w_in_2"][1], a["ffn2_w_in_2"][1]]
        ffn_out = [a["ffn1_w_out_2"][0], a["ffn2_w_out_2"][0], a["ffn1_w_out_2"][1], a["ffn2_w_out_2"][1]]

        def source(item):
            if item[0] == "ada":
                return col_chunk(a["w_ada"][item[1]], item[2] * CC)
            kind, *at = item[1:]
            if kind == "in1":
                return col_chunk(a["w_in"][at[0]], at[1] * CC)
            if kind == "out1":
                return row_chunk(a["w_out"][at[0]], at[1])
            if kind == "fin":
                return col_chunk(ffn_in[at[0]], at[2] * DFF + at[1] * CC)
            if kind == "fout":
                return row_chunk(ffn_out[at[0]], at[1])
            if kind == "nsa":
                return col_chunk(a["nsa_w_in_2"][0], at[0] * CC, NGATE if at[0] == 10 else CC)
            if kind == "cmp":
                return a["nsa_cmp_w1_2"][0, at[0]].rearrange("(k p) n -> p k n", p=P)[:, at[1] * 8:at[1] * 8 + 8, :]
            if kind == "nsao":
                return row_chunk(a["nsa_w_out_2"][0], at[0])
            if kind == "diff":
                return col_chunk(a["diff_w_in_2"][0], at[0] * CC)
            return row_chunk(a["diff_w_out_2"][0], at[0])

        def size(item):
            return 8 * NGATE if item[1:] == ("nsa", 10) else CH

        def raw_view(slot, ap):
            k, n = ap.shape[1], ap.shape[2]
            return raw[:, slot, 0:k * n].rearrange("p (k n) -> p k n", k=k)

        out_last = [w_at[k] for k in (("out1", 0, 1), ("out1", 1, 1), ("fout", 0, 10), ("nsao", 3), ("fout", 1, 10),
                                      ("fout", 2, 10), ("diffo", 3), ("fout", 3, 10))]

        def bank_complete(eng, o, k):
            if k < 3:
                eng.wait_ge(y_ps, 3 * o + k + 1)
            else:
                eng.wait_ge(chunk_used, out_last[o] + 1)

        def pair_at(j):
            return 3 * j - 1 if j else 0

        def landed_value(r, it=0):
            return it * (16 * 6 // RAW) + 16 * (r // RAW + 1)

        block = ctx.enter_context(nc.Block())

        @block.sync
        def _(sp):
            def load(r):
                if r >= RAW:
                    sp.wait_ge(raw_done, r - RAW + 1)
                src = source(items[r])
                sp.dma_start(raw_view(r % RAW, src), src).then_inc(raw_landed[r % RAW], 16)

            def ffn_loads(q, r0):
                w_in_v = ffn_in[q].rearrange("(k p) n -> p k n", p=P)
                w_out_v = ffn_out[q].rearrange("(c k p) n -> p c k n", p=P, k=2)
                for r in range(r0, r0 + 5):
                    load(r)
                with sp.Fori(0, 4) as it:
                    for c in range(6):
                        r, j = r0 + 5 + c, 2 + c // 3
                        sp.wait_ge(raw_done, it * 6 + (r - RAW + 1))
                        if c % 3 < 2:
                            src = w_in_v[:, :, bass.ds(it * (2 * CC) + ((c % 3) * DFF + j * CC), CC)]
                            dst = raw_view(r % RAW, w_in_v[:, :, 0:CC])
                        else:
                            src = w_out_v[:, bass.ds(it * 2 + (j - 1), 1)].rearrange("p c k n -> p (c k) n")
                            dst = raw_view(r % RAW, w_out_v[:, 0])
                        sp.dma_start(dst, src).then_inc(raw_landed[r % RAW], 16)
                for r in range(r0 + 29, r0 + 33):
                    load(r)

            r = 0
            while r < len(items):
                if items[r][1] == "fin":
                    ffn_loads(items[r][2], r)
                    r += 3 * NPAIR
                else:
                    if r == RAW:
                        sp.dma_start(x[:, :, :], a["x"][0].rearrange("(t p) n -> p t n", p=P)).then_inc(x_landed, 16)
                    load(r)
                    r += 1
            for tt in range(TT):
                sp.wait_ge(x_ready, 2 * 7 + tt + 1)
                sp.dma_start(out[0].rearrange("(t p) n -> p t n", p=P)[:, tt], x[:, tt, :]).then_inc(out_stored, 16)
            sp.wait_ge(out_stored, 16 * TT)

        @block.gpsimd
        def _(pool):
            steps = Tally(pool_step)

            def step(ins):
                pool.wait_ge(pool_step, steps.add(ins))

            step(nc.gpsimd.memset(ident[:, :], 0.0))
            step(nc.gpsimd.affine_select(out=ident[:, :], in_=ident[:, :], compare_op=ALU.not_equal, fill=1.0,
                                         base=0, pattern=[[-1, P]], channel_multiplier=1))
            nc.gpsimd.iota(pos1[:, :], pattern=[[1, 16]], base=1, channel_multiplier=0,
                           allow_small_or_imprecise_dtypes=True).then_inc(consts_ready, 1)
            nc.gpsimd.memset(ones[:, :], 1.0).then_inc(consts_ready, 1)
            for at, name in ((A_GPRE, "g_pre"), (A_GPOST, "g_post"), (A_F1, "ffn1_norm_2"), (A_MIX, "mix_norm_2"),
                             (A_F2, "ffn2_norm_2")):
                pool.dma_start(rowsA[at:at + 16, :], a[name].rearrange("l (k p) -> (l k) p", p=P))\
                    .then_inc(params_landed, 16)
            pool.dma_start(rowsA[A_POOL:A_CONV, :], a["pool_scale"].rearrange("l (k p) -> (l k) p", p=P))\
               .then_inc(params_landed, 16)
            pool.dma_start(rowsA[A_CONV:A_N, :], a["w_conv"].rearrange("l j (k p) -> (l j k) p", p=P))\
               .then_inc(params_landed, 16)
            pool.dma_start(rowsB[B_BADA:B_POS, :], a["b_ada"].rearrange("l (k p) -> (l k) p", p=P))\
               .then_inc(params_landed, 16)
            pool.dma_start(rowsB[B_POS:B_NQ, :], a["nsa_cmp_pos_2"][0].rearrange("v (m j) d -> (v m) (j d)", j=2))\
               .then_inc(params_landed, 16)
            n_params = 9
            for c in range(2):
                for at, name, n in ((B_NQ, "nsa_q_norm_2", 1), (B_NK, "nsa_k_norm_2", 3), (B_DQ, "diff_q_norm_2", 1),
                                    (B_DK, "diff_k_norm_2", 1)):
                    src = a[name][0] if n == 3 else a[name]
                    pool.dma_start(rowsB[at:at + n, c * DH:(c + 1) * DH], src).then_inc(params_landed, 16)
                    n_params += 1
            pool.dma_start(rowsB[B_SUB:B_N, :], a["diff_subln_2"]).then_inc(params_landed, 16)
            n_params += 1
            pool.dma_start(wpool[:, :, :, :], a["w_pool"].rearrange("l g c d -> c l g d")).then_inc(wsmall_landed, 16)
            pool.dma_start(w2[:, :, :, :], a["nsa_cmp_w2_2"][0].rearrange("v (k p) d -> p v k d", p=P))\
               .then_inc(wsmall_landed, 16)
            pool.dma_start(lam[:, :, :], a["diff_lambda_2"][0].partition_broadcast(P)).then_inc(wsmall_landed, 16)
            assert n_params == N_PARAMS

            step(nc.gpsimd.iota(dist[:, :], pattern=[[-1, T]], base=P, channel_multiplier=1,
                                allow_small_or_imprecise_dtypes=True))
            step(nc.gpsimd.iota(dist_c[:, :, :], pattern=[[P, TT], [-16, NCMP]], base=-31, channel_multiplier=1,
                                allow_small_or_imprecise_dtypes=True))
            pool.wait_ge(x_ready, 4)
            for h in range(HQ):
                slope = 2.0 ** (-0.5 * (h + 1))
                step(nc.gpsimd.tensor_scalar(bias[:, h, :], dist[:, :], -slope, None, ALU.mult))
                step(nc.gpsimd.affine_select(out=bias[:, h, :], in_=bias[:, h, :], compare_op=ALU.is_ge,
                                             fill=NEG, base=P, pattern=[[-1, T]], channel_multiplier=1))
                step(nc.gpsimd.tensor_scalar(bias_c[:, :, h, :], dist_c[:, :, :], -slope, None, ALU.mult))
                step(nc.gpsimd.affine_select(out=bias_c[:, :, h, :], in_=bias_c[:, :, h, :], compare_op=ALU.is_ge,
                                             fill=NEG, base=-31, pattern=[[P, TT], [-16, NCMP]],
                                             channel_multiplier=1))
            step(nc.gpsimd.memset(kblk[:, :, :], 0.0))
            step(nc.gpsimd.memset(sel[:, :, :], 0.0))
            for f in range(2):
                v = sel[:, f, :].rearrange("p (j g n) -> p j g n", j=2, g=G)
                step(nc.gpsimd.affine_select(out=v, in_=v, compare_op=ALU.not_equal, fill=1.0, base=-2 * NCMP * f,
                                             pattern=[[-NCMP, 2], [0, G], [-1, NCMP]], channel_multiplier=1))
            step(nc.gpsimd.memset(vmask[:, :], 1.0))
            step(nc.gpsimd.affine_select(out=vmask[:, :], in_=vmask[:, :], compare_op=ALU.is_ge, fill=0.0, base=0,
                                         pattern=[[-NCMP, 8]], channel_multiplier=1))
            step(nc.gpsimd.affine_select(out=vmask[:, :], in_=vmask[:, :], compare_op=ALU.is_ge, fill=0.0,
                                         base=NCMP - 1, pattern=[[NCMP, 8]], channel_multiplier=-1))
            step(nc.gpsimd.memset(dist_c[:, :, :], 1.0))
            nc.gpsimd.affine_select(out=dist_c[:, :, :], in_=dist_c[:, :, :], compare_op=ALU.is_ge, fill=0.0,
                                    base=-31, pattern=[[P, TT], [-16, NCMP]],
                                    channel_multiplier=1).then_inc(bias_ready, 1)

        nsa_steps = [(b, hkv, tt) for b in ("sel", "win") for hkv in range(HKV) for tt in range(TT)]
        nsa_steps += [("cmp", None, tt) for tt in range(TT)]
        diff_steps = [("diff", hp, tt) for hp in range(DIFF_H // 2) for tt in range(TT)]
        NS = len(nsa_steps)
        att_steps = nsa_steps + diff_steps
        NA = len(att_steps)
        pj = proj[:, 0:TT * NSA_IN].rearrange("p (t n) -> p t n", t=TT)
        vblk = pj[0:8 * NCMP, :, 1024:1536]
        pd = proj[:, :].rearrange("p (t n) -> p t n", t=TT)
        pf = proj[:, :].rearrange("p (k t) -> p k t", t=T)
        twice = xn.rearrange("p t (b h c d) -> p t b h c d", b=2, h=HKV, c=2)
        mapsA = []
        na = nd = 0
        for s in att_steps:
            mapsA.append((na, nd))
            na += 1
            nd += 1 if s[0] in ("sel", "win") and s[2] == 1 else 0

        def nk(step):
            return NCMP if step[0] == "cmp" else P * (step[2] + 1)

        @block.scalar
        def _(act):
            steps = Tally(act_step)

            def step(ins):
                act.wait_ge(act_step, steps.value(steps.add(ins)))

            act.dma_start(rowsC[:, :], a["c"].rearrange("b (k p) -> (b k) p", p=P)).then_inc(c_landed, 16)

            split_at = [0]

            def split_hi(w, it=0, n=CH):
                r = w_raw[w]
                act.wait_ge(raw_landed[r % RAW], landed_value(r, it))
                if w >= SPL:
                    act.wait_ge(chunk_used, it * 6 + (w - SPL + 1))
                nc.scalar.activation(whi[:, w % SPL, 0:n], raw[:, r % RAW, 0:n], ACT.Copy).then_inc(hi_ready, 1)

            def split_to(w):
                while split_at[0] <= min(w, NW - 1):
                    split_hi(split_at[0], n=size(items[w_raw[split_at[0]]]))
                    split_at[0] += 1

            def sumsq(n_x, n_ss):
                for tt in range(TT):
                    act.wait_ge(x_ready, 2 * n_x + tt + 1)
                    step(nc.scalar.activation(scratch[:, tt * D:(tt + 1) * D], x[:, tt, :], ACT.Square,
                                              accum_out=stat[:, tt:tt + 1]))
                    act.sem_inc(ss_ready, 1)

            def to_features(f, dst, scale=None, shift=None):
                for kt in range(KD):
                    if kt % 2 == 0:
                        act.wait_ge(turned, 4 * f + kt // 2 + 1)
                    src = acc[:, kt // 2, (kt % 2) * T:(kt % 2) * T + T]
                    if shift is not None:
                        nc.scalar.activation(h1[:, kt, :], src, ACT.Identity, bias=shift(kt), scale=scale(kt))\
                          .then_inc(feat_hi, 1)
                    elif scale is not None:
                        nc.scalar.activation(dst[:, kt, :], src, ACT.Copy, scale=scale(kt)).then_inc(feat_hi, 1)
                    else:
                        nc.scalar.activation(dst[:, kt, :], src, ACT.Copy).then_inc(feat_hi, 1)

            def ffn(q):
                w0 = w_at[("fin", q, 0, 0)]

                def silu_pair(j, it=0):
                    act.wait_ge(chunk_used, it * 6 + (w0 + pair_at(j) + 1))
                    act.wait_ge(gated, it * 2 + (NPAIR * q + j))
                    nc.scalar.activation(silu_a[:, j % 2, :], acc[:, (2 * j) % 4, :], ACT.Silu).then_inc(silu_ready, 1)

                for j in range(2):
                    split_to(w0 + pair_at(j) + LEAD)
                    silu_pair(j)
                split_to(w0 + 4 + LEAD)
                with act.Fori(0, 4) as it:
                    for c in range(6):
                        split_hi(w0 + 5 + c + LEAD, it)
                        if c % 3 == 0:
                            silu_pair(2 + c // 3, it)
                split_at[0] = w0 + 29 + LEAD
                split_to(w0 + 29 + LEAD)
                silu_pair(10)
                split_to(w0 + 32 + LEAD)

            def evict(n, w, dst, func=ACT.Copy, width=None):
                act.wait_ge(chunk_used, w + 1)
                src = acc[:, n % 4, :]
                if width is not None:
                    src = src.rearrange("p (t n) -> p t n", t=TT)[:, :, 0:width]
                nc.scalar.activation(dst, src, func).then_inc(proj_ready, 1)

            act.wait_ge(c_ps, 1)
            nc.scalar.activation(cact[:, :], acc[:, 7, 0:KD], ACT.Silu).then_inc(cact_ready, 1)
            nc.scalar.activation(lam_s[:, 7:8], acc[:, 7, 0:1], ACT.Copy).then_inc(silu_ready, 1)
            for l in range(2):
                if l == 0:
                    act.wait_ge(x_landed, 16)
                    for tt in range(TT):
                        step(nc.scalar.activation(scratch[:, tt * D:(tt + 1) * D], x[:, tt, :], ACT.Square,
                                                  accum_out=stat[:, tt:tt + 1]))
                        act.sem_inc(ss_ready, 1)
                else:
                    sumsq(1 - 1, None)
                split_to(w_at[("in1", l, IN1_ORDER[0])] + LEAD - 1)
                act.wait_ge(diag_ready, 1 if l == 0 else 4)
                to_features(l, hT_hi, scale=lambda kt: gain1[:, l, kt:kt + 1], shift=lambda kt: shift1[:, l, kt:kt + 1])
                for n, c in enumerate(IN1_ORDER):
                    w = w_at[("in1", l, c)]
                    split_to(w + LEAD)
                    func = ACT.Silu if c in (6, 7, 10, 11) else ACT.Copy
                    evict(n, w, proj[:, c * 512:(c + 1) * 512], func)
                act.wait_ge(gate_ps, l + 1)
                nc.scalar.activation(gate_row[:, :], acc[:, 4:6, :].rearrange("p b n -> p (b n)"), ACT.Copy)\
                  .then_inc(gate_sb, 1)
                for c in OUT1_ORDER:
                    split_to(w_at[("out1", l, c)] + LEAD)
                for tt in range(TT):
                    bank_complete(act, l, 2 * tt + 1)
                    step(nc.scalar.activation(scratch[:, tt * D:(tt + 1) * D],
                                              acc[:, 4 + 2 * tt:6 + 2 * tt, :].rearrange("p b n -> p (b n)"),
                                              ACT.Square, accum_out=stat[:, 2 + tt:3 + tt]))
                    act.sem_inc(ss_ready, 1)
            ffn_x = {0: 1, 1: 3, 2: 4, 3: 6}
            gain_of = {0: A_F1, 1: A_F2, 2: A_F1 + KD, 3: A_F2 + KD}

            def ffn_all(q):
                sumsq(ffn_x[q], None)
                g0 = gain_of[q]
                to_features(CONV_FFN[q], hT_hi, scale=lambda kt: colA[:, g0 + kt:g0 + kt + 1])
                ffn(q)

            def turn_out(n, dst, gain, who):
                for b in range(n):
                    yield b

            def attention(first, last):
                for i in range(first, last + 1):
                    if i < last:
                        s = att_steps[i]
                        act.wait_ge(scored, i + 1)
                        b = i % 2
                        if s[0] == "cmp":
                            nc.scalar.activation(sc[:, b, 0:HQ * NCMP], sc[:, b, 0:HQ * NCMP], ACT.Exp)\
                              .then_inc(probs, 1)
                        else:
                            for m in range(4):
                                v = sc[:, b, m * nk(s):(m + 1) * nk(s)]
                                ins = nc.scalar.activation(v, v, ACT.Exp, bias=nmax[:, b, m:m + 1],
                                                           accum_out=psums[:, i % 4, m:m + 1])
                            ins.then_inc(probs, 1)
                    if i > first:
                        j = i - 1
                        s = att_steps[j]
                        act.wait_ge(probs_turned, j + 1)
                        if j >= first + 2:
                            act.wait_ge(pv_ps, j - 1)
                        if s[0] == "cmp":
                            nc.scalar.activation(pT[0:8 * NCMP, j % 2, 0:T], acc[0:8 * NCMP, 4, 0:T], ACT.Copy)\
                              .then_inc(pT_act, 1)
                        else:
                            n = 4 * P if s[0] != "diff" else 2 * nk(s)
                            nc.scalar.activation(pT[:, j % 2, 0:n], acc[:, 4, 0:n], ACT.Copy).then_inc(pT_act, 1)

            ffn_all(0)
            sumsq(2, None)
            to_features(CONV_NSA, hT_hi, scale=lambda kt: colA[:, A_MIX + kt:A_MIX + kt + 1])
            for n, c in enumerate(NSA_ORDER):
                w = w_at[("nsa", c)]
                split_to(w + LEAD)
                if c in (4, 5):
                    act.wait_ge(chunk_used, w + 1)
                    for tt in range(TT):
                        ins = nc.scalar.activation(
                            twice[:, tt, c - 4], acc[:, n % 4, tt * T:(tt + 1) * T].rearrange("p (h d) -> p h d", d=DH)
                            .unsqueeze(2).to_broadcast([P, HKV, 2, DH]), ACT.Copy)
                    ins.then_inc(proj_ready, 1)
                else:
                    wd = NGATE if c == 10 else CC
                    evict(n, w, pj[:, :, c * CC:c * CC + wd], width=wd)
                if n == 4:
                    for kv in range(2):
                        for hb in range(2):
                            act.wait_ge(kc_ps, 2 * kv + hb + 1)
                            nc.scalar.activation(
                                kcT[0:DH, kv, 2 * hb:2 * hb + 2, :],
                                acc[0:DH, 4 + 2 * kv + hb, :].rearrange("p (h t) -> p h t", h=2),
                                ACT.Copy).then_inc(kc_act, 1)
            nc_proj = 24 + 11
            split_to(w_at[("cmp", 0, 0)] + LEAD)
            act.wait_ge(proj_ready, nc_proj)
            nc.scalar.activation(gates[:, :, :], pj[:, :, NSA_IN - NGATE:NSA_IN], ACT.Exp, scale=-1.0)\
              .then_inc(gexp_ready, 1)
            act.wait_ge(cmpr_ready, 2)
            for tt in range(TT):
                if tt:
                    act.wait_ge(sq_free, 1)
                nc.scalar.activation(scratch[:, 0:D], pj[:, tt, 0:D], ACT.Square).then_inc(qsq_ready, 1)
                ksw = pj[:, tt, 1536:2560].rearrange("p (b n) -> p b n", b=2)[:, :, 0:256]
                nc.scalar.activation(scratch[:, D:D + 512].rearrange("p (b n) -> p b n", b=2), ksw,
                                     ACT.Square).then_inc(qsq_ready, 1)
            for kv in range(2):
                for half in range(2):
                    split_to(w_at[("cmp", kv, half)] + LEAD)
            for kv in range(2):
                act.wait_ge(chunk_used, w_at[("cmp", kv, 1)] + 1)
                nc.scalar.activation(cmp_gt[:, kv, :], acc[0:HKV * NCMP, 4 + kv, 0:CMP_HIDDEN],
                                     ACT.Gelu_apprx_tanh).then_inc(gelu_ready, 1)

            def evict_heads(rnd, b):
                act.wait_ge(qk_turned, 4 * rnd + b + 1)
                dst = (qT if rnd == 0 else kT)[:, 2 * b:2 * b + 2, :]
                gcol = gq[:, 0:1] if rnd == 0 else colB[:, B_NK + 1 + b // 2:B_NK + 2 + b // 2]
                nc.scalar.activation(dst, acc[:, b, :].rearrange("p (h t) -> p h t", h=2), ACT.Copy,
                                     scale=gcol).then_inc(qk_act, 1)

            evict_heads(0, 0)
            evict_heads(0, 2)
            act.wait_ge(g_turned, 1)
            nc.scalar.activation(cmp_g.rearrange("p k c n -> p (k c n)"), acc[:, 6, 0:4 * HKV * NCMP], ACT.Copy)\
              .then_inc(g_sb, 1)
            evict_heads(1, 0)
            act.wait_ge(cmpk_ps, 1)
            step(nc.scalar.activation(otmp[0:HKV * NCMP, 0:DH], acc[0:HKV * NCMP, 4, 0:DH], ACT.Square,
                                      accum_out=stat[0:HKV * NCMP, 4:5]))
            act.sem_inc(cmpk_sq, 1)
            act.wait_ge(cmpv_ps, 1)
            nc.scalar.activation(v60, acc[0:HKV * NCMP, 5, 0:DH], ACT.Copy).then_inc(cmp_sb, 1)
            evict_heads(1, 2)
            act.wait_ge(kcn_ps, 1)
            act.wait_ge(bias_ready, 1)
            for e in range(2):
                half = slice(e * DH, (e + 1) * DH)
                nc.scalar.activation(kblk[half, :, e * NCMP:(e + 1) * NCMP],
                                     acc[half, 4, P:P + HKV * NCMP].rearrange("p (h n) -> p h n", h=HKV), ACT.Copy,
                                     scale=colB[half, B_NK:B_NK + 1]).then_inc(cmp_sb, 1)
            attention(0, NS)
            to_features(CONV_NSA_O, sT_hi)
            for c in range(4):
                split_to(w_at[("nsao", c)] + LEAD)
            ffn_all(1)
            ffn_all(2)
            sumsq(5, None)
            to_features(CONV_DIFF, hT_hi, scale=lambda kt: colA[:, A_MIX + KD + kt:A_MIX + KD + kt + 1])
            for n in range(12):
                w = w_at[("diff", n)]
                split_to(w + LEAD)
                evict(n, w, pd[:, :, n * CC:(n + 1) * CC], width=CC)
            act.wait_ge(proj_ready, 35 + 8)
            nq = 4
            for tt in range(TT):
                if tt:
                    act.wait_ge(sq_free, 2 + tt)
                nc.scalar.activation(scratch[:, 0:2 * D], pd[:, tt, 0:2 * D], ACT.Square).then_inc(qsq_ready, 1)
            for b in (0, 2, 4, 6):
                act.wait_ge(qk_turned, 8 + b + 1)
                dst = (qT if b < 4 else kT)[:, 2 * (b % 4):2 * (b % 4) + 2, :]
                gcol = gq[:, 1:2] if b < 4 else colB[:, B_DK:B_DK + 1]
                nc.scalar.activation(dst, acc[:, b, :].rearrange("p (h t) -> p h t", h=2), ACT.Copy,
                                     scale=gcol).then_inc(qk_act, 1)
            act.wait_ge(gexp_ready, 2)
            nc.scalar.activation(lam_s[:, 2:4], lam_s[:, 0:2], ACT.Exp).then_inc(gexp_ready, 1)
            attention(NS, NA)
            for tt in range(TT):
                act.wait_ge(combined, NA)
                nc.scalar.activation(scratch[:, tt * D:(tt + 1) * D], xn[:, tt, :], ACT.Square).then_inc(osq_ready, 1)
            to_features(CONV_DIFF_O, sT_hi, scale=lambda kt: gsub[:, 0:1])
            for c in range(4):
                split_to(w_at[("diffo", c)] + LEAD)
            ffn_all(3)

        @block.vector
        def _(dve):
            steps = Tally(dve_step)

            def step(ins):
                dve.wait_ge(dve_step, steps.value(steps.add(ins)))

            raw_at = [0]

            def split_lo(r, n, w, it=0):
                dve.wait_ge(hi_ready, it * 6 + (w + 1))
                nc.vector.tensor_tensor(wlo[:, w % SPL, 0:n], raw[:, r % RAW, 0:n], whi_f[:, w % SPL, 0:n],
                                        ALU.subtract).then_inc(raw_done, 1)

            def accumulate_ada(r, l, c):
                dve.wait_ge(raw_landed[r % RAW], landed_value(r))
                if l == 1 and c == 8:
                    dve.wait_ge(mod_ps, 2)
                dst = acc_ada[:, c * CC:(c + 1) * CC]
                v = raw[:, r % RAW, :].rearrange("p (k n) -> p k n", k=8)
                n0 = steps.n
                for k in range(8):
                    to = dst if k % 2 == 0 else ada2[:, :]
                    if k < 2:
                        ins = nc.vector.tensor_scalar(to, v[:, k, :], cact[:, k:k + 1], None, ALU.mult)
                    else:
                        dve.wait_ge(dve_step, n0 + k - 1)
                        ins = nc.vector.scalar_tensor_tensor(out=to, in0=v[:, k, :], scalar=cact[:, k:k + 1], in1=to,
                                                             op0=ALU.mult, op1=ALU.add)
                    steps.add(ins)
                dve.wait_ge(dve_step, steps.n)
                nc.vector.tensor_tensor(dst, dst, ada2[:, :], ALU.add).then_inc(raw_done, 1)
                dve.wait_ge(raw_done, r + 1)
                if (l, c) != (0, 7) and c in (7, 11):
                    dve.sem_inc(ada_ready, 1)

            def stream_to(w):
                end = w_raw[min(w, NW - 1)] + 1
                while raw_at[0] < end:
                    r = raw_at[0]
                    if items[r][0] == "ada":
                        accumulate_ada(r, items[r][1], items[r][2])
                    else:
                        split_lo(r, size(items[r]), w_raw.index(r))
                    raw_at[0] += 1

            def rsqrt(dst, src, n, inv_n, parts=P):
                m, u, v, h = (t[0:parts, 0:n] for t in (nt0, nt1, nt2, nt3))
                step(nc.vector.tensor_scalar(m, src, inv_n, EPS, ALU.mult, ALU.add))
                step(nc.vector.tensor_scalar(h, m, -0.5, None, ALU.mult))
                step(nc.vector.tensor_scalar(u.bitcast(I32), m.bitcast(I32), 1, None, ALU.logical_shift_right))
                step(nc.vector.tensor_scalar(v.bitcast(I32), u.bitcast(I32), -1.0, float(0x5F3759DF), ALU.mult,
                                             ALU.add))
                for i in range(3):
                    if n == 1:
                        step(nc.vector.scalar_tensor_tensor(out=u, in0=v, scalar=h, in1=v, op0=ALU.mult, op1=ALU.mult))
                    else:
                        step(nc.vector.tensor_tensor(u, v, v, ALU.mult))
                        step(nc.vector.tensor_tensor(u, u, h, ALU.mult))
                    step(nc.vector.scalar_tensor_tensor(out=dst if i == 2 else v, in0=u, scalar=1.5, in1=v,
                                                        op0=ALU.add, op1=ALU.mult))

            def normalise(n_ss, tiles=range(TT)):
                for tt in tiles:
                    dve.wait_ge(ss_ready, n_ss + tt + 1)
                    rsqrt(rs[:, tt:tt + 1], stat[:, tt:tt + 1], 1, 1.0 / D)
                    nc.vector.tensor_scalar(xn[:, tt, :], x[:, tt, :], rs[:, tt:tt + 1], None, ALU.mult)\
                      .then_inc(xn_ready, 1)

            def to_features(f, dst_hi, dst_lo, scale=None):
                for kt in range(KD):
                    if kt % 2 == 0:
                        dve.wait_ge(feat_hi, 8 * f + kt + 2)
                    src = acc[:, kt // 2, (kt % 2) * T:(kt % 2) * T + T]
                    if scale is not None:
                        nc.vector.scalar_tensor_tensor(out=dst_lo[:, kt, :], in0=src, scalar=scale(kt),
                                                       in1=dst_hi[:, kt, :], op0=ALU.mult, op1=ALU.subtract)\
                          .then_inc(feat_ready, 1)
                    else:
                        nc.vector.tensor_tensor(dst_lo[:, kt, :], src, dst_hi[:, kt, :], ALU.subtract)\
                          .then_inc(feat_ready, 1)

            def residual(o, factor):
                for tt in range(TT):
                    for nh in range(2):
                        bank_complete(dve, o, 2 * tt + nh)
                        xv = x[:, tt, nh * 512:(nh + 1) * 512]
                        ins = nc.vector.scalar_tensor_tensor(out=xv, in0=acc[:, 4 + 2 * tt + nh, :], scalar=factor,
                                                             in1=xv, op0=ALU.mult, op1=ALU.add)
                        if nh == 0:
                            step(ins)
                    ins.then_inc(x_ready, 1)
                dve.wait_ge(x_ready, 2 * (o + 1))

            def ffn(q):
                w0, r0 = w_at[("fin", q, 0, 0)], w_raw[w_at[("fin", q, 0, 0)]]

                def gate_pair(j, it=0):
                    dve.wait_ge(silu_ready, it * 2 + (NPAIR * q + j + 2))
                    dve.wait_ge(chunk_used, it * 6 + (w0 + pair_at(j) + 2))
                    dve.wait_ge(s_ready, it * 2 + (8 + NPAIR * q + j))
                    nc.vector.tensor_tensor(sact[:, :], silu_a[:, j % 2, :], acc[:, (2 * j + 1) % 4, :],
                                            ALU.mult).then_inc(gated, 1)
                    dve.wait_ge(gated, it * 2 + (NPAIR * q + j + 2))
                    at = slice(2 * (j % 2), 2 * (j % 2) + 2)
                    sv = sact.rearrange("p (k t) -> p k t", t=T)
                    step(nc.vector.tensor_copy(sT_hi[:, at, :], sv))
                    nc.vector.tensor_tensor(sT_lo[:, at, :], sv, sT_hi_f[:, at, :], ALU.subtract).then_inc(s_ready, 1)

                for j in range(2):
                    stream_to(w0 + pair_at(j) + 1 + LEAD)
                    gate_pair(j)
                stream_to(w0 + 4 + LEAD)
                n0 = steps.n
                with dve.Fori(0, 4) as it:
                    steps.it, steps.per = it, 2
                    for c in range(6):
                        split_lo(r0 + 5 + c + LEAD, CH, w0 + 5 + c + LEAD, it)
                        if c % 3 == 1:
                            gate_pair(2 + c // 3, it)
                    steps.it = None
                steps.n = n0 + 8
                raw_at[0] = r0 + 29 + LEAD
                stream_to(w0 + 30 + LEAD)
                gate_pair(10)
                stream_to(w0 + 32 + LEAD)

            def ada_chunks(n):
                for _ in range(n):
                    accumulate_ada(raw_at[0], 0, items[raw_at[0]][2])
                    raw_at[0] += 1

            dve.wait_ge(cact_ready, 1)
            ada_chunks(3)
            dve.wait_ge(cols_ready, 1)
            step(nc.vector.tensor_copy(colA[:, :], acc[:, 0, 0:A_N]))
            step(nc.vector.tensor_copy(colB[:, :], acc[:, 1, 0:B_N]))
            dve.sem_inc(colsd_ready, 1)
            nc.vector.memset(otmp[:, 0:1], 0.0).then_inc(gated, 1)

            def modulation(l, part):
                dve.wait_ge(mod_ps, 2 * l + part + 1)
                if part == 0:
                    step(nc.vector.tensor_tensor(mod[:, 0:16], acc[:, 6 if l == 0 else 0, 0:16], colB[:, 24 * l:24 * l + 16], ALU.add))
                    step(nc.vector.tensor_copy(shift1[:, l, :], mod[:, 0:8]))
                    step(nc.vector.scalar_tensor_tensor(out=gain1[:, l, :], in0=mod[:, 8:16], scalar=1.0,
                                                        in1=colA[:, A_GPRE + 8 * l:A_GPRE + 8 * l + 8], op0=ALU.add,
                                                        op1=ALU.mult))
                    dve.sem_inc(diag_ready, 1)
                else:
                    step(nc.vector.tensor_tensor(mod[:, 16:24], acc[:, 6, 16:24],
                                                 colB[:, 24 * l + 16:24 * l + 24], ALU.add))
                    step(nc.vector.tensor_tensor(gate_col[:, :], mod[:, 16:24],
                                                 colA[:, A_GPOST + 8 * l:A_GPOST + 8 * l + 8], ALU.mult))
                    for kt in range(KD):
                        ins = nc.vector.tensor_scalar(diag[:, kt * P:(kt + 1) * P], ident[:, :],
                                                      gate_col[:, kt:kt + 1], None, ALU.mult)
                        step(ins)
                    dve.sem_inc(diag_ready, 2)

            def pooling(l):
                p0 = pf[:, 16:20, :]
                src, dst = p0, pool_a
                for g, d in enumerate((1, 2, 4, 8)):
                    step(nc.vector.tensor_copy(dst[:, g:4, 0:d], src[:, g:4, 0:d]))
                    step(nc.vector.tensor_tensor(dst[:, g:4, d:T], src[:, g:4, d:T], src[:, g:4, 0:T - d], ALU.add))
                    src, dst = dst, (pool_b if dst is pool_a else pool_a)
                for g, w in enumerate(WINDOWS):
                    sv = (pool_a if g % 2 == 0 else pool_b)[:, g, :]
                    step(nc.vector.tensor_tensor(sv[:, 0:16], sv[:, 0:16], count_fix[:, g, :], ALU.mult))
                    step(nc.vector.scalar_tensor_tensor(out=pool_b[:, g, :], in0=sv, scalar=1.0 / w, in1=p0[:, g, :],
                                                        op0=ALU.mult, op1=ALU.subtract))
                dve.sem_inc(pooled_ready, 1)

            def conv(l):
                step(nc.vector.tensor_tensor(z1[:, :, :], pf[:, 8:12, :], pf[:, 0:4, :], ALU.mult))
                tap = lambda j, i: colA[:, A_CONV + 12 * l + 4 * j + i:A_CONV + 12 * l + 4 * j + i + 1]
                for i in range(4):
                    step(nc.vector.tensor_scalar(v1[:, i, :], z1[:, i, :], tap(2, i), None, ALU.mult))
                    for j, d in ((1, 1), (0, 2)):
                        step(nc.vector.scalar_tensor_tensor(out=v1[:, i, d:T], in0=z1[:, i, 0:T - d],
                                                            scalar=tap(j, i), in1=v1[:, i, d:T], op0=ALU.mult,
                                                            op1=ALU.add))

            def y_split(k0, n):
                for k in range(k0, k0 + n, 2):
                    step(nc.vector.tensor_copy(sT_hi[:, k:k + 2, :], y1[:, k:k + 2, :]))
                    nc.vector.tensor_tensor(sT_lo[:, k:k + 2, :], y1[:, k:k + 2, :], sT_hi_f[:, k:k + 2, :],
                                            ALU.subtract).then_inc(s_ready, 1)

            n_ss = 0
            x_updates = 0
            n_proj = 0
            for l in range(2):
                if l == 0:
                    ada_chunks(1)
                    normalise(n_ss, [0])
                    ada_chunks(2)
                    normalise(n_ss, [1])
                    ada_chunks(2)
                    modulation(0, 0)
                    stream_to(LEAD - 1)
                else:
                    normalise(n_ss)
                n_ss += 2
                for kt in range(KD):
                    dve.wait_ge(feat_hi, 8 * l + kt + 1)
                    step(nc.vector.tensor_copy(hT_hi[:, kt, :], h1[:, kt, :]))
                    nc.vector.tensor_tensor(hT_lo[:, kt, :], h1[:, kt, :], hT_hi_f[:, kt, :], ALU.subtract)\
                      .then_inc(feat_ready, 1)
                for n, c in enumerate(IN1_ORDER):
                    stream_to(w_at[("in1", l, c)] + LEAD)
                    if n == 0 and l == 0:
                        dve.wait_ge(consts_ready, 1)
                        step(nc.vector.reciprocal(pos1[:, :], pos1[:, :]))
                        for g, w in enumerate(WINDOWS):
                            step(nc.vector.tensor_scalar(count_fix[:, g, :], pos1[:, :], float(w), 1.0, ALU.mult, ALU.max))
                        step(nc.vector.tensor_scalar(gq[:, 0:1], colB[:, B_NQ:B_NQ + 1], DH ** -0.5, None, ALU.mult))
                        step(nc.vector.tensor_scalar(gq[:, 1:2], colB[:, B_DQ:B_DQ + 1], DH ** -0.5, None, ALU.mult))
                        step(nc.vector.tensor_scalar(gsub[:, :], colB[:, B_SUB:B_SUB + 1], 1.0 - LAM_INIT, None, ALU.mult))
                        dve.wait_ge(wsmall_landed, 48)
                        lp = otmp[:, 0:2 * DH].rearrange("p (a d) -> p a d", a=2)
                        lv = lam.rearrange("p (a b) d -> p a b d", b=2)
                        step(nc.vector.tensor_tensor(lp, lv[:, :, 0, :], lv[:, :, 1, :], ALU.mult))
                        step(nc.vector.tensor_reduce(out=lam_s[:, 0:2], in_=lp, axis=AX.X, op=ALU.add))
                    if n == 2:
                        dve.wait_ge(proj_ready, n_proj + 2)
                        pooling(l)
                    if n == 6:
                        dve.wait_ge(proj_ready, n_proj + 6)
                        conv(l)
                    if n == 8:
                        dve.wait_ge(proj_ready, n_proj + 8)
                        dve.wait_ge(mixed_ps, l + 1)
                        for g in range(4):
                            step(nc.vector.scalar_tensor_tensor(
                                out=y1[:, 4 + g, :], in0=acc[:, 6 + g // 2, (g % 2) * T:(g % 2) * T + T],
                                scalar=colA[:, A_POOL + 4 * l + g:A_POOL + 4 * l + g + 1], in1=pf[:, 20 + g, :],
                                op0=ALU.mult, op1=ALU.mult))
                        y_split(4, 4)
                    if n == 9:
                        modulation(l, 1)
                    if n == 10:
                        dve.wait_ge(proj_ready, n_proj + 10)
                        step(nc.vector.tensor_tensor(v1[:, :, :], v1[:, :, :], pf[:, 12:16, :], ALU.mult))
                for hf in range(2):
                    dve.wait_ge(proj_ready, n_proj + 11 + hf)
                    step(nc.vector.tensor_tensor(y1[:, 2 * hf:2 * hf + 2, :], v1[:, 2 * hf:2 * hf + 2, :],
                                                 pf[:, 4 + 2 * hf:6 + 2 * hf, :], ALU.mult))
                    y_split(2 * hf, 2)
                n_proj += 12
                for c in OUT1_ORDER:
                    stream_to(w_at[("out1", l, c)] + LEAD)
                if l == 0:
                    modulation(1, 0)
                dve.wait_ge(gate_sb, l + 1)
                for tt in range(TT):
                    dve.wait_ge(ss_ready, n_ss + tt + 1)
                    rsqrt(rs[:, 2 + tt:3 + tt], stat[:, 2 + tt:3 + tt], 1, 1.0 / D)
                    step(nc.vector.scalar_tensor_tensor(
                        out=xn[:, tt, :], in0=acc[:, 4 + 2 * tt:6 + 2 * tt, :].rearrange("p b n -> p (b n)"),
                        scalar=rs[:, 2 + tt:3 + tt], in1=gate_row[:, :], op0=ALU.mult, op1=ALU.mult))
                    nc.vector.tensor_tensor(x[:, tt, :], x[:, tt, :], xn[:, tt, :], ALU.add).then_inc(x_ready, 1)
                n_ss += 2
                dve.wait_ge(x_ready, 2 * (l + 1))

            gain_of = {0: A_F1, 1: A_F2, 2: A_F1 + KD, 3: A_F2 + KD}

            def ffn_all(q, n_ss):
                normalise(n_ss)
                g0 = gain_of[q]
                to_features(CONV_FFN[q], hT_hi_f, hT_lo, scale=lambda kt: colA[:, g0 + kt:g0 + kt + 1])
                ffn(q)
                residual(OUT_FFN[q], 0.5)

            def attention(first, last):
                for i in range(first, last + 2):
                    if i < last:
                        s = att_steps[i]
                        b = i % 2
                        dve.wait_ge(qk_ps, i + 1)
                        if i >= first + 2:
                            dve.wait_ge(probs_turned, i - 1)
                        n = nk(s)
                        S = acc[:, 2 * b:2 * b + 2, :]
                        if s[0] == "cmp":
                            flat = sc[:, b, 0:HQ * n].rearrange("p (m n) -> p m n", m=HQ)
                            step(nc.vector.tensor_tensor(flat, S[:, 0, 0:HQ * n].rearrange("p (m n) -> p m n", m=HQ),
                                                         bias_c[:, s[2]], ALU.add))
                            step(nc.vector.tensor_reduce(out=nmax[:, b, :], in_=flat, axis=AX.X, op=ALU.max))
                            nc.vector.tensor_tensor(flat, flat, nmax[:, b, :].unsqueeze(2).to_broadcast([P, HQ, n]),
                                                    ALU.subtract).then_inc(scored, 1)
                        else:
                            off = P if s[2] == 0 else 0
                            scv = sc[:, b, 0:4 * n].rearrange("p (e h n) -> p e h n", e=2, h=2)
                            if s[0] == "diff":
                                bv = bias.rearrange("p (h e) s -> p h e s", e=2)[:, 2 * s[1]:2 * s[1] + 2, 1,
                                                                                off:off + n]
                                for e in range(2):
                                    ins = nc.vector.tensor_tensor(
                                        scv[:, e], S[:, e, :].rearrange("p (h s) -> p h s", h=2)[:, :, 0:n], bv,
                                        ALU.add)
                                    step(ins)
                            else:
                                bv = bias[:, 4 * s[1]:4 * s[1] + 4, off:off + n].rearrange(
                                    "p (h e) s -> p e h s", e=2)
                                step(nc.vector.tensor_tensor(
                                    scv, S.rearrange("p e (h s) -> p e h s", h=2)[:, :, :, 0:n], bv, ALU.add))
                            flat = sc[:, b, 0:4 * n].rearrange("p (m n) -> p m n", m=4)
                            nc.vector.tensor_reduce(out=nmax[:, b, 0:4], in_=flat, axis=AX.X, op=ALU.max,
                                                    negate=True).then_inc(scored, 1)
                    if first < i <= last:
                        j = i - 1
                        s = att_steps[j]
                        n = nk(s)
                        if s[0] == "cmp":
                            dve.wait_ge(probs, j + 1)
                            flat = sc[:, j % 2, 0:HQ * n].rearrange("p (m n) -> p m n", m=HQ)
                            step(nc.vector.tensor_reduce(out=psums[:, j % 4, :], in_=flat, axis=AX.X, op=ALU.add))
                            nc.vector.tensor_tensor(flat, flat,
                                                    dist_c[:, s[2], :].unsqueeze(1).to_broadcast([P, HQ, n]),
                                                    ALU.mult).then_inc(mixed, 1)
                        elif s[0] == "diff":
                            dve.wait_ge(probs, j + 1)
                            pv = sc[:, j % 2, 0:4 * n].rearrange("p (m n) -> p m n", m=4)
                            ps = psums[:, j % 4, :]
                            step(nc.vector.reciprocal(ps[:, 0:4], ps[:, 0:4]))
                            step(nc.vector.tensor_scalar(ps[:, 2:4], ps[:, 2:4], lam_s[:, 5:6], None, ALU.mult))
                            for h in range(2):
                                step(nc.vector.tensor_scalar(pv[:, 2 + h, :], pv[:, 2 + h, :], ps[:, 2 + h:3 + h],
                                                             None, ALU.mult))
                                ins = nc.vector.scalar_tensor_tensor(out=pv[:, h, :], in0=pv[:, h, :],
                                                                     scalar=ps[:, h:h + 1], in1=pv[:, 2 + h, :],
                                                                     op0=ALU.mult, op1=ALU.add)
                                if h == 0:
                                    step(ins)
                            ins.then_inc(mixed, 1)
                        if mapsA[j][1] != (mapsA[j + 1][1] if j + 1 < NA else nd):
                            dve.wait_ge(probs_turned, j + 1)
                            if j >= first + 2:
                                dve.wait_ge(pv_ps, j - 1)
                            nc.vector.tensor_copy(pT[:, j % 2, 512:1024], acc[:, 5, :]).then_inc(pT_dve, 1)
                    if i >= first + 2:
                        j = i - 2
                        s = att_steps[j]
                        dve.wait_ge(pv_ps, j + 1)
                        O = acc[:, 6 + j % 2, :]
                        if s[0] == "diff":
                            nc.vector.tensor_copy(xn[:, s[2], s[1] * 256:(s[1] + 1) * 256], O[:, 0:256])\
                              .then_inc(combined, 1)
                            continue
                        if s[0] == "cmp":
                            tt = s[2]
                            step(nc.vector.reciprocal(rw[:, :], psums[:, j % 4, :]))
                            step(nc.vector.tensor_tensor(
                                rw[:, :], rw[:, :], gates[:, tt, :].rearrange("p (h b) -> p h b", b=3)[:, :, 0],
                                ALU.mult))
                            for half in range(2):
                                tv = otmp.rearrange("p (m d) -> p m d", d=DH)
                                rb = rw[:, 8 * half:8 * half + 8].unsqueeze(2).to_broadcast([P, 8, DH])
                                ov = xn[:, tt, half * 512:(half + 1) * 512]
                                step(nc.vector.tensor_tensor(
                                    tv, acc[:, 6 + half, :].rearrange("p (m d) -> p m d", d=DH), rb, ALU.mult))
                                ins = nc.vector.tensor_tensor(ov, ov, otmp, ALU.add)
                                if half == 0:
                                    step(ins)
                            ins.then_inc(combined, 1)
                            dve.wait_ge(combined, j + 1)
                            continue
                        br = {"sel": 1, "win": 2}[s[0]]
                        tt, nh, h0 = s[2], 4, 4 * s[1]
                        ps = psums[:, j % 4, 0:nh]
                        gv = gates[:, tt, 3 * h0:3 * (h0 + nh)].rearrange("p (h e b) -> p e h b", e=2, b=3)[:, :, :, br]
                        step(nc.vector.reciprocal(rw[:, 0:nh], ps))
                        rv = rw[:, 0:nh].rearrange("p (e h) -> p e h", e=2)
                        step(nc.vector.tensor_tensor(rv, rv, gv, ALU.mult))
                        Ov = O[:, 0:nh * DH].rearrange("p (m d) -> p m d", d=DH)
                        tv = otmp[:, 0:nh * DH].rearrange("p (m d) -> p m d", d=DH)
                        ov = xn[:, tt, h0 * DH:(h0 + nh) * DH].rearrange("p (h e d) -> p e h d", e=2, d=DH)
                        rb = rw[:, 0:nh].unsqueeze(2).to_broadcast([P, nh, DH])
                        step(nc.vector.tensor_tensor(tv, Ov, rb, ALU.mult))
                        tv4 = otmp[:, 0:nh * DH].rearrange("p (e h d) -> p e h d", e=2, d=DH)
                        if s[0] == "sel":
                            nc.vector.tensor_copy(ov, tv4).then_inc(combined, 1)
                        else:
                            nc.vector.tensor_tensor(ov, ov, tv4, ALU.add).then_inc(combined, 1)
                        dve.wait_ge(combined, j + 1)

            ffn_all(0, n_ss)
            n_ss += 2
            normalise(n_ss)
            n_ss += 2
            to_features(CONV_NSA, hT_hi_f, hT_lo, scale=lambda kt: colA[:, A_MIX + kt:A_MIX + kt + 1])
            for n, c in enumerate(NSA_ORDER):
                stream_to(w_at[("nsa", c)] + LEAD)
                if n == 4:
                    for kv in range(2):
                        for hb in range(2):
                            dve.wait_ge(kc_ps, 2 * kv + hb + 1)
                            step(nc.vector.tensor_copy(
                                kcT[DH:P, kv, 2 * hb:2 * hb + 2, 0:T - 1],
                                acc[DH:P, 4 + 2 * kv + hb, :].rearrange("p (h t) -> p h t", h=2)[:, :, 1:T]))
                    dve.wait_ge(kc_act, 4)
                    for kv in range(2):
                        kv_v = kcT[:, kv].rearrange("p h (n m r) -> p m h n r", m=8, r=2)
                        for mh in range(2):
                            src = kv_v[:, :, :, mh:mh + NCMP, 0]
                            dst = cmpR[:, kv, 8 * mh:8 * mh + 8, :].rearrange("p m (h n) -> p m h n", h=HKV)
                            pos = colB[:, B_POS + 16 * kv + 8 * mh:B_POS + 16 * kv + 8 * mh + 8]
                            step(nc.vector.tensor_tensor(
                                dst, src, pos.unsqueeze(2).unsqueeze(3).to_broadcast([P, 8, HKV, NCMP]), ALU.add))
                        step(nc.vector.tensor_copy(cmp_hi[:, kv], cmpR[:, kv]))
                        nc.vector.tensor_tensor(cmp_lo[:, kv], cmpR[:, kv], cmp_hi_f[:, kv], ALU.subtract)\
                          .then_inc(cmpr_ready, 1)
            stream_to(w_at[("cmp", 0, 0)] + LEAD)
            dve.wait_ge(gexp_ready, 1)
            step(nc.vector.tensor_scalar(gates[:, :, :], gates[:, :, :], 1.0, None, ALU.add))
            step(nc.vector.reciprocal(gates[:, :, :], gates[:, :, :]))
            dve.sem_inc(gexp_ready, 1)
            for tt in range(TT):
                dve.wait_ge(qsq_ready, 2 * tt + 2)
                step(nc.vector.tensor_reduce(out=stat[:, 8 + 24 * tt:32 + 24 * tt],
                                             in_=scratch[:, 0:24 * DH].rearrange("p (g d) -> p g d", d=DH),
                                             axis=AX.X, op=ALU.add))
                dve.sem_inc(sq_free, 1)
            stream_to(w_at[("cmp", 0, 1)] + LEAD)
            rsqrt(rs[:, 8:56], stat[:, 8:56], 48, 1.0 / DH)
            for tt in range(TT):
                qv = pj[:, tt, 0:D].rearrange("p (h d) -> p h d", d=DH)
                rq = rs[:, 8 + 24 * tt:24 + 24 * tt].unsqueeze(2).to_broadcast([P, HQ, DH])
                nc.vector.tensor_tensor(qv, qv, rq, ALU.mult).then_inc(qn_ready, 1)
                for b in range(2):
                    kv_ = pj[:, tt, 1536 + 512 * b:1792 + 512 * b].rearrange("p (h d) -> p h d", d=DH)
                    rk = rs[:, 24 + 24 * tt + 4 * b:28 + 24 * tt + 4 * b]
                    shape = [P, HKV, 2, DH]
                    nc.vector.tensor_tensor(twice[:, tt, b], kv_.unsqueeze(2).to_broadcast(shape),
                                            rk.unsqueeze(2).unsqueeze(3).to_broadcast(shape),
                                            ALU.mult).then_inc(qn_ready, 1)
            stream_to(w_at[("cmp", 1, 0)] + LEAD)
            stream_to(w_at[("cmp", 1, 1)] + LEAD)

            def evict_heads(rnd, b):
                dve.wait_ge(qk_turned, 4 * rnd + b + 1)
                dst = (qT if rnd == 0 else kT)[:, 2 * b:2 * b + 2, :]
                gcol = gq[:, 0:1] if rnd == 0 else colB[:, B_NK + 1 + b // 2:B_NK + 2 + b // 2]
                nc.vector.tensor_scalar(dst, acc[:, b, :].rearrange("p (h t) -> p h t", h=2), gcol, None,
                                        ALU.mult).then_inc(qk_dve, 1)

            evict_heads(0, 1)
            evict_heads(0, 3)
            evict_heads(1, 1)
            dve.wait_ge(cmpk_sq, 1)
            nk_rows = HKV * NCMP
            rsqrt(rs[0:nk_rows, 4:5], stat[0:nk_rows, 4:5], 1, 1.0 / DH, parts=nk_rows)
            for c in range(2):
                ins = nc.vector.tensor_scalar(kcn[:, c, :], acc[0:nk_rows, 4, 0:DH], rs[0:nk_rows, 4:5], None, ALU.mult)
                ins.then_inc(kcn_ready, 1)
            evict_heads(1, 3)
            dve.wait_ge(vsel_ps, 1)
            dve.wait_ge(bias_ready, 1)
            for f in range(2):
                shape = [8 * NCMP, 8, DH]
                nc.vector.tensor_tensor(
                    vblk[:, f, :].rearrange("p (m d) -> p m d", d=DH),
                    acc[0:8 * NCMP, 7, f * DH:(f + 1) * DH].unsqueeze(1).to_broadcast(shape),
                    vmask[:, :].unsqueeze(2).to_broadcast(shape), ALU.mult).then_inc(vblk_ready, 1)
            dve.wait_ge(bias_ready, 1)
            attention(0, NS)
            for tt in range(TT):
                dve.sem_inc(xn_ready, 1)
            to_features(CONV_NSA_O, sT_hi_f, sT_lo)
            for c in range(4):
                stream_to(w_at[("nsao", c)] + LEAD)
            residual(OUT_NSA, 1.0)
            ffn_all(1, n_ss)
            n_ss += 2
            ffn_all(2, n_ss)
            n_ss += 2
            normalise(n_ss)
            n_ss += 2
            to_features(CONV_DIFF, hT_hi_f, hT_lo, scale=lambda kt: colA[:, A_MIX + KD + kt:A_MIX + KD + kt + 1])
            for n in range(12):
                stream_to(w_at[("diff", n)] + LEAD)
            for tt in range(TT):
                dve.wait_ge(qsq_ready, 4 + tt + 1)
                step(nc.vector.tensor_reduce(out=stat[:, 32 * tt:32 * tt + 32],
                                             in_=scratch[:, 0:2 * D].rearrange("p (g d) -> p g d", d=DH), axis=AX.X,
                                             op=ALU.add))
                dve.sem_inc(sq_free, 1)
            rsqrt(rs[:, 0:64], stat[:, 0:64], 64, 1.0 / DH)
            for tt in range(TT):
                qv = pd[:, tt, 0:2 * D].rearrange("p (h d) -> p h d", d=DH)
                rq = rs[:, 32 * tt:32 * tt + 32].unsqueeze(2).to_broadcast([P, 32, DH])
                nc.vector.tensor_tensor(qv, qv, rq, ALU.mult).then_inc(qn_ready, 1)
            for b in (1, 3, 5, 7):
                dve.wait_ge(qk_turned, 8 + b + 1)
                dst = (qT if b < 4 else kT)[:, 2 * (b % 4):2 * (b % 4) + 2, :]
                gcol = gq[:, 1:2] if b < 4 else colB[:, B_DK:B_DK + 1]
                nc.vector.tensor_scalar(dst, acc[:, b, :].rearrange("p (h t) -> p h t", h=2), gcol, None,
                                        ALU.mult).then_inc(qk_dve, 1)
            dve.wait_ge(gexp_ready, 3)
            step(nc.vector.tensor_tensor(lam_s[:, 4:5], lam_s[:, 3:4], lam_s[:, 2:3], ALU.subtract))
            step(nc.vector.tensor_scalar(lam_s[:, 5:6], lam_s[:, 4:5], LAM_INIT, None, ALU.subtract))
            attention(NS, NA)
            for tt in range(TT):
                dve.wait_ge(osq_ready, tt + 1)
                step(nc.vector.tensor_reduce(out=stat[:, 8 * tt:8 * tt + 8],
                                             in_=scratch[:, tt * D:(tt + 1) * D].rearrange("p (g d) -> p g d", d=P),
                                             axis=AX.X, op=ALU.add))
            rsqrt(rs[:, 0:16], stat[:, 0:16], 16, 1.0 / P)
            for tt in range(TT):
                ov = xn[:, tt, :].rearrange("p (h d) -> p h d", d=P)
                ro = rs[:, 8 * tt:8 * tt + 8].unsqueeze(2).to_broadcast([P, DIFF_H, P])
                nc.vector.tensor_tensor(ov, ov, ro, ALU.mult).then_inc(xn_ready, 1)
            to_features(CONV_DIFF_O, sT_hi_f, sT_lo, scale=lambda kt: gsub[:, 0:1])
            for c in range(4):
                stream_to(w_at[("diffo", c)] + LEAD)
            residual(OUT_DIFF, 1.0)
            ffn_all(3, n_ss)

        @block.tensor
        def _(pe):
            def turn(f):
                for tt in range(TT):
                    pe.wait_ge(xn_ready, 2 * f + tt + 1)
                    for kt in range(KD):
                        ins = nc.tensor.transpose(acc[:, kt // 2, (kt % 2) * T + tt * P:(kt % 2) * T + tt * P + P],
                                                  xn[:, tt, kt * P:(kt + 1) * P], ident[:, :])
                        if tt == 1 and kt % 2 == 1:
                            ins.then_inc(turned, 1)

            def chunk_ready(w, it=0):
                pe.wait_ge(raw_done, it * 6 + (w_raw[w] + 1))

            def cols_by_tokens(w, bank, it=0, first=None):
                s = w % SPL
                hi = whi[:, s, :].rearrange("p (k n) -> p k n", k=8)
                lo = wlo[:, s, :].rearrange("p (k n) -> p k n", k=8)
                for ft in range(2):
                    o = acc[:, bank, ft * T:(ft + 1) * T]
                    cs = slice(ft * P, (ft + 1) * P)
                    for kt in range(KD):
                        if first is not None and ft == 0 and kt % 2 == 0:
                            pe.wait_ge(feat_ready, 8 * first + kt + 2)
                        nc.tensor.matmul(o, hi[:, kt, cs], hT_hi[:, kt, :], start=kt == 0, stop=False)
                        nc.tensor.matmul(o, hi[:, kt, cs], hT_lo[:, kt, :], start=False, stop=False)
                        ins = nc.tensor.matmul(o, lo[:, kt, cs], hT_hi[:, kt, :], start=False, stop=kt == KD - 1)
                ins.then_inc(chunk_used, 1)

            def tokens_by_cols(w, bank, n=CC, first=None):
                s = w % SPL
                hi = whi[:, s, 0:8 * n].rearrange("p (k n) -> p k n", k=8)
                lo = wlo[:, s, 0:8 * n].rearrange("p (k n) -> p k n", k=8)
                for tt in range(TT):
                    o = acc[:, bank, tt * T:tt * T + n]
                    ts = slice(tt * P, (tt + 1) * P)
                    for kt in range(KD):
                        if first is not None and tt == 0 and kt % 2 == 0:
                            pe.wait_ge(feat_ready, 8 * first + kt + 2)
                        nc.tensor.matmul(o, hT_hi[:, kt, ts], hi[:, kt, :], start=kt == 0, stop=False)
                        nc.tensor.matmul(o, hT_hi[:, kt, ts], lo[:, kt, :], start=False, stop=False)
                        ins = nc.tensor.matmul(o, hT_lo[:, kt, ts], hi[:, kt, :], start=False, stop=kt == KD - 1)
                ins.then_inc(chunk_used, 1)

            def out_chunk(w, kts, start, stop):
                s = w % SPL
                hi = whi[:, s, :].rearrange("p (k n) -> p k n", k=2)
                lo = wlo[:, s, :].rearrange("p (k n) -> p k n", k=2)
                for tt in range(TT):
                    ts = slice(tt * P, (tt + 1) * P)
                    for nh in range(2):
                        o = acc[:, 4 + 2 * tt + nh, :]
                        ns = slice(nh * 512, (nh + 1) * 512)
                        for k in range(2):
                            sh, sl = sT_hi[:, kts[k], ts], sT_lo[:, kts[k], ts]
                            nc.tensor.matmul(o, sh, hi[:, k, ns], start=start and k == 0, stop=False)
                            nc.tensor.matmul(o, sh, lo[:, k, ns], start=False, stop=False)
                            ins = nc.tensor.matmul(o, sl, hi[:, k, ns], start=False, stop=stop and k == 1)
                        if stop and tt + nh < 2:
                            ins.then_inc(y_ps, 1)
                ins.then_inc(chunk_used, 1)

            pe.wait_ge(consts_ready, 2)
            pe.wait_ge(c_landed, 16)
            nc.tensor.transpose(acc[:, 7, 0:KD], rowsC[:, :], ident[0:KD, 0:KD]).then_inc(c_ps, 1)
            pe.wait_ge(params_landed, 16 * N_PARAMS)
            nc.tensor.transpose(acc[:, 0, 0:A_N], rowsA[0:A_N, :], ident[0:A_N, 0:A_N])
            nc.tensor.transpose(acc[:, 1, 0:B_N], rowsB[0:B_N, :], ident[0:B_N, 0:B_N]).then_inc(cols_ready, 1)

            def sum_modulation(l, part):
                pe.wait_ge(ada_ready, 2 * l + part)
                b = 0 if (l, part) == (1, 0) else 6
                for j in (range(0, 16) if part == 0 else range(16, 24)):
                    ins = nc.tensor.matmul(acc[:, b, j:j + 1], acc_ada[:, j * P:(j + 1) * P], ones[:, 0:1],
                                           start=True, stop=True)
                ins.then_inc(mod_ps, 1)

            for r in range(8):
                pe.wait_ge(raw_done, r + 1)
                for j in (2 * r, 2 * r + 1):
                    ins = nc.tensor.matmul(acc[:, 6, j:j + 1], acc_ada[:, j * P:(j + 1) * P], ones[:, 0:1],
                                           start=True, stop=True)
                if r == 5:
                    turn(0)
            ins.then_inc(mod_ps, 1)
            n_s = n_proj = 0
            for l in range(2):
                if l:
                    turn(l)
                for n, c in enumerate(IN1_ORDER):
                    w = w_at[("in1", l, c)]
                    chunk_ready(w)
                    if n >= 4:
                        pe.wait_ge(proj_ready, n_proj + n - 3)
                    cols_by_tokens(w, n % 4, first=l if n == 0 else None)
                    if n == 6:
                        pe.wait_ge(wsmall_landed, 48)
                        pe.wait_ge(pooled_ready, l + 1)
                        for g in range(4):
                            ins = nc.tensor.matmul(acc[:, 6 + g // 2, (g % 2) * T:(g % 2) * T + T], wpool[:, l, g, :],
                                                   pool_b[:, g, :], start=True, stop=True)
                        ins.then_inc(mixed_ps, 1)
                    if n == 8:
                        pe.wait_ge(s_ready, n_s + 2)
                        sum_modulation(l, 1)
                    if n == 10:
                        pe.wait_ge(diag_ready, 3 * (l + 1) if l == 0 else 6)
                        for nh in range(2):
                            ins = nc.tensor.matmul(acc[:, 4 + nh, :], ones[:, :], diag[:, nh * 512:(nh + 1) * 512],
                                                   start=True, stop=True)
                        ins.then_inc(gate_ps, 1)
                n_proj += 12
                pe.wait_ge(gate_sb, l + 1)
                for n, c in enumerate(OUT1_ORDER):
                    w = w_at[("out1", l, c)]
                    chunk_ready(w)
                    pe.wait_ge(s_ready, n_s + n + 1)
                    out_chunk(w, [2 * c, 2 * c + 1], n == 0, n == 3)
                    if l == 0 and n == 2:
                        sum_modulation(1, 0)
                n_s += 4

            def ffn(q, n_s):
                f = CONV_FFN[q]
                turn(f)
                w0 = w_at[("fin", q, 0, 0)]

                def in_chunk(j, half, it=0):
                    w = w0 + pair_at(j) + half
                    chunk_ready(w, it)
                    pe.wait_ge(gated if half else silu_ready, it * 2 + (NPAIR * q + j))
                    cols_by_tokens(w, (2 * j + half) % 4, first=f if j + half == 0 else None)

                def down(j, it=0):
                    w = w0 + 3 * j + 4 if j < NPAIR - 1 else w0 + 32
                    chunk_ready(w, it)
                    pe.wait_ge(s_ready, it * 2 + (n_s + j + 1))
                    out_chunk(w, [2 * (j % 2), 2 * (j % 2) + 1], j == 0, j == NPAIR - 1)

                for j in range(2):
                    in_chunk(j, 0)
                    in_chunk(j, 1)
                    if j:
                        down(0)
                with pe.Fori(0, 4) as it:
                    for j in (2, 3):
                        in_chunk(j, 0, it)
                        in_chunk(j, 1, it)
                        down(j - 1, it)
                in_chunk(10, 0)
                in_chunk(10, 1)
                down(9)
                down(10)

            def scores(i):
                s = att_steps[i]
                b = 2 * (i % 2)
                n = nk(s)
                if s[0] == "cmp":
                    if s[2] == 0:
                        pe.wait_ge(cmp_sb, 3)
                    for pair in range(HQ // 2):
                        ins = nc.tensor.matmul(acc[:, b, pair * 2 * n:(pair + 1) * 2 * n],
                                               qT[:, pair, s[2] * P:(s[2] + 1) * P], kblk[:, pair // 2, :],
                                               start=True, stop=True)
                    ins.then_inc(qk_ps, 1)
                    return
                for m in range(4):
                    if s[0] == "diff":
                        tt = s[2]
                        e, slot = m % 2, m // 2
                        h = 2 * s[1] + slot
                        q, k = qT[e * DH:(e + 1) * DH, h, tt * P:(tt + 1) * P], kT[e * DH:(e + 1) * DH, h, 0:n]
                        o = acc[:, b + e, slot * T:slot * T + n]
                    else:
                        tt, h = s[2], 4 * s[1] + m
                        e, slot = m % 2, m // 2
                        br = 0 if s[0] == "sel" else 4
                        q, k = qT[e * DH:(e + 1) * DH, h // 2, tt * P:(tt + 1) * P], \
                            kT[e * DH:(e + 1) * DH, br + s[1], 0:n]
                        o = acc[:, b + e, slot * T:slot * T + n]
                    ins = nc.tensor.matmul(o, q, k, start=True, stop=True)
                ins.then_inc(qk_ps, 1)

            def turn_probs(i):
                s = att_steps[i]
                b = i % 2
                n = nk(s)
                if s[0] == "cmp":
                    for f in range(2):
                        ins = nc.tensor.transpose(acc[0:8 * NCMP, 4, f * P:(f + 1) * P],
                                                  sc[:, b, 8 * f * n:8 * (f + 1) * n], ident[:, :])
                else:
                    blocks = s[2] + 1
                    for m in range(2 if s[0] == "diff" else 4):
                        for kt in range(blocks):
                            at = (m + 2 * kt if s[0] == "diff" else m + 4 * kt) * P
                            ins = nc.tensor.transpose(acc[:, 4 + at // 512, at % 512:at % 512 + P],
                                                      sc[:, b, m * n + kt * P:m * n + (kt + 1) * P], ident[:, :])
                ins.then_inc(probs_turned, 1)

            def values(i):
                s = att_steps[i]
                b = i % 2
                O = acc[:, 6 + i % 2, :]
                if s[0] == "cmp":
                    pe.wait_ge(vblk_ready, 2)
                    for f in range(2):
                        ins = nc.tensor.matmul(acc[:, 6 + f, :], pT[0:8 * NCMP, b, f * P:(f + 1) * P],
                                               vblk[:, f, :], start=True, stop=True)
                else:
                    blocks = s[2] + 1
                    diff = s[0] == "diff"
                    for m in range(2 if diff else 4):
                        for kt in range(blocks):
                            at = (m + 2 * kt if diff else m + 4 * kt) * P
                            if diff:
                                v = pd[:, kt, 2 * D + (2 * s[1] + m) * P:2 * D + (2 * s[1] + m + 1) * P]
                                o = O[:, m * P:(m + 1) * P]
                            else:
                                c0 = (1792 if s[0] == "sel" else 2304) + s[1] * DH
                                v = pj[:, kt, c0:c0 + DH]
                                o = O[:, m * DH:(m + 1) * DH]
                            ins = nc.tensor.matmul(o, pT[:, b, at:at + P], v, start=kt == 0, stop=kt == blocks - 1)
                ins.then_inc(pv_ps, 1)

            def attention(first, last):
                n_mixed = 0 if first == 0 else 2
                for i in range(first, last + 2):
                    if i < last:
                        if i >= first + 2:
                            pe.wait_ge(scored, i - 1)
                        scores(i)
                    if first < i <= last:
                        j = i - 1
                        s = att_steps[j]
                        pe.wait_ge(probs, j + 1)
                        if s[0] in ("cmp", "diff"):
                            n_mixed += 1
                            pe.wait_ge(mixed, n_mixed)
                        if j > first:
                            pe.wait_ge(pT_act, mapsA[j][0])
                            if mapsA[j][1]:
                                pe.wait_ge(pT_dve, mapsA[j][1])
                        turn_probs(j)
                    if i >= first + 2:
                        j = i - 2
                        pe.wait_ge(pT_act, mapsA[j][0] + 1)
                        n_dve = mapsA[j + 1][1] if j + 1 < NA else nd
                        if n_dve:
                            pe.wait_ge(pT_dve, n_dve)
                        if att_steps[j][0] == "cmp":
                            pe.wait_ge(combined, j)
                        elif j >= first + 2:
                            pe.wait_ge(combined, j - 1)
                        values(j)

            ffn(0, n_s)
            n_s += NPAIR
            turn(CONV_NSA)
            for n, c in enumerate(NSA_ORDER):
                w = w_at[("nsa", c)]
                chunk_ready(w)
                if n >= 4:
                    pe.wait_ge(proj_ready, n_proj + n - 3)
                tokens_by_cols(w, n % 4, NGATE if c == 10 else CC, first=CONV_NSA if n == 0 else None)
                if n == 3:
                    for kv in range(2):
                        pe.wait_ge(proj_ready, n_proj + kv + 1)
                        for h in range(HKV):
                            for tt in range(TT):
                                src = xn[:, tt, (4 * kv + h) * P:(4 * kv + h + 1) * P]
                                ins = nc.tensor.transpose(
                                    acc[:, 4 + 2 * kv + h // 2, (h % 2) * T + tt * P:(h % 2) * T + tt * P + P],
                                    src, ident[:, :])
                            if h % 2 == 1:
                                ins.then_inc(kc_ps, 1)
            n_proj += 11

            pe.wait_ge(cmpr_ready, 2)
            for kv in range(2):
                for half in range(2):
                    w = w_at[("cmp", kv, half)]
                    chunk_ready(w)
                    hi = whi[:, w % SPL, :].rearrange("p (k n) -> p k n", k=8)
                    lo = wlo[:, w % SPL, :].rearrange("p (k n) -> p k n", k=8)
                    o = acc[:, 4 + kv, 0:CMP_HIDDEN]
                    for k in range(8):
                        m = 8 * half + k
                        c0 = (CMP_TILES * kv + m) * HKV * NCMP
                        bh, bl = (v[:, c0:c0 + P] for v in cmp_flat)
                        nc.tensor.matmul(o, bh, hi[:, k, :], start=m == 0, stop=False)
                        nc.tensor.matmul(o, bh, lo[:, k, :], start=False, stop=False)
                        ins = nc.tensor.matmul(o, bl, hi[:, k, :], start=False, stop=m == 15)
                    ins.then_inc(chunk_used, 1)

            def turn_heads(src, bank, pair, tt):
                return nc.tensor.transpose(acc[:, bank, (pair % 2) * T + tt * P:(pair % 2) * T + tt * P + P], src,
                                           ident[:, :])

            pe.wait_ge(qn_ready, 6)
            pe.wait_ge(proj_ready, n_proj)
            for pair in range(8):
                for tt in range(TT):
                    ins = turn_heads(pj[:, tt, pair * P:(pair + 1) * P], pair // 2, pair, tt)
                if pair % 2 == 1:
                    ins.then_inc(qk_turned, 1)

            def turn_keys(b):
                for h in range(HKV):
                    k = 4 * b + h
                    if h % 2 == 0:
                        pe.wait_ge(qk_dve if (k // 2) % 2 else qk_act, k // 4 + 1)
                    for tt in range(TT):
                        ins = turn_heads(xn[:, tt, k * P:(k + 1) * P], k // 2, k, tt)
                    if h % 2 == 1:
                        ins.then_inc(qk_turned, 1)

            rows = HKV * NCMP
            pe.wait_ge(gelu_ready, 2)
            for kv in range(2):
                for ct in range(2):
                    ins = nc.tensor.transpose(acc[:, 6, (2 * kv + ct) * rows:(2 * kv + ct + 1) * rows],
                                              cmp_gt[:, kv, ct * P:(ct + 1) * P], ident[0:rows, 0:rows])
            ins.then_inc(g_turned, 1)
            turn_keys(0)
            pe.wait_ge(g_sb, 1)
            pe.wait_ge(wsmall_landed, 48)
            for kv, done in ((0, cmpk_ps), (1, cmpv_ps)):
                for ct in range(2):
                    ins = nc.tensor.matmul(acc[0:rows, 4 + kv, 0:DH], cmp_g[:, kv, ct, :], w2[:, kv, ct, :],
                                           start=ct == 0, stop=ct == 1)
                ins.then_inc(done, 1)
            turn_keys(1)
            pe.wait_ge(cmp_sb, 1)
            pe.wait_ge(bias_ready, 1)
            for f in range(2):
                ins = nc.tensor.matmul(acc[0:8 * NCMP, 7, f * DH:(f + 1) * DH], sel[:, f, :], v60, start=True,
                                       stop=True)
            ins.then_inc(vsel_ps, 1)
            pe.wait_ge(kcn_ready, 2)
            nc.tensor.transpose(acc[:, 4, P:P + rows], kcn.rearrange("p c d -> p (c d)"), ident[0:rows, 0:rows])\
              .then_inc(kcn_ps, 1)
            pe.wait_ge(qk_act, 4)
            pe.wait_ge(qk_dve, 4)
            attention(0, NS)
            turn(CONV_NSA_O)
            for n in range(4):
                w = w_at[("nsao", n)]
                chunk_ready(w)
                pe.wait_ge(feat_ready, 8 * CONV_NSA_O + 2 * n + 2)
                out_chunk(w, [2 * n, 2 * n + 1], n == 0, n == 3)
            ffn(1, n_s)
            n_s += NPAIR
            ffn(2, n_s)
            n_s += NPAIR
            turn(CONV_DIFF)
            for n in range(12):
                w = w_at[("diff", n)]
                chunk_ready(w)
                if n >= 4:
                    pe.wait_ge(proj_ready, n_proj + n - 3)
                tokens_by_cols(w, n % 4, first=CONV_DIFF if n == 0 else None)
            n_proj += 12
            pe.wait_ge(qn_ready, 8)
            pe.wait_ge(proj_ready, n_proj)
            for pair in range(16):
                for tt in range(TT):
                    ins = turn_heads(pd[:, tt, pair * P:(pair + 1) * P], pair // 2, pair, tt)
                if pair % 2 == 1:
                    ins.then_inc(qk_turned, 1)
            pe.wait_ge(qk_act, 8)
            pe.wait_ge(qk_dve, 8)
            attention(NS, NA)
            turn(CONV_DIFF_O)
            for n in range(4):
                w = w_at[("diffo", n)]
                chunk_ready(w)
                pe.wait_ge(feat_ready, 8 * CONV_DIFF_O + 2 * n + 2)
                out_chunk(w, [2 * n, 2 * n + 1], n == 0, n == 3)
            ffn(3, n_s)


N_PARAMS = 18


_USED = ["x", "c", "w_ada", "b_ada", "g_pre", "w_in", "w_conv", "w_pool", "pool_scale", "w_out", "g_post",
         "ffn1_norm_2", "ffn1_w_in_2", "ffn1_w_out_2", "mix_norm_2", "ffn2_norm_2", "ffn2_w_in_2", "ffn2_w_out_2",
         "nsa_w_in_2", "nsa_w_out_2", "nsa_q_norm_2", "nsa_k_norm_2", "nsa_cmp_pos_2", "nsa_cmp_w1_2",
         "nsa_cmp_w2_2", "diff_w_in_2", "diff_w_out_2", "diff_q_norm_2", "diff_k_norm_2", "diff_lambda_2",
         "diff_subln_2"]


def kernel(**inputs):
    import numpy as _np
    import concourse.bacc as _bacc
    from concourse import mybir as _mybir
    from concourse.bass_utils import run_bass_kernel_spmd as _run

    nc = _bacc.Bacc("TRN2", target_bir_lowering=False, num_devices=1)
    arrays, args = {}, {}
    for name in _USED:
        arr = _np.ascontiguousarray(inputs[name])
        arrays[f"in_{name}_dram"] = arr
        args[name] = nc.dram_tensor(f"in_{name}_dram", arr.shape, _mybir.dt.from_np(arr.dtype),
                                    kind="ExternalInput").ap()
    out = nc.dram_tensor("out_dram", (1, T, D), F32, kind="ExternalOutput").ap()
    two_blocks_kernel(nc, args, out)
    r = _run(nc, [arrays], core_ids=[0])
    return r.results[0]["out_dram"]
```

```python
import math
from contextlib import ExitStack

import concourse.bass as bass
from concourse import mybir
from concourse.alu_op_type import AluOpType as ALU

F32 = mybir.dt.float32
F32R = mybir.dt.float32r
I32 = mybir.dt.int32
ACT = mybir.ActivationFunctionType
AX = mybir.AxisListType

P = 128
T = 256
TT = T // P
D = 1024
KD = D // P
EPS = 1e-6
NEG = -1e30

CW = 512
IN1 = 6 * CW
WINDOWS = (2, 4, 8, 16)
DFF = 2816
NPAIR = DFF // 256
DH = 64
HQ = 16
HKV = 4
G = HQ // HKV
CMP_HIDDEN = 256
CMP_TILES = 32 * DH // P
NCMP = T // 16 - 1
NSA_IN = HQ * DH + 6 * HKV * DH + 3 * HQ
NGATE = 3 * HQ
DIFF_H = 8
LAM_INIT = 0.8 - 0.6 * math.exp(-0.3)

RAW = 3
SPL = 3
LEAD = SPL - 1
CH = 2048
CC = 256

A_GPRE, A_GPOST, A_F1, A_MIX, A_F2, A_POOL, A_CONV, A_N = 0, 16, 32, 48, 64, 80, 88, 112
B_BADA, B_POS, B_NQ, B_NK, B_DQ, B_DK, B_SUB, B_N = 0, 48, 80, 81, 84, 85, 86, 87

IN1_ORDER = [8, 9, 0, 1, 4, 5, 10, 11, 6, 7, 2, 3]
DIFF_BANKS = [4, 5, 6, 7, 0, 1, 2, 3]
SEED = 0x5F3759DF - 0x400000 - 2 ** 31
OUT1_ORDER = [2, 3, 0, 1]
NSA_ORDER = [4, 5, 0, 1, 2, 3, 6, 8, 7, 9, 10]

CONV_BLK = (0, 1)
CONV_FFN = {0: 2, 1: 5, 2: 6, 3: 9}
CONV_NSA, CONV_NSA_O, CONV_DIFF, CONV_DIFF_O = 3, 4, 7, 8
OUT_BLK, OUT_NSA, OUT_DIFF = (0, 1), 3, 6
OUT_FFN = {0: 2, 1: 4, 2: 5, 3: 7}


class Tally:

    def __init__(self, sem):
        self.sem, self.n, self.it, self.per = sem, 0, None, 0

    def add(self, ins):
        ins.then_inc(self.sem, 1)
        self.n += 1
        return self.n

    def value(self, n):
        return n if self.it is None else n + self.it * self.per


def stream_items():
    items = [("ada", 0, c) for c in range(8)]
    side = [("ada", 0, c) for c in range(8, 12)] + [("ada", 1, c) for c in range(8)]
    for c in IN1_ORDER:
        items.append(("w", "in1", 0, c))
        items.append(side.pop(0))
        if c == IN1_ORDER[8]:
            break
    items += [("w", "in1", 0, c) for c in IN1_ORDER[9:]]
    for c in OUT1_ORDER:
        items.append(("w", "out1", 0, c))
        if c != OUT1_ORDER[0]:
            items.append(side.pop(0))
    assert not side
    side = [("ada", 1, c) for c in range(8, 12)]
    for c in IN1_ORDER:
        items.append(("w", "in1", 1, c))
        if side:
            items.append(side.pop(0))
    items += [("w", "out1", 1, c) for c in OUT1_ORDER]

    def ffn(q):
        got = []
        for j in range(NPAIR):
            got += [("w", "fin", q, j, 0), ("w", "fin", q, j, 1)]
            if j:
                got.append(("w", "fout", q, j - 1))
        return got + [("w", "fout", q, NPAIR - 1)]

    items += ffn(0)
    items += [("w", "nsa", c) for c in NSA_ORDER]
    items += [("w", "cmp", kv, half) for kv in range(2) for half in range(2)]
    items += [("w", "nsao", c) for c in range(4)]
    items += ffn(1) + ffn(2)
    items += [("w", "diff", c) for c in range(12)]
    items += [("w", "diffo", c) for c in range(4)]
    items += ffn(3)
    return items


def two_blocks_kernel(nc, a, out):
    ctx = ExitStack()
    with ctx:
        def sb(name, shape, dt=F32):
            return ctx.enter_context(nc.sbuf_tensor(name, shape, dt))

        def sem(name):
            return ctx.enter_context(nc.semaphore(name))

        x = sb("x", [P, TT, D])
        xn = sb("xn", [P, TT, D])
        proj = sb("proj", [P, 2 * 3072])
        pf = proj[:, :].rearrange("p (k t) -> p k t", t=T)
        raw = sb("raw", [P, RAW, CH])
        whi = sb("whi", [P, SPL, CH], F32R)
        wlo = sb("wlo", [P, SPL, CH], F32R)
        hT_hi = sb("hT_hi", [P, KD, T], F32R)
        hT_lo = sb("hT_lo", [P, KD, T], F32R)
        sT_hi = sb("sT_hi", [P, KD, T], F32R)
        sT_lo = sb("sT_lo", [P, KD, T], F32R)
        bias = sb("bias", [P, HQ, T])
        wpool = bias[:, 0:4, :].rearrange("p (l g) n -> p l (g n)", l=2).rearrange("p l (g n) -> p l g n", g=4)
        gate_row = bias[:, 4:8, :].rearrange("p h n -> p (h n)")
        bias_c = sb("bias_c", [P, TT, HQ, NCMP])
        dist = sb("dist", [P, T])
        dist_c = sb("dist_c", [P, TT, NCMP])
        ident = sb("ident", [P, P])
        ones = sb("ones", [P, P])
        colA = sb("colA", [P, A_N])
        colB = sb("colB", [P, B_N])
        w2 = sb("w2", [P, 2, 2, DH])
        lam = sb("lam", [P, 4, DH])
        lam_s = sb("lam_s", [P, 8])
        count_fix = sb("count_fix", [P, 4, 16])
        pos1 = sb("pos1", [P, 16])
        cact = sb("cact", [P, KD])
        mod = sb("mod", [P, 24])
        gain1 = sb("gain1", [P, 2, KD])
        shift1 = sb("shift1", [P, 2, KD])
        gate_col = sb("gate_col", [P, KD])
        gq = sb("gq", [P, 2])
        gsub = sb("gsub", [P, 1])
        stat = sb("stat", [P, 64])
        rs = sb("rs", [P, 64])
        nt0 = sb("nt0", [P, 64])
        nt1 = sb("nt1", [P, 64])
        nt2 = sb("nt2", [P, 64])
        scratch = sb("scratch", [P, 2048])
        region = sb("region", [P, 7 * 1024])
        acc_ada = region[:, 0:3072]
        diag = xn[:, 0, :]
        rowsA = region[:, 5120:5120 + P]
        rowsB = region[:, 5120 + P:5120 + 2 * P]
        y1 = region[:, 3072:5120].rearrange("p (k t) -> p k t", t=T)
        pool_a = region[:, 5120:6144].rearrange("p (g t) -> p g t", t=T)
        pool_b = region[:, 6144:7168].rearrange("p (g t) -> p g t", t=T)
        z1 = pool_a
        v1 = scratch[:, 0:1024].rearrange("p (g t) -> p g t", t=T)
        v2 = scratch[:, 1024:2048].rearrange("p (g t) -> p g t", t=T)
        silu_a = region[:, 4096:5120].rearrange("p (b n) -> p b n", b=2)
        sact = region[:, 5120:5632]
        h1 = region[:, 5120:7168].rearrange("p (k t) -> p k t", t=T)
        qT = region[:, 0:2048].rearrange("p (h t) -> p h t", t=T)
        kT = region[:, 2048:4096].rearrange("p (h t) -> p h t", t=T)
        sc = region[:, 4096:7168].rearrange("p (b n) -> p b n", b=3)
        pT = scratch.rearrange("p (b n) -> p b n", b=2)
        kcT = region[:, 0:2048].rearrange("p (k h t) -> p k h t", k=2, h=HKV)
        cmpR = scratch[:, 0:1920].rearrange("p (k m n) -> p k m n", k=2, m=CMP_TILES)
        cmp_hi, cmp_lo = (v.rearrange("p k t -> p (k t)")[:, 0:1920]
                          .rearrange("p (k m n) -> p k m n", k=2, m=CMP_TILES) for v in (sT_hi, sT_lo))
        cmp_flat = [v.rearrange("p k t -> p (k t)") for v in (sT_hi, sT_lo)]
        cmp_g = region[:, 6656:6896].rearrange("p (k c n) -> p k c n", k=2, c=2)
        v60 = region[0:HKV * NCMP, 6896:6896 + DH]
        cmp_gt = region[0:HKV * NCMP, 4096:4608].rearrange("p (k n) -> p k n", k=2)
        cmp_small = sb("cmp_small", [P, 2 * DH + 2 * HKV * NCMP])
        kcn = cmp_small[0:HKV * NCMP, 0:2 * DH].rearrange("p (c d) -> p c d", c=2)
        kblk = cmp_small[:, 2 * DH:2 * DH + 2 * HKV * NCMP].rearrange("p (h m) -> p h m", h=HKV)
        sel = dist[0:HKV * NCMP, 0:240].rearrange("p (f m) -> p f m", f=2)
        vmask = sb("vmask", [8 * NCMP, 8])
        gates = sb("gates", [P, TT, NGATE])
        nmax = sb("nmax", [P, 3, HQ])
        psums = sb("psums", [P, 4, HQ])
        rw = sb("rw", [P, HQ])
        ada2 = sb("ada2", [P, CC])
        rowsC = cmp_small[0:KD, 0:P]
        otmp = region[:, 6144:6656]
        wtmp = proj[:, TT * NSA_IN:TT * NSA_IN + 512]

        whi_f, hT_hi_f, sT_hi_f, cmp_hi_f = (v.bitcast(F32) for v in (whi[:, :, :], hT_hi[:, :, :], sT_hi[:, :, :], cmp_hi))

        acc = ctx.enter_context(nc.psum_tensor("acc", [P, 8, 512], F32))

        raw_landed = [sem(f"raw_landed{i}") for i in range(RAW)]
        params_landed = sem("params_landed")
        x_landed = sem("x_landed")
        wsmall_landed = sem("wsmall_landed")
        out_stored = sem("out_stored")
        consts_ready = sem("consts_ready")
        pool_step = sem("pool_step")
        bias_ready = sem("bias_ready")
        hi_ready = sem("hi_ready")
        raw_done = sem("raw_done")
        chunk_used = sem("chunk_used")
        cols_ready = sem("cols_ready")
        colsd_ready = sem("colsd_ready")
        cact_ready = sem("cact_ready")
        ada_ready = sem("ada_ready")
        mod_ps = sem("mod_ps")
        diag_ready = sem("diag_ready")
        gate_ps = sem("gate_ps")
        gate_sb = sem("gate_sb")
        x_ready = sem("x_ready")
        ss_ready = sem("ss_ready")
        xn_ready = sem("xn_ready")
        turned = sem("turned")
        feat_hi = sem("feat_hi")
        feat_ready = sem("feat_ready")
        proj_ready = sem("proj_ready")
        pooled_ready = sem("pooled_ready")
        conv_ready = sem("conv_ready")
        mixed_ps = sem("mixed_ps")
        y_ps = sem("y_ps")
        silu_ready = sem("silu_ready")
        gated = sem("gated")
        s_ready = sem("s_ready")
        dve_step = sem("dve_step")
        act_step = sem("act_step")
        kc_ps = sem("kc_ps")
        kc_act = sem("kc_act")
        cmpr_ready = sem("cmpr_ready")
        g_turned = sem("g_turned")
        g_sb = sem("g_sb")
        vsel_ps = sem("vsel_ps")
        vblk_ready = sem("vblk_ready")
        c_landed = sem("c_landed")
        c_ps = sem("c_ps")
        gelu_ready = sem("gelu_ready")
        cmpk_ps = sem("cmpk_ps")
        cmpv_ps = sem("cmpv_ps")
        cmpk_sq = sem("cmpk_sq")
        kcn_ready = sem("kcn_ready")
        kcn_ps = sem("kcn_ps")
        cmp_sb = sem("cmp_sb")
        qsq_ready = sem("qsq_ready")
        sq_free = sem("sq_free")
        qn_ready = sem("qn_ready")
        qk_turned = sem("qk_turned")
        qk_act = sem("qk_act")
        qk_dve = sem("qk_dve")
        gexp_ready = sem("gexp_ready")
        qk_ps = sem("qk_ps")
        scored = sem("scored")
        probs = sem("probs")
        mixed = sem("mixed")
        probs_turned = sem("probs_turned")
        pT_act = sem("pT_act")
        pv_ps = sem("pv_ps")
        combined = sem("combined")
        osq_ready = sem("osq_ready")

        items = stream_items()
        w_raw = [r for r, it in enumerate(items) if it[0] == "w"]
        w_at = {items[r][1:]: w for w, r in enumerate(w_raw)}
        NW = len(w_raw)

        def col_chunk(ap, c0, n=CC):
            return ap.rearrange("(k p) n -> p k n", p=P)[:, :, c0:c0 + n]

        def row_chunk(ap, c):
            return ap.rearrange("(c k p) n -> p c k n", p=P, k=2)[:, c, :, :]

        ffn_in = [a["ffn1_w_in_2"][0], a["ffn2_w_in_2"][0], a["ffn1_w_in_2"][1], a["ffn2_w_in_2"][1]]
        ffn_out = [a["ffn1_w_out_2"][0], a["ffn2_w_out_2"][0], a["ffn1_w_out_2"][1], a["ffn2_w_out_2"][1]]

        def source(item):
            if item[0] == "ada":
                return col_chunk(a["w_ada"][item[1]], item[2] * CC)
            kind, *at = item[1:]
            if kind == "in1":
                return col_chunk(a["w_in"][at[0]], at[1] * CC)
            if kind == "out1":
                return row_chunk(a["w_out"][at[0]], at[1])
            if kind == "fin":
                return col_chunk(ffn_in[at[0]], at[2] * DFF + at[1] * CC)
            if kind == "fout":
                return row_chunk(ffn_out[at[0]], at[1])
            if kind == "nsa":
                return col_chunk(a["nsa_w_in_2"][0], at[0] * CC, NGATE if at[0] == 10 else CC)
            if kind == "cmp":
                return a["nsa_cmp_w1_2"][0, at[0]].rearrange("(k p) n -> p k n", p=P)[:, at[1] * 8:at[1] * 8 + 8, :]
            if kind == "nsao":
                return row_chunk(a["nsa_w_out_2"][0], at[0])
            if kind == "diff":
                return col_chunk(a["diff_w_in_2"][0], at[0] * CC)
            return row_chunk(a["diff_w_out_2"][0], at[0])

        def size(item):
            return 8 * NGATE if item[1:] == ("nsa", 10) else CH

        def raw_view(slot, ap):
            k, n = ap.shape[1], ap.shape[2]
            return raw[:, slot, 0:k * n].rearrange("p (k n) -> p k n", k=k)

        out_last = [w_at[k] for k in (("out1", 0, 1), ("out1", 1, 1), ("fout", 0, 10), ("nsao", 3), ("fout", 1, 10),
                                      ("fout", 2, 10), ("diffo", 3), ("fout", 3, 10))]

        def bank_complete(eng, o, k):
            if k < 3:
                eng.wait_ge(y_ps, 3 * o + k + 1)
            else:
                eng.wait_ge(chunk_used, out_last[o] + 1)

        def pair_at(j):
            return 3 * j - 1 if j else 0

        def landed_value(r, it=0):
            return it * (16 * 6 // RAW) + 16 * (r // RAW + 1)

        block = ctx.enter_context(nc.Block())

        @block.sync
        def _(sp):
            def load(r):
                if r >= RAW:
                    sp.wait_ge(raw_done, r - RAW + 1)
                src = source(items[r])
                sp.dma_start(raw_view(r % RAW, src), src).then_inc(raw_landed[r % RAW], 16)

            def ffn_loads(q, r0):
                w_in_v = ffn_in[q].rearrange("(k p) n -> p k n", p=P)
                w_out_v = ffn_out[q].rearrange("(c k p) n -> p c k n", p=P, k=2)
                for r in range(r0, r0 + 5):
                    load(r)
                with sp.Fori(0, 4) as it:
                    for c in range(6):
                        r, j = r0 + 5 + c, 2 + c // 3
                        sp.wait_ge(raw_done, it * 6 + (r - RAW + 1))
                        if c % 3 < 2:
                            src = w_in_v[:, :, bass.ds(it * (2 * CC) + ((c % 3) * DFF + j * CC), CC)]
                            dst = raw_view(r % RAW, w_in_v[:, :, 0:CC])
                        else:
                            src = w_out_v[:, bass.ds(it * 2 + (j - 1), 1)].rearrange("p c k n -> p (c k) n")
                            dst = raw_view(r % RAW, w_out_v[:, 0])
                        sp.dma_start(dst, src).then_inc(raw_landed[r % RAW], 16)
                for r in range(r0 + 29, r0 + 33):
                    load(r)

            r = 0
            while r < len(items):
                if items[r][1] == "fin":
                    ffn_loads(items[r][2], r)
                    r += 3 * NPAIR
                else:
                    if r == RAW:
                        sp.dma_start(x[:, :, :], a["x"][0].rearrange("(t p) n -> p t n", p=P)).then_inc(x_landed, 16)
                    load(r)
                    r += 1
            for tt in range(TT):
                sp.wait_ge(x_ready, 2 * 7 + tt + 1)
                sp.dma_start(out[0].rearrange("(t p) n -> p t n", p=P)[:, tt], x[:, tt, :]).then_inc(out_stored, 16)
            sp.wait_ge(out_stored, 16 * TT)

        @block.gpsimd
        def _(pool):
            steps = Tally(pool_step)

            def step(ins):
                pool.wait_ge(pool_step, steps.add(ins))

            step(nc.gpsimd.memset(ident[:, :], 0.0))
            step(nc.gpsimd.affine_select(out=ident[:, :], in_=ident[:, :], compare_op=ALU.not_equal, fill=1.0,
                                         base=0, pattern=[[-1, P]], channel_multiplier=1))
            nc.gpsimd.iota(pos1[:, :], pattern=[[1, 16]], base=1, channel_multiplier=0,
                           allow_small_or_imprecise_dtypes=True).then_inc(consts_ready, 1)
            nc.gpsimd.memset(ones[:, :], 1.0).then_inc(consts_ready, 1)
            for at, name in ((A_GPRE, "g_pre"), (A_GPOST, "g_post"), (A_F1, "ffn1_norm_2"), (A_MIX, "mix_norm_2"),
                             (A_F2, "ffn2_norm_2")):
                pool.dma_start(rowsA[at:at + 16, :], a[name].rearrange("l (k p) -> (l k) p", p=P))\
                    .then_inc(params_landed, 16)
            pool.dma_start(rowsA[A_POOL:A_CONV, :], a["pool_scale"].rearrange("l (k p) -> (l k) p", p=P))\
               .then_inc(params_landed, 16)
            pool.dma_start(rowsA[A_CONV:A_N, :], a["w_conv"].rearrange("l j (k p) -> (l j k) p", p=P))\
               .then_inc(params_landed, 16)
            pool.dma_start(rowsB[B_BADA:B_POS, :], a["b_ada"].rearrange("l (k p) -> (l k) p", p=P))\
               .then_inc(params_landed, 16)
            pool.dma_start(rowsB[B_POS:B_NQ, :], a["nsa_cmp_pos_2"][0].rearrange("v (m j) d -> (v m) (j d)", j=2))\
               .then_inc(params_landed, 16)
            n_params = 9
            for c in range(2):
                for at, name, n in ((B_NQ, "nsa_q_norm_2", 1), (B_NK, "nsa_k_norm_2", 3), (B_DQ, "diff_q_norm_2", 1),
                                    (B_DK, "diff_k_norm_2", 1)):
                    src = a[name][0] if n == 3 else a[name]
                    pool.dma_start(rowsB[at:at + n, c * DH:(c + 1) * DH], src).then_inc(params_landed, 16)
                    n_params += 1
            pool.dma_start(rowsB[B_SUB:B_N, :], a["diff_subln_2"]).then_inc(params_landed, 16)
            n_params += 1
            pool.dma_start(wpool[:, :, :, :], a["w_pool"].rearrange("l g c d -> c l g d")).then_inc(wsmall_landed, 16)
            pool.dma_start(w2[:, :, :, :], a["nsa_cmp_w2_2"][0].rearrange("v (k p) d -> p v k d", p=P))\
               .then_inc(wsmall_landed, 16)
            pool.dma_start(lam[:, :, :], a["diff_lambda_2"][0].partition_broadcast(P)).then_inc(wsmall_landed, 16)
            assert n_params == N_PARAMS

            step(nc.gpsimd.iota(dist[:, :], pattern=[[-1, T]], base=P, channel_multiplier=1,
                                allow_small_or_imprecise_dtypes=True))
            step(nc.gpsimd.iota(dist_c[:, :, :], pattern=[[P, TT], [-16, NCMP]], base=-31, channel_multiplier=1,
                                allow_small_or_imprecise_dtypes=True))
            def pooling(l):
                p0 = pf[:, 16:20, :]
                src, dst = p0, pool_a
                for g, d in enumerate((1, 2, 4, 8)):
                    step(nc.gpsimd.tensor_copy(dst[:, g:4, 0:d], src[:, g:4, 0:d]))
                    step(nc.gpsimd.tensor_tensor(dst[:, g:4, d:T], src[:, g:4, d:T], src[:, g:4, 0:T - d], ALU.add))
                    src, dst = dst, (pool_b if dst is pool_a else pool_a)
                for g, w in enumerate(WINDOWS):
                    sv = (pool_a if g % 2 == 0 else pool_b)[:, g, :]
                    step(nc.gpsimd.tensor_tensor(sv[:, 0:16], sv[:, 0:16], count_fix[:, g, :], ALU.mult))
                    step(nc.gpsimd.tensor_scalar(sv, sv, 1.0 / w, None, ALU.mult))
                    step(nc.gpsimd.tensor_tensor(pool_b[:, g, :], sv, p0[:, g, :], ALU.subtract))
                pool.sem_inc(pooled_ready, 1)

            def conv(l):
                step(nc.gpsimd.tensor_tensor(z1[:, :, :], pf[:, 8:12, :], pf[:, 0:4, :], ALU.mult))
                tap = lambda j, n: colA[:, A_CONV + 12 * l + 4 * j:A_CONV + 12 * l + 4 * j + 4].unsqueeze(2)\
                    .to_broadcast([P, 4, n])
                step(nc.gpsimd.tensor_tensor(v1[:, :, :], z1[:, :, :], tap(2, T), ALU.mult))
                for j, d in ((1, 1), (0, 2)):
                    step(nc.gpsimd.tensor_tensor(v2[:, :, d:T], z1[:, :, 0:T - d], tap(j, T - d), ALU.mult))
                    step(nc.gpsimd.tensor_tensor(v1[:, :, d:T], v1[:, :, d:T], v2[:, :, d:T], ALU.add))
                pool.sem_inc(conv_ready, 1)

            for l in range(2):
                pool.wait_ge(colsd_ready, 2)
                pool.wait_ge(proj_ready, 12 * l + 2)
                pooling(l)
                pool.wait_ge(proj_ready, 12 * l + 6)
                conv(l)
            pool.wait_ge(x_ready, 4)
            for h in range(HQ):
                slope = 2.0 ** (-0.5 * (h + 1))
                step(nc.gpsimd.tensor_scalar(bias[:, h, :], dist[:, :], -slope, None, ALU.mult))
                step(nc.gpsimd.affine_select(out=bias[:, h, :], in_=bias[:, h, :], compare_op=ALU.is_ge,
                                             fill=NEG, base=P, pattern=[[-1, T]], channel_multiplier=1))
                step(nc.gpsimd.tensor_scalar(bias_c[:, :, h, :], dist_c[:, :, :], -slope, None, ALU.mult))
                step(nc.gpsimd.affine_select(out=bias_c[:, :, h, :], in_=bias_c[:, :, h, :], compare_op=ALU.is_ge,
                                             fill=NEG, base=-31, pattern=[[P, TT], [-16, NCMP]],
                                             channel_multiplier=1))
            step(nc.gpsimd.memset(kblk[:, :, :], 0.0))
            step(nc.gpsimd.memset(sel[:, :, :], 0.0))
            for f in range(2):
                v = sel[:, f, :].rearrange("p (j g n) -> p j g n", j=2, g=G)
                step(nc.gpsimd.affine_select(out=v, in_=v, compare_op=ALU.not_equal, fill=1.0, base=-2 * NCMP * f,
                                             pattern=[[-NCMP, 2], [0, G], [-1, NCMP]], channel_multiplier=1))
            step(nc.gpsimd.memset(vmask[:, :], 1.0))
            step(nc.gpsimd.affine_select(out=vmask[:, :], in_=vmask[:, :], compare_op=ALU.is_ge, fill=0.0, base=0,
                                         pattern=[[-NCMP, 8]], channel_multiplier=1))
            step(nc.gpsimd.affine_select(out=vmask[:, :], in_=vmask[:, :], compare_op=ALU.is_ge, fill=0.0,
                                         base=NCMP - 1, pattern=[[NCMP, 8]], channel_multiplier=-1))
            step(nc.gpsimd.memset(dist_c[:, :, :], 1.0))
            nc.gpsimd.affine_select(out=dist_c[:, :, :], in_=dist_c[:, :, :], compare_op=ALU.is_ge, fill=0.0,
                                    base=-31, pattern=[[P, TT], [-16, NCMP]],
                                    channel_multiplier=1).then_inc(bias_ready, 1)

        nsa_steps = [(b, hkv, tt) for b in ("sel", "win") for hkv in range(HKV) for tt in range(TT)]
        nsa_steps += [("cmp", half, tt) for half in range(2) for tt in range(TT)]
        diff_steps = [("diff", hp, tt) for hp in range(DIFF_H // 2) for tt in range(TT)]
        NS = len(nsa_steps)
        att_steps = nsa_steps + diff_steps
        NA = len(att_steps)
        pj = proj[:, 0:TT * NSA_IN].rearrange("p (t n) -> p t n", t=TT)
        vblk = pj[0:8 * NCMP, :, 1024:1536]
        pd = proj[:, :].rearrange("p (t n) -> p t n", t=TT)
        twice = xn.rearrange("p t (b h c d) -> p t b h c d", b=2, h=HKV, c=2)

        def nk(step):
            return NCMP if step[0] == "cmp" else P * (step[2] + 1)

        @block.scalar
        def _(act):
            steps = Tally(act_step)

            def step(ins):
                act.wait_ge(act_step, steps.value(steps.add(ins)))

            act.dma_start(rowsC[:, :], a["c"].rearrange("b (k p) -> (b k) p", p=P)).then_inc(c_landed, 16)

            split_at = [0]

            def split_hi(w, it=0, n=CH):
                r = w_raw[w]
                act.wait_ge(raw_landed[r % RAW], landed_value(r, it))
                if w >= SPL:
                    act.wait_ge(chunk_used, it * 6 + (w - SPL + 1))
                nc.scalar.activation(whi[:, w % SPL, 0:n], raw[:, r % RAW, 0:n], ACT.Copy).then_inc(hi_ready, 1)

            def split_to(w):
                while split_at[0] <= min(w, NW - 1):
                    split_hi(split_at[0], n=size(items[w_raw[split_at[0]]]))
                    split_at[0] += 1

            def sumsq(n_x):
                for tt in range(TT):
                    act.wait_ge(x_ready, 2 * n_x + tt + 1)
                    step(nc.scalar.activation(scratch[:, tt * D:(tt + 1) * D], x[:, tt, :], ACT.Square,
                                              accum_out=stat[:, tt:tt + 1]))
                    act.sem_inc(ss_ready, 1)

            def to_features(f, dst, scale=None, shift=None):
                for kt in range(KD):
                    if kt % 2 == 0:
                        act.wait_ge(turned, 4 * f + kt // 2 + 1)
                    src = acc[:, kt // 2, (kt % 2) * T:(kt % 2) * T + T]
                    if shift is not None:
                        nc.scalar.activation(h1[:, kt, :], src, ACT.Identity, bias=shift(kt), scale=scale(kt))\
                          .then_inc(feat_hi, 1)
                    elif scale is not None:
                        nc.scalar.activation(dst[:, kt, :], src, ACT.Copy, scale=scale(kt)).then_inc(feat_hi, 1)
                    else:
                        nc.scalar.activation(dst[:, kt, :], src, ACT.Copy).then_inc(feat_hi, 1)

            def ffn(q):
                w0 = w_at[("fin", q, 0, 0)]

                def silu_pair(j, it=0):
                    act.wait_ge(chunk_used, it * 6 + (w0 + pair_at(j) + 1))
                    act.wait_ge(gated, it * 2 + (NPAIR * q + j))
                    nc.scalar.activation(silu_a[:, j % 2, :], acc[:, (2 * j) % 4, :], ACT.Silu).then_inc(silu_ready, 1)

                for j in range(2):
                    split_to(w0 + pair_at(j) + LEAD)
                    silu_pair(j)
                split_to(w0 + 4 + LEAD)
                with act.Fori(0, 4) as it:
                    for c in range(6):
                        split_hi(w0 + 5 + c + LEAD, it)
                        if c % 3 == 0:
                            silu_pair(2 + c // 3, it)
                split_at[0] = w0 + 29 + LEAD
                split_to(w0 + 29 + LEAD)
                silu_pair(10)
                split_to(w0 + 31 + LEAD)

            def evict(n, w, dst, func=ACT.Copy, width=None):
                act.wait_ge(chunk_used, w + 1)
                src = acc[:, n % 4, :]
                if width is not None:
                    src = src.rearrange("p (t n) -> p t n", t=TT)[:, :, 0:width]
                nc.scalar.activation(dst, src, func).then_inc(proj_ready, 1)

            act.wait_ge(c_ps, 1)
            nc.scalar.activation(cact[:, :], acc[:, 7, 0:KD], ACT.Silu).then_inc(cact_ready, 1)
            nc.scalar.activation(lam_s[:, 7:8], acc[:, 7, 0:1], ACT.Copy).then_inc(silu_ready, 1)
            for l in range(2):
                if l == 0:
                    act.wait_ge(x_landed, 16)
                    for tt in range(TT):
                        step(nc.scalar.activation(scratch[:, tt * D:(tt + 1) * D], x[:, tt, :], ACT.Square,
                                                  accum_out=stat[:, tt:tt + 1]))
                        act.sem_inc(ss_ready, 1)
                else:
                    sumsq(0)
                split_to(w_at[("in1", l, IN1_ORDER[0])])
                act.wait_ge(diag_ready, 1 if l == 0 else 4)
                to_features(l, hT_hi, scale=lambda kt: gain1[:, l, kt:kt + 1], shift=lambda kt: shift1[:, l, kt:kt + 1])
                for n, c in enumerate(IN1_ORDER):
                    w = w_at[("in1", l, c)]
                    split_to(w + LEAD)
                    func = ACT.Silu if c in (6, 7, 10, 11) else ACT.Copy
                    evict(n, w, proj[:, c * 512:(c + 1) * 512], func)
                act.wait_ge(gate_ps, l + 1)
                nc.scalar.activation(gate_row[:, :], acc[:, 4:6, :].rearrange("p b n -> p (b n)"), ACT.Copy)\
                  .then_inc(gate_sb, 1)
                for c in OUT1_ORDER[:3]:
                    split_to(w_at[("out1", l, c)] + LEAD)
                for tt in range(TT):
                    bank_complete(act, l, 2 * tt + 1)
                    step(nc.scalar.activation(scratch[:, tt * D:(tt + 1) * D],
                                              acc[:, 4 + 2 * tt:6 + 2 * tt, :].rearrange("p b n -> p (b n)"),
                                              ACT.Square, accum_out=stat[:, 2 + tt:3 + tt]))
                    act.sem_inc(ss_ready, 1)
            ffn_x = {0: 1, 1: 3, 2: 4, 3: 6}
            gain_of = {0: A_F1, 1: A_F2, 2: A_F1 + KD, 3: A_F2 + KD}

            def ffn_all(q):
                sumsq(ffn_x[q])
                g0 = gain_of[q]
                to_features(CONV_FFN[q], hT_hi, scale=lambda kt: colA[:, g0 + kt:g0 + kt + 1])
                ffn(q)

            def attention(first, last):
                for i in range(first, last + 4):
                    if i >= first + 4 and att_steps[i - 4][0] == "diff":
                        j = i - 4
                        hp, tt = att_steps[j][1:]
                        act.wait_ge(pv_ps, j + 1)
                        for h in range(2):
                            ins = nc.scalar.activation(xn[:, tt, (2 * hp + h) * P:(2 * hp + h + 1) * P],
                                                       acc[:, 6 + j % 2, h * P:(h + 1) * P], ACT.Copy,
                                                       scale=psums[:, j % 4, 4 + h:5 + h])
                        ins.then_inc(combined, 1)
                        if j >= NA - TT:
                            act.wait_ge(combined, j + 1)
                            nc.scalar.activation(scratch[:, tt * D:(tt + 1) * D], xn[:, tt, :], ACT.Square)\
                              .then_inc(osq_ready, 1)
                    if first + 2 <= i < last + 2:
                        j = i - 2
                        s = att_steps[j]
                        act.wait_ge(probs_turned, j + 1)
                        if j >= first + 2:
                            act.wait_ge(pv_ps, j - 1)
                        if s[0] == "cmp":
                            nc.scalar.activation(pT[0:8 * NCMP, j % 2, 0:P], acc[0:8 * NCMP, 4, 0:P], ACT.Copy)\
                              .then_inc(pT_act, 1)
                        else:
                            n = (4 if s[0] != "diff" else 2) * nk(s)
                            nc.scalar.activation(pT[:, j % 2, 0:n],
                                                 acc[:, 4:6, :].rearrange("p b n -> p (b n)")[:, 0:n],
                                                 ACT.Copy).then_inc(pT_act, 1)
                            if i >= NA:
                                split_to(w_at[("diffo", i - NA)])
                    if i < last:
                        s = att_steps[i]
                        act.wait_ge(scored, i + 1)
                        b = i % 3
                        if s[0] == "cmp":
                            nc.scalar.activation(sc[:, b, 0:8 * NCMP], sc[:, b, 0:8 * NCMP], ACT.Exp)\
                              .then_inc(probs, 1)
                        else:
                            for m in range(4):
                                v = sc[:, b, m * nk(s):(m + 1) * nk(s)]
                                ins = nc.scalar.activation(v, v, ACT.Exp, bias=nmax[:, b, m:m + 1],
                                                           accum_out=psums[:, i % 4, m:m + 1])
                            ins.then_inc(probs, 1)

            ffn_all(0)
            sumsq(2)
            to_features(CONV_NSA, hT_hi, scale=lambda kt: colA[:, A_MIX + kt:A_MIX + kt + 1])
            for n, c in enumerate(NSA_ORDER):
                w = w_at[("nsa", c)]
                split_to(w + LEAD)
                if n in (8, 9):
                    tt = n - 8
                    act.wait_ge(proj_ready, 24 + 8)
                    act.wait_ge(cmpr_ready, 2)
                    if tt:
                        act.wait_ge(sq_free, 1)
                    nc.scalar.activation(scratch[:, 0:D], pj[:, tt, 0:D], ACT.Square).then_inc(qsq_ready, 1)
                    ksw = pj[:, tt, 1536:2560].rearrange("p (b n) -> p b n", b=2)[:, :, 0:256]
                    nc.scalar.activation(scratch[:, D:D + 512].rearrange("p (b n) -> p b n", b=2), ksw,
                                         ACT.Square).then_inc(qsq_ready, 1)
                if c in (4, 5):
                    act.wait_ge(chunk_used, w + 1)
                    for tt in range(TT):
                        ins = nc.scalar.activation(
                            twice[:, tt, c - 4], acc[:, n % 4, tt * T:(tt + 1) * T].rearrange("p (h d) -> p h d", d=DH)
                            .unsqueeze(2).to_broadcast([P, HKV, 2, DH]), ACT.Copy)
                    ins.then_inc(proj_ready, 1)
                else:
                    wd = NGATE if c == 10 else CC
                    evict(n, w, pj[:, :, c * CC:c * CC + wd], width=wd)
                if n == 4:
                    for kv in range(2):
                        for hb in range(2):
                            act.wait_ge(kc_ps, 2 * kv + hb + 1)
                            nc.scalar.activation(
                                kcT[0:DH, kv, 2 * hb:2 * hb + 2, :],
                                acc[0:DH, 4 + 2 * kv + hb, :].rearrange("p (h t) -> p h t", h=2),
                                ACT.Copy).then_inc(kc_act, 1)
            split_to(w_at[("cmp", 0, 0)] + LEAD)
            act.wait_ge(proj_ready, 24 + 11)
            nc.scalar.activation(gates[:, :, :], pj[:, :, NSA_IN - NGATE:NSA_IN], ACT.Exp, scale=-1.0)\
              .then_inc(gexp_ready, 1)
            for kv in range(2):
                for half in range(2):
                    split_to(w_at[("cmp", kv, half)] + LEAD)
            for kv in range(2):
                act.wait_ge(chunk_used, w_at[("cmp", kv, 1)] + 1)
                nc.scalar.activation(cmp_gt[:, kv, :], acc[0:HKV * NCMP, 4 + kv, 0:CMP_HIDDEN],
                                     ACT.Gelu_apprx_tanh).then_inc(gelu_ready, 1)

            def evict_heads(rnd, b):
                act.wait_ge(qk_turned, 4 * rnd + b + 1)
                dst = (qT if rnd == 0 else kT)[:, 2 * b:2 * b + 2, :]
                gcol = gq[:, 0:1] if rnd == 0 else colB[:, B_NK + 1 + b // 2:B_NK + 2 + b // 2]
                nc.scalar.activation(dst, acc[:, b, :].rearrange("p (h t) -> p h t", h=2), ACT.Copy,
                                     scale=gcol).then_inc(qk_act, 1)

            evict_heads(0, 0)
            evict_heads(0, 2)
            act.wait_ge(g_turned, 1)
            nc.scalar.activation(cmp_g.rearrange("p k c n -> p (k c n)"), acc[:, 6, 0:4 * HKV * NCMP], ACT.Copy)\
              .then_inc(g_sb, 1)
            evict_heads(1, 0)
            act.wait_ge(cmpk_ps, 1)
            step(nc.scalar.activation(otmp[0:HKV * NCMP, 0:DH], acc[0:HKV * NCMP, 4, 0:DH], ACT.Square,
                                      accum_out=stat[0:HKV * NCMP, 4:5]))
            act.sem_inc(cmpk_sq, 1)
            act.wait_ge(cmpv_ps, 1)
            nc.scalar.activation(v60, acc[0:HKV * NCMP, 5, 0:DH], ACT.Copy).then_inc(cmp_sb, 1)
            evict_heads(1, 2)
            act.wait_ge(kcn_ps, 1)
            act.wait_ge(bias_ready, 1)
            for e in range(2):
                half = slice(e * DH, (e + 1) * DH)
                nc.scalar.activation(kblk[half, :, e * NCMP:(e + 1) * NCMP],
                                     acc[half, 4, P:P + HKV * NCMP].rearrange("p (h n) -> p h n", h=HKV), ACT.Copy,
                                     scale=colB[half, B_NK:B_NK + 1]).then_inc(cmp_sb, 1)
            attention(0, NS)
            to_features(CONV_NSA_O, sT_hi)
            for c in range(3):
                split_to(w_at[("nsao", c)] + LEAD)
            ffn_all(1)
            ffn_all(2)
            sumsq(5)
            to_features(CONV_DIFF, hT_hi, scale=lambda kt: colA[:, A_MIX + KD + kt:A_MIX + KD + kt + 1])
            for n in range(12):
                w = w_at[("diff", n)]
                split_to(min(w + LEAD, w_at[("diff", 11)]))
                if n in (8, 9):
                    tt = n - 8
                    act.wait_ge(proj_ready, 35 + 8)
                    if tt:
                        act.wait_ge(sq_free, 2 + tt)
                    nc.scalar.activation(scratch[:, 0:2 * D], pd[:, tt, 0:2 * D], ACT.Square).then_inc(qsq_ready, 1)
                evict(n, w, pd[:, :, n * CC:(n + 1) * CC], width=CC)
            for b in (4, 6, 0, 2):
                act.wait_ge(qk_turned, 8 + DIFF_BANKS.index(b) + 1)
                dst = (qT if b < 4 else kT)[:, 2 * (b % 4):2 * (b % 4) + 2, :]
                gcol = gq[:, 1:2] if b < 4 else colB[:, B_DK:B_DK + 1]
                nc.scalar.activation(dst, acc[:, b, :].rearrange("p (h t) -> p h t", h=2), ACT.Copy,
                                     scale=gcol).then_inc(qk_act, 1)
            act.wait_ge(gexp_ready, 2)
            nc.scalar.activation(lam_s[:, 2:4], lam_s[:, 0:2], ACT.Exp).then_inc(gexp_ready, 1)
            attention(NS, NA)
            to_features(CONV_DIFF_O, sT_hi, scale=lambda kt: gsub[:, 0:1])
            for c in range(3):
                split_to(w_at[("diffo", c)] + LEAD)
            ffn_all(3)

        @block.vector
        def _(dve):
            steps = Tally(dve_step)

            def step(ins):
                dve.wait_ge(dve_step, steps.value(steps.add(ins)))

            raw_at = [0]

            def split_lo(r, n, w, it=0):
                dve.wait_ge(hi_ready, it * 6 + (w + 1))
                nc.vector.tensor_tensor(wlo[:, w % SPL, 0:n], raw[:, r % RAW, 0:n], whi_f[:, w % SPL, 0:n],
                                        ALU.subtract).then_inc(raw_done, 1)

            def accumulate_ada(r, l, c):
                dve.wait_ge(raw_landed[r % RAW], landed_value(r))
                if l == 1 and c == 8:
                    dve.wait_ge(mod_ps, 2)
                dst = acc_ada[:, c * CC:(c + 1) * CC]
                v = raw[:, r % RAW, :].rearrange("p (k n) -> p k n", k=8)
                n0 = steps.n
                for k in range(8):
                    to = dst if k % 2 == 0 else ada2[:, :]
                    if k < 2:
                        ins = nc.vector.tensor_scalar(to, v[:, k, :], cact[:, k:k + 1], None, ALU.mult)
                    else:
                        dve.wait_ge(dve_step, n0 + k - 1)
                        ins = nc.vector.scalar_tensor_tensor(out=to, in0=v[:, k, :], scalar=cact[:, k:k + 1], in1=to,
                                                             op0=ALU.mult, op1=ALU.add)
                    steps.add(ins)
                dve.wait_ge(dve_step, steps.n)
                nc.vector.tensor_tensor(dst, dst, ada2[:, :], ALU.add).then_inc(raw_done, 1)
                dve.wait_ge(raw_done, r + 1)
                if (l, c) != (0, 7) and c in (7, 11):
                    dve.sem_inc(ada_ready, 1)

            def stream_to(w):
                end = w_raw[min(w, NW - 1)] + 1
                while raw_at[0] < end:
                    r = raw_at[0]
                    if items[r][0] == "ada":
                        accumulate_ada(r, items[r][1], items[r][2])
                    else:
                        split_lo(r, size(items[r]), w_raw.index(r))
                    raw_at[0] += 1

            def rsqrt(dst, src, n, inv_n, parts=P):
                h, u, v = (t[0:parts, 0:n] for t in (nt0, nt1, nt2))
                step(nc.vector.tensor_scalar(h, src, 0.5 * inv_n, 0.5 * EPS, ALU.mult, ALU.add))
                step(nc.vector.tensor_scalar(v.bitcast(I32), h.bitcast(I32), -0.5, float(SEED), ALU.mult, ALU.add))
                for i in range(3):
                    if n == 1:
                        step(nc.vector.scalar_tensor_tensor(out=u, in0=v, scalar=h, in1=v, op0=ALU.mult, op1=ALU.mult))
                    else:
                        step(nc.vector.tensor_tensor(u, v, v, ALU.mult))
                        step(nc.vector.tensor_tensor(u, u, h, ALU.mult))
                    step(nc.vector.scalar_tensor_tensor(out=dst if i == 2 else v, in0=u, scalar=-1.5, in1=v,
                                                        op0=ALU.add, op1=ALU.mult))

            def normalise(n_ss, tiles=range(TT)):
                for tt in tiles:
                    dve.wait_ge(ss_ready, n_ss + tt + 1)
                    rsqrt(rs[:, tt:tt + 1], stat[:, tt:tt + 1], 1, 1.0 / D)
                    nc.vector.tensor_scalar(xn[:, tt, :], x[:, tt, :], rs[:, tt:tt + 1], None, ALU.mult)\
                      .then_inc(xn_ready, 1)

            def to_features(f, dst_hi, dst_lo, scale=None):
                for kt in range(KD):
                    if kt % 2 == 0:
                        dve.wait_ge(feat_hi, 8 * f + kt + 2)
                    src = acc[:, kt // 2, (kt % 2) * T:(kt % 2) * T + T]
                    if scale is not None:
                        nc.vector.scalar_tensor_tensor(out=dst_lo[:, kt, :], in0=src, scalar=scale(kt),
                                                       in1=dst_hi[:, kt, :], op0=ALU.mult, op1=ALU.subtract)\
                          .then_inc(feat_ready, 1)
                    else:
                        nc.vector.tensor_tensor(dst_lo[:, kt, :], src, dst_hi[:, kt, :], ALU.subtract)\
                          .then_inc(feat_ready, 1)

            def residual(o, factor):
                for tt in range(TT):
                    for nh in range(2):
                        bank_complete(dve, o, 2 * tt + nh)
                        xv = x[:, tt, nh * 512:(nh + 1) * 512]
                        ins = nc.vector.scalar_tensor_tensor(out=xv, in0=acc[:, 4 + 2 * tt + nh, :], scalar=factor,
                                                             in1=xv, op0=ALU.mult, op1=ALU.add)
                        if nh == 0:
                            step(ins)
                    ins.then_inc(x_ready, 1)
                dve.wait_ge(x_ready, 2 * (o + 1))

            def ffn(q):
                w0, r0 = w_at[("fin", q, 0, 0)], w_raw[w_at[("fin", q, 0, 0)]]

                def gate_pair(j, it=0):
                    dve.wait_ge(silu_ready, it * 2 + (NPAIR * q + j + 2))
                    dve.wait_ge(chunk_used, it * 6 + (w0 + pair_at(j) + 2))
                    dve.wait_ge(s_ready, it * 2 + (8 + NPAIR * q + j))
                    nc.vector.tensor_tensor(sact[:, :], silu_a[:, j % 2, :], acc[:, (2 * j + 1) % 4, :],
                                            ALU.mult).then_inc(gated, 1)
                    dve.wait_ge(gated, it * 2 + (NPAIR * q + j + 2))
                    at = slice(2 * (j % 2), 2 * (j % 2) + 2)
                    sv = sact.rearrange("p (k t) -> p k t", t=T)
                    step(nc.vector.tensor_copy(sT_hi[:, at, :], sv))
                    nc.vector.tensor_tensor(sT_lo[:, at, :], sv, sT_hi_f[:, at, :], ALU.subtract).then_inc(s_ready, 1)

                for j in range(2):
                    stream_to(w0 + pair_at(j) + 1 + LEAD)
                    gate_pair(j)
                stream_to(w0 + 4 + LEAD)
                n0 = steps.n
                with dve.Fori(0, 4) as it:
                    steps.it, steps.per = it, 2
                    for c in range(6):
                        split_lo(r0 + 5 + c + LEAD, CH, w0 + 5 + c + LEAD, it)
                        if c % 3 == 1:
                            gate_pair(2 + c // 3, it)
                    steps.it = None
                steps.n = n0 + 8
                raw_at[0] = r0 + 29 + LEAD
                stream_to(w0 + 30 + LEAD)
                gate_pair(10)
                stream_to(w0 + 31 + LEAD)

            def ada_chunks(n):
                for _ in range(n):
                    accumulate_ada(raw_at[0], 0, items[raw_at[0]][2])
                    raw_at[0] += 1

            dve.wait_ge(cact_ready, 1)
            ada_chunks(3)
            normalise(0, [0])
            ada_chunks(1)
            normalise(0, [1])
            ada_chunks(1)
            dve.wait_ge(cols_ready, 1)
            step(nc.vector.tensor_copy(colA[:, :], acc[:, 4, 0:A_N]))
            step(nc.vector.tensor_copy(colB[:, :], acc[:, 5, 0:B_N]))
            dve.sem_inc(colsd_ready, 1)
            nc.vector.memset(otmp[:, 0:1], 0.0).then_inc(gated, 1)

            def modulation(l, part):
                dve.wait_ge(mod_ps, 2 * l + part + 1)
                if part == 0:
                    step(nc.vector.tensor_tensor(mod[:, 0:16], acc[:, 6 if l == 0 else 0, 0:16], colB[:, 24 * l:24 * l + 16], ALU.add))
                    step(nc.vector.tensor_copy(shift1[:, l, :], mod[:, 0:8]))
                    step(nc.vector.scalar_tensor_tensor(out=gain1[:, l, :], in0=mod[:, 8:16], scalar=1.0,
                                                        in1=colA[:, A_GPRE + 8 * l:A_GPRE + 8 * l + 8], op0=ALU.add,
                                                        op1=ALU.mult))
                    dve.sem_inc(diag_ready, 1)
                else:
                    step(nc.vector.tensor_tensor(mod[:, 16:24], acc[:, 4, 16:24],
                                                 colB[:, 24 * l + 16:24 * l + 24], ALU.add))
                    step(nc.vector.tensor_tensor(gate_col[:, :], mod[:, 16:24],
                                                 colA[:, A_GPOST + 8 * l:A_GPOST + 8 * l + 8], ALU.mult))
                    for kt in range(KD):
                        ins = nc.vector.tensor_scalar(diag[:, kt * P:(kt + 1) * P], ident[:, :],
                                                      gate_col[:, kt:kt + 1], None, ALU.mult)
                        step(ins)
                    dve.sem_inc(diag_ready, 2)

            def y_split(k0, n):
                for k in range(k0, k0 + n, 2):
                    step(nc.vector.tensor_copy(sT_hi[:, k:k + 2, :], y1[:, k:k + 2, :]))
                    nc.vector.tensor_tensor(sT_lo[:, k:k + 2, :], y1[:, k:k + 2, :], sT_hi_f[:, k:k + 2, :],
                                            ALU.subtract).then_inc(s_ready, 1)

            n_ss = 0
            n_proj = 0
            for l in range(2):
                if l == 0:
                    ada_chunks(3)
                    modulation(0, 0)
                    stream_to(0)
                else:
                    normalise(n_ss)
                n_ss += 2
                for kt in range(KD):
                    dve.wait_ge(feat_hi, 8 * l + kt + 1)
                    step(nc.vector.tensor_copy(hT_hi[:, kt, :], h1[:, kt, :]))
                    nc.vector.tensor_tensor(hT_lo[:, kt, :], h1[:, kt, :], hT_hi_f[:, kt, :], ALU.subtract)\
                      .then_inc(feat_ready, 1)
                for n, c in enumerate(IN1_ORDER):
                    stream_to(w_at[("in1", l, c)] + LEAD)
                    if n == 0 and l == 0:
                        dve.wait_ge(consts_ready, 1)
                        step(nc.vector.reciprocal(pos1[:, :], pos1[:, :]))
                        for g, w in enumerate(WINDOWS):
                            step(nc.vector.tensor_scalar(count_fix[:, g, :], pos1[:, :], float(w), 1.0, ALU.mult, ALU.max))
                        step(nc.vector.tensor_scalar(gq[:, 0:1], colB[:, B_NQ:B_NQ + 1], DH ** -0.5, None, ALU.mult))
                        step(nc.vector.tensor_scalar(gq[:, 1:2], colB[:, B_DQ:B_DQ + 1], DH ** -0.5, None, ALU.mult))
                        step(nc.vector.tensor_scalar(gsub[:, :], colB[:, B_SUB:B_SUB + 1], 1.0 - LAM_INIT, None, ALU.mult))
                        dve.wait_ge(wsmall_landed, 48)
                        lp = otmp[:, 0:2 * DH].rearrange("p (a d) -> p a d", a=2)
                        lv = lam.rearrange("p (a b) d -> p a b d", b=2)
                        step(nc.vector.tensor_tensor(lp, lv[:, :, 0, :], lv[:, :, 1, :], ALU.mult))
                        step(nc.vector.tensor_reduce(out=lam_s[:, 0:2], in_=lp, axis=AX.X, op=ALU.add))
                        dve.sem_inc(colsd_ready, 1)
                    if n == 8:
                        dve.wait_ge(proj_ready, n_proj + 8)
                        dve.wait_ge(mixed_ps, l + 1)
                        for g in range(4):
                            step(nc.vector.scalar_tensor_tensor(
                                out=y1[:, 4 + g, :], in0=acc[:, 6 + g // 2, (g % 2) * T:(g % 2) * T + T],
                                scalar=colA[:, A_POOL + 4 * l + g:A_POOL + 4 * l + g + 1], in1=pf[:, 20 + g, :],
                                op0=ALU.mult, op1=ALU.mult))
                        y_split(4, 4)
                    if n == 6:
                        modulation(l, 1)
                    if n == 10:
                        dve.wait_ge(proj_ready, n_proj + 10)
                        dve.wait_ge(conv_ready, l + 1)
                        step(nc.vector.tensor_tensor(v1[:, :, :], v1[:, :, :], pf[:, 12:16, :], ALU.mult))
                for hf in range(2):
                    dve.wait_ge(proj_ready, n_proj + 11 + hf)
                    step(nc.vector.tensor_tensor(y1[:, 2 * hf:2 * hf + 2, :], v1[:, 2 * hf:2 * hf + 2, :],
                                                 pf[:, 4 + 2 * hf:6 + 2 * hf, :], ALU.mult))
                    y_split(2 * hf, 2)
                n_proj += 12
                for c in OUT1_ORDER[:3]:
                    stream_to(w_at[("out1", l, c)] + LEAD)
                dve.wait_ge(gate_sb, l + 1)
                for tt in range(TT):
                    dve.wait_ge(ss_ready, n_ss + tt + 1)
                    step(nc.vector.tensor_tensor(
                        xn[:, tt, :], acc[:, 4 + 2 * tt:6 + 2 * tt, :].rearrange("p b n -> p (b n)"),
                        gate_row[:, :], ALU.mult))
                    rsqrt(rs[:, 2 + tt:3 + tt], stat[:, 2 + tt:3 + tt], 1, 1.0 / D)
                    nc.vector.scalar_tensor_tensor(out=x[:, tt, :], in0=xn[:, tt, :], scalar=rs[:, 2 + tt:3 + tt],
                                                   in1=x[:, tt, :], op0=ALU.mult, op1=ALU.add).then_inc(x_ready, 1)
                n_ss += 2
                dve.wait_ge(x_ready, 2 * (l + 1))
                if l == 0:
                    modulation(1, 0)

            gain_of = {0: A_F1, 1: A_F2, 2: A_F1 + KD, 3: A_F2 + KD}

            def ffn_all(q, n_ss):
                normalise(n_ss)
                g0 = gain_of[q]
                to_features(CONV_FFN[q], hT_hi_f, hT_lo, scale=lambda kt: colA[:, g0 + kt:g0 + kt + 1])
                ffn(q)
                residual(OUT_FFN[q], 0.5)

            def combine(j):
                s = att_steps[j]
                dve.wait_ge(pv_ps, j + 1)
                O = acc[:, 6 + j % 2, :]
                if s[0] == "cmp":
                    half, tt = s[1:]
                    step(nc.vector.reciprocal(rw[:, 0:8], psums[:, j % 4, 0:8]))
                    step(nc.vector.tensor_tensor(
                        rw[:, 0:8], rw[:, 0:8],
                        gates[:, tt, :].rearrange("p (h b) -> p h b", b=3)[:, 8 * half:8 * half + 8, 0], ALU.mult))
                    rb = rw[:, 0:8].unsqueeze(2).to_broadcast([P, 8, DH])
                    ov = xn[:, tt, half * 512:(half + 1) * 512]
                    step(nc.vector.tensor_tensor(wtmp.rearrange("p (m d) -> p m d", d=DH),
                                                 O.rearrange("p (m d) -> p m d", d=DH), rb, ALU.mult))
                    nc.vector.tensor_tensor(ov, ov, wtmp, ALU.add).then_inc(combined, 1)
                    dve.wait_ge(combined, j + 1)
                    return
                br = {"sel": 1, "win": 2}[s[0]]
                tt, nh, h0 = s[2], 4, 4 * s[1]
                ps = psums[:, j % 4, 0:nh]
                gv = gates[:, tt, 3 * h0:3 * (h0 + nh)].rearrange("p (h e b) -> p e h b", e=2, b=3)[:, :, :, br]
                step(nc.vector.reciprocal(rw[:, 0:nh], ps))
                rv = rw[:, 0:nh].rearrange("p (e h) -> p e h", e=2)
                step(nc.vector.tensor_tensor(rv, rv, gv, ALU.mult))
                ov = xn[:, tt, h0 * DH:(h0 + nh) * DH].rearrange("p (h e d) -> p e h d", e=2, d=DH)
                for e in range(2):
                    Oe = O[:, 2 * e * DH:2 * (e + 1) * DH].rearrange("p (h d) -> p h d", d=DH)
                    re = rw[:, 2 * e:2 * e + 2].unsqueeze(2).to_broadcast([P, 2, DH])
                    te = wtmp[:, 2 * e * DH:2 * (e + 1) * DH].rearrange("p (h d) -> p h d", d=DH)
                    ins = nc.vector.tensor_tensor(ov[:, e] if s[0] == "sel" else te, Oe, re, ALU.mult)
                if s[0] == "sel":
                    ins.then_inc(combined, 1)
                else:
                    step(ins)
                    nc.vector.tensor_tensor(ov, ov, wtmp[:, 0:nh * DH].rearrange("p (e h d) -> p e h d", e=2, d=DH),
                                            ALU.add).then_inc(combined, 1)
                dve.wait_ge(combined, j + 1)

            def attention(first, last):
                for i in range(first, last + (4 if first == 0 else 1)):
                    if i >= first + 4 and first == 0:
                        combine(i - 4)
                    if i < last:
                        s = att_steps[i]
                        b = i % 3
                        dve.wait_ge(qk_ps, i + 1)
                        if i >= first + 3:
                            dve.wait_ge(probs_turned, i - 2)
                        n = nk(s)
                        S = acc[:, 2 * (i % 2):2 * (i % 2) + 2, :]
                        if s[0] == "cmp":
                            flat = sc[:, b, 0:8 * n].rearrange("p (m n) -> p m n", m=8)
                            step(nc.vector.tensor_tensor(flat, S[:, 0, 0:8 * n].rearrange("p (m n) -> p m n", m=8),
                                                         bias_c[:, s[2], 8 * s[1]:8 * s[1] + 8], ALU.add))
                            step(nc.vector.tensor_reduce(out=nmax[:, b, 0:8], in_=flat, axis=AX.X, op=ALU.max))
                            nc.vector.tensor_tensor(flat, flat, nmax[:, b, 0:8].unsqueeze(2).to_broadcast([P, 8, n]),
                                                    ALU.subtract).then_inc(scored, 1)
                        else:
                            off = P if s[2] == 0 else 0
                            scv = sc[:, b, 0:4 * n].rearrange("p (e h n) -> p e h n", e=2, h=2)
                            if s[0] == "diff":
                                bv = bias.rearrange("p (h e) s -> p h e s", e=2)[:, 2 * s[1]:2 * s[1] + 2, 1,
                                                                                off:off + n]
                                for e in range(2):
                                    ins = nc.vector.tensor_tensor(
                                        scv[:, e], S[:, e, :].rearrange("p (h s) -> p h s", h=2)[:, :, 0:n], bv,
                                        ALU.add)
                                    step(ins)
                            else:
                                bv = bias[:, 4 * s[1]:4 * s[1] + 4, off:off + n].rearrange(
                                    "p (h e) s -> p e h s", e=2)
                                step(nc.vector.tensor_tensor(
                                    scv, S.rearrange("p e (h s) -> p e h s", h=2)[:, :, :, 0:n], bv, ALU.add))
                            flat = sc[:, b, 0:4 * n].rearrange("p (m n) -> p m n", m=4)
                            nc.vector.tensor_reduce(out=nmax[:, b, 0:4], in_=flat, axis=AX.X, op=ALU.max,
                                                    negate=True).then_inc(scored, 1)
                    if first < i <= last:
                        j = i - 1
                        s = att_steps[j]
                        n = nk(s)
                        if s[0] == "cmp":
                            dve.wait_ge(probs, j + 1)
                            flat = sc[:, j % 3, 0:8 * n].rearrange("p (m n) -> p m n", m=8)
                            step(nc.vector.tensor_reduce(out=psums[:, j % 4, 0:8], in_=flat, axis=AX.X, op=ALU.add))
                            nc.vector.tensor_tensor(flat, flat,
                                                    dist_c[:, s[2], :].unsqueeze(1).to_broadcast([P, 8, n]),
                                                    ALU.mult).then_inc(mixed, 1)
                        elif s[0] == "diff":
                            dve.wait_ge(probs, j + 1)
                            pv = sc[:, j % 3, 0:4 * n].rearrange("p (m n) -> p m n", m=4)
                            ps = psums[:, j % 4, :]
                            step(nc.vector.reciprocal(ps[:, 4:8], ps[:, 0:4]))
                            step(nc.vector.scalar_tensor_tensor(out=ps[:, 8:10], in0=ps[:, 6:8],
                                                                scalar=lam_s[:, 5:6], in1=ps[:, 0:2], op0=ALU.mult,
                                                                op1=ALU.mult))
                            for h in range(2):
                                ins = nc.vector.scalar_tensor_tensor(out=pv[:, h, :], in0=pv[:, 2 + h, :],
                                                                     scalar=ps[:, 8 + h:9 + h], in1=pv[:, h, :],
                                                                     op0=ALU.mult, op1=ALU.add)
                            ins.then_inc(mixed, 1)

            ffn_all(0, n_ss)
            n_ss += 2
            normalise(n_ss)
            n_ss += 2
            to_features(CONV_NSA, hT_hi_f, hT_lo, scale=lambda kt: colA[:, A_MIX + kt:A_MIX + kt + 1])
            for n, c in enumerate(NSA_ORDER):
                stream_to(w_at[("nsa", c)] + LEAD)
                if n == 4:
                    for kv in range(2):
                        for hb in range(2):
                            dve.wait_ge(kc_ps, 2 * kv + hb + 1)
                            step(nc.vector.tensor_copy(
                                kcT[DH:P, kv, 2 * hb:2 * hb + 2, 0:T - 1],
                                acc[DH:P, 4 + 2 * kv + hb, :].rearrange("p (h t) -> p h t", h=2)[:, :, 1:T]))
                    dve.wait_ge(kc_act, 4)
                    for kv in range(2):
                        kv_v = kcT[:, kv].rearrange("p h (n m r) -> p m h n r", m=8, r=2)
                        for mh in range(2):
                            src = kv_v[:, :, :, mh:mh + NCMP, 0]
                            dst = cmpR[:, kv, 8 * mh:8 * mh + 8, :].rearrange("p m (h n) -> p m h n", h=HKV)
                            pos = colB[:, B_POS + 16 * kv + 8 * mh:B_POS + 16 * kv + 8 * mh + 8]
                            step(nc.vector.tensor_tensor(
                                dst, src, pos.unsqueeze(2).unsqueeze(3).to_broadcast([P, 8, HKV, NCMP]), ALU.add))
                        step(nc.vector.tensor_copy(cmp_hi[:, kv], cmpR[:, kv]))
                        nc.vector.tensor_tensor(cmp_lo[:, kv], cmpR[:, kv], cmp_hi_f[:, kv], ALU.subtract)\
                          .then_inc(cmpr_ready, 1)
                if n in (8, 9):
                    tt = n - 8
                    dve.wait_ge(qsq_ready, 2 * tt + 2)
                    step(nc.vector.tensor_reduce(out=stat[:, 8 + 24 * tt:32 + 24 * tt],
                                                 in_=scratch[:, 0:24 * DH].rearrange("p (g d) -> p g d", d=DH),
                                                 axis=AX.X, op=ALU.add))
                    dve.sem_inc(sq_free, 1)
                if n == 9:
                    rsqrt(rs[:, 8:56], stat[:, 8:56], 48, 1.0 / DH)
                if n == 10:
                    for tt in range(TT):
                        qv = pj[:, tt, 0:D].rearrange("p (h d) -> p h d", d=DH)
                        rq = rs[:, 8 + 24 * tt:24 + 24 * tt].unsqueeze(2).to_broadcast([P, HQ, DH])
                        nc.vector.tensor_tensor(qv, qv, rq, ALU.mult).then_inc(qn_ready, 1)
                        for b in range(2):
                            kv_ = pj[:, tt, 1536 + 512 * b:1792 + 512 * b].rearrange("p (h d) -> p h d", d=DH)
                            rk = rs[:, 24 + 24 * tt + 4 * b:28 + 24 * tt + 4 * b]
                            shape = [P, HKV, 2, DH]
                            nc.vector.tensor_tensor(twice[:, tt, b], kv_.unsqueeze(2).to_broadcast(shape),
                                                    rk.unsqueeze(2).unsqueeze(3).to_broadcast(shape),
                                                    ALU.mult).then_inc(qn_ready, 1)
            stream_to(w_at[("cmp", 0, 0)] + LEAD)
            dve.wait_ge(gexp_ready, 1)
            step(nc.vector.tensor_scalar(gates[:, :, :], gates[:, :, :], 1.0, None, ALU.add))
            step(nc.vector.reciprocal(gates[:, :, :], gates[:, :, :]))
            dve.sem_inc(gexp_ready, 1)
            stream_to(w_at[("cmp", 0, 1)] + LEAD)
            stream_to(w_at[("cmp", 1, 0)] + LEAD)
            stream_to(w_at[("cmp", 1, 1)] + LEAD)

            def evict_heads(rnd, b):
                dve.wait_ge(qk_turned, 4 * rnd + b + 1)
                dst = (qT if rnd == 0 else kT)[:, 2 * b:2 * b + 2, :]
                gcol = gq[:, 0:1] if rnd == 0 else colB[:, B_NK + 1 + b // 2:B_NK + 2 + b // 2]
                nc.vector.tensor_scalar(dst, acc[:, b, :].rearrange("p (h t) -> p h t", h=2), gcol, None,
                                        ALU.mult).then_inc(qk_dve, 1)

            evict_heads(0, 1)
            evict_heads(0, 3)
            evict_heads(1, 1)
            dve.wait_ge(cmpk_sq, 1)
            nk_rows = HKV * NCMP
            rsqrt(rs[0:nk_rows, 4:5], stat[0:nk_rows, 4:5], 1, 1.0 / DH, parts=nk_rows)
            for c in range(2):
                ins = nc.vector.tensor_scalar(kcn[:, c, :], acc[0:nk_rows, 4, 0:DH], rs[0:nk_rows, 4:5], None, ALU.mult)
                ins.then_inc(kcn_ready, 1)
            evict_heads(1, 3)
            dve.wait_ge(vsel_ps, 1)
            dve.wait_ge(bias_ready, 1)
            for f in range(2):
                shape = [8 * NCMP, 8, DH]
                nc.vector.tensor_tensor(
                    vblk[:, f, :].rearrange("p (m d) -> p m d", d=DH),
                    acc[0:8 * NCMP, 7, f * DH:(f + 1) * DH].unsqueeze(1).to_broadcast(shape),
                    vmask[:, :].unsqueeze(2).to_broadcast(shape), ALU.mult).then_inc(vblk_ready, 1)
            dve.wait_ge(bias_ready, 1)
            attention(0, NS)
            for tt in range(TT):
                dve.sem_inc(xn_ready, 1)
            to_features(CONV_NSA_O, sT_hi_f, sT_lo)
            for c in range(3):
                stream_to(w_at[("nsao", c)] + LEAD)
            residual(OUT_NSA, 1.0)
            ffn_all(1, n_ss)
            n_ss += 2
            ffn_all(2, n_ss)
            n_ss += 2
            normalise(n_ss)
            n_ss += 2
            to_features(CONV_DIFF, hT_hi_f, hT_lo, scale=lambda kt: colA[:, A_MIX + KD + kt:A_MIX + KD + kt + 1])
            for n in range(12):
                stream_to(w_at[("diff", min(n + LEAD, 11))])
                if n in (8, 9):
                    tt = n - 8
                    dve.wait_ge(qsq_ready, 4 + tt + 1)
                    step(nc.vector.tensor_reduce(out=stat[:, 32 * tt:32 * tt + 32],
                                                 in_=scratch[:, 0:2 * D].rearrange("p (g d) -> p g d", d=DH),
                                                 axis=AX.X, op=ALU.add))
                    dve.sem_inc(sq_free, 1)
                if n == 9:
                    rsqrt(rs[:, 0:64], stat[:, 0:64], 64, 1.0 / DH)
                for tt in range(TT if n == 10 else 0):
                    qv = pd[:, tt, 0:2 * D].rearrange("p (h d) -> p h d", d=DH)
                    rq = rs[:, 32 * tt:32 * tt + 32].unsqueeze(2).to_broadcast([P, 32, DH])
                    nc.vector.tensor_tensor(qv, qv, rq, ALU.mult).then_inc(qn_ready, 1)
            for b in (5, 7, 1, 3):
                dve.wait_ge(qk_turned, 8 + DIFF_BANKS.index(b) + 1)
                dst = (qT if b < 4 else kT)[:, 2 * (b % 4):2 * (b % 4) + 2, :]
                gcol = gq[:, 1:2] if b < 4 else colB[:, B_DK:B_DK + 1]
                nc.vector.tensor_scalar(dst, acc[:, b, :].rearrange("p (h t) -> p h t", h=2), gcol, None,
                                        ALU.mult).then_inc(qk_dve, 1)
            dve.wait_ge(gexp_ready, 3)
            step(nc.vector.tensor_tensor(lam_s[:, 4:5], lam_s[:, 3:4], lam_s[:, 2:3], ALU.subtract))
            step(nc.vector.tensor_scalar(lam_s[:, 5:6], lam_s[:, 4:5], LAM_INIT, None, ALU.subtract))
            attention(NS, NA)
            stream_to(w_at[("diffo", 1)])
            for tt in range(TT):
                dve.wait_ge(osq_ready, tt + 1)
                step(nc.vector.tensor_reduce(out=stat[:, 8 * tt:8 * tt + 8],
                                             in_=scratch[:, tt * D:(tt + 1) * D].rearrange("p (g d) -> p g d", d=P),
                                             axis=AX.X, op=ALU.add))
                rsqrt(rs[:, 8 * tt:8 * tt + 8], stat[:, 8 * tt:8 * tt + 8], 8, 1.0 / P)
                ov = xn[:, tt, :].rearrange("p (h d) -> p h d", d=P)
                ro = rs[:, 8 * tt:8 * tt + 8].unsqueeze(2).to_broadcast([P, DIFF_H, P])
                nc.vector.tensor_tensor(ov, ov, ro, ALU.mult).then_inc(xn_ready, 1)
            to_features(CONV_DIFF_O, sT_hi_f, sT_lo, scale=lambda kt: gsub[:, 0:1])
            for c in range(3):
                stream_to(w_at[("diffo", c)] + LEAD)
            residual(OUT_DIFF, 1.0)
            ffn_all(3, n_ss)

        @block.tensor
        def _(pe):
            def turn(f):
                for tt in range(TT):
                    pe.wait_ge(xn_ready, 2 * f + tt + 1)
                    for kt in range(KD):
                        ins = nc.tensor.transpose(acc[:, kt // 2, (kt % 2) * T + tt * P:(kt % 2) * T + tt * P + P],
                                                  xn[:, tt, kt * P:(kt + 1) * P], ident[:, :])
                        if tt == 1 and kt % 2 == 1:
                            ins.then_inc(turned, 1)

            def chunk_ready(w, it=0):
                pe.wait_ge(raw_done, it * 6 + (w_raw[w] + 1))

            def cols_by_tokens(w, bank, it=0, first=None):
                s = w % SPL
                hi = whi[:, s, :].rearrange("p (k n) -> p k n", k=8)
                lo = wlo[:, s, :].rearrange("p (k n) -> p k n", k=8)
                for ft in range(2):
                    o = acc[:, bank, ft * T:(ft + 1) * T]
                    cs = slice(ft * P, (ft + 1) * P)
                    for kt in range(KD):
                        if first is not None and ft == 0 and kt % 2 == 0:
                            pe.wait_ge(feat_ready, 8 * first + kt + 2)
                        nc.tensor.matmul(o, hi[:, kt, cs], hT_hi[:, kt, :], start=kt == 0, stop=False)
                        nc.tensor.matmul(o, hi[:, kt, cs], hT_lo[:, kt, :], start=False, stop=False)
                        ins = nc.tensor.matmul(o, lo[:, kt, cs], hT_hi[:, kt, :], start=False, stop=kt == KD - 1)
                ins.then_inc(chunk_used, 1)

            def tokens_by_cols(w, bank, n=CC, first=None):
                s = w % SPL
                hi = whi[:, s, 0:8 * n].rearrange("p (k n) -> p k n", k=8)
                lo = wlo[:, s, 0:8 * n].rearrange("p (k n) -> p k n", k=8)
                for tt in range(TT):
                    o = acc[:, bank, tt * T:tt * T + n]
                    ts = slice(tt * P, (tt + 1) * P)
                    for kt in range(KD):
                        if first is not None and tt == 0 and kt % 2 == 0:
                            pe.wait_ge(feat_ready, 8 * first + kt + 2)
                        nc.tensor.matmul(o, hT_hi[:, kt, ts], hi[:, kt, :], start=kt == 0, stop=False)
                        nc.tensor.matmul(o, hT_hi[:, kt, ts], lo[:, kt, :], start=False, stop=False)
                        ins = nc.tensor.matmul(o, hT_lo[:, kt, ts], hi[:, kt, :], start=False, stop=kt == KD - 1)
                ins.then_inc(chunk_used, 1)

            def out_chunk(w, kts, start, stop):
                s = w % SPL
                hi = whi[:, s, :].rearrange("p (k n) -> p k n", k=2)
                lo = wlo[:, s, :].rearrange("p (k n) -> p k n", k=2)
                for tt in range(TT):
                    ts = slice(tt * P, (tt + 1) * P)
                    for nh in range(2):
                        o = acc[:, 4 + 2 * tt + nh, :]
                        ns = slice(nh * 512, (nh + 1) * 512)
                        for k in range(2):
                            sh, sl = sT_hi[:, kts[k], ts], sT_lo[:, kts[k], ts]
                            nc.tensor.matmul(o, sh, hi[:, k, ns], start=start and k == 0, stop=False)
                            nc.tensor.matmul(o, sh, lo[:, k, ns], start=False, stop=False)
                            ins = nc.tensor.matmul(o, sl, hi[:, k, ns], start=False, stop=stop and k == 1)
                        if stop and tt + nh < 2:
                            ins.then_inc(y_ps, 1)
                ins.then_inc(chunk_used, 1)

            pe.wait_ge(consts_ready, 2)
            pe.wait_ge(c_landed, 16)
            nc.tensor.transpose(acc[:, 7, 0:KD], rowsC[:, :], ident[0:KD, 0:KD]).then_inc(c_ps, 1)
            pe.wait_ge(params_landed, 16 * N_PARAMS)
            nc.tensor.transpose(acc[:, 4, 0:A_N], rowsA[0:A_N, :], ident[0:A_N, 0:A_N])
            nc.tensor.transpose(acc[:, 5, 0:B_N], rowsB[0:B_N, :], ident[0:B_N, 0:B_N]).then_inc(cols_ready, 1)

            def sum_modulation(l, part):
                pe.wait_ge(ada_ready, 2 * l + part)
                b = 4 if part else 0
                for j in (range(0, 16) if part == 0 else range(16, 24)):
                    ins = nc.tensor.matmul(acc[:, b, j:j + 1], acc_ada[:, j * P:(j + 1) * P], ones[:, 0:1],
                                           start=True, stop=True)
                ins.then_inc(mod_ps, 1)

            for r in range(8):
                pe.wait_ge(raw_done, r + 1)
                for j in (2 * r, 2 * r + 1):
                    ins = nc.tensor.matmul(acc[:, 6, j:j + 1], acc_ada[:, j * P:(j + 1) * P], ones[:, 0:1],
                                           start=True, stop=True)
                if r == 4:
                    turn(0)
            ins.then_inc(mod_ps, 1)
            n_s = n_proj = 0
            for l in range(2):
                if l:
                    turn(l)
                for n, c in enumerate(IN1_ORDER):
                    w = w_at[("in1", l, c)]
                    chunk_ready(w)
                    if n >= 4:
                        pe.wait_ge(proj_ready, n_proj + n - 3)
                    cols_by_tokens(w, n % 4, first=l if n == 0 else None)
                    if n == 6:
                        pe.wait_ge(wsmall_landed, 48)
                        pe.wait_ge(pooled_ready, l + 1)
                        for g in range(4):
                            ins = nc.tensor.matmul(acc[:, 6 + g // 2, (g % 2) * T:(g % 2) * T + T], wpool[:, l, g, :],
                                                   pool_b[:, g, :], start=True, stop=True)
                        ins.then_inc(mixed_ps, 1)
                    if n == 5:
                        sum_modulation(l, 1)
                    if n == 10:
                        pe.wait_ge(diag_ready, 3 * (l + 1) if l == 0 else 6)
                        for nh in range(2):
                            ins = nc.tensor.matmul(acc[:, 4 + nh, :], ones[:, :], diag[:, nh * 512:(nh + 1) * 512],
                                                   start=True, stop=True)
                        ins.then_inc(gate_ps, 1)
                n_proj += 12
                pe.wait_ge(gate_sb, l + 1)
                for n, c in enumerate(OUT1_ORDER):
                    w = w_at[("out1", l, c)]
                    chunk_ready(w)
                    pe.wait_ge(s_ready, n_s + n + 1)
                    out_chunk(w, [2 * c, 2 * c + 1], n == 0, n == 3)
                n_s += 4
                if l == 0:
                    sum_modulation(1, 0)

            def ffn(q, n_s):
                f = CONV_FFN[q]
                turn(f)
                w0 = w_at[("fin", q, 0, 0)]

                def in_chunk(j, half, it=0):
                    w = w0 + pair_at(j) + half
                    chunk_ready(w, it)
                    pe.wait_ge(gated if half else silu_ready, it * 2 + (NPAIR * q + j))
                    cols_by_tokens(w, (2 * j + half) % 4, first=f if j + half == 0 else None)

                def down(j, it=0):
                    w = w0 + 3 * j + 4 if j < NPAIR - 1 else w0 + 32
                    chunk_ready(w, it)
                    pe.wait_ge(s_ready, it * 2 + (n_s + j + 1))
                    out_chunk(w, [2 * (j % 2), 2 * (j % 2) + 1], j == 0, j == NPAIR - 1)

                for j in range(2):
                    in_chunk(j, 0)
                    in_chunk(j, 1)
                    if j:
                        down(0)
                with pe.Fori(0, 4) as it:
                    for j in (2, 3):
                        in_chunk(j, 0, it)
                        in_chunk(j, 1, it)
                        down(j - 1, it)
                in_chunk(10, 0)
                in_chunk(10, 1)
                down(9)
                down(10)

            def scores(i):
                s = att_steps[i]
                b = 2 * (i % 2)
                n = nk(s)
                if s[0] == "cmp":
                    pe.wait_ge(cmp_sb, 3)
                    for p4 in range(4):
                        pair = 4 * s[1] + p4
                        ins = nc.tensor.matmul(acc[:, b, p4 * 2 * n:(p4 + 1) * 2 * n],
                                               qT[:, pair, s[2] * P:(s[2] + 1) * P], kblk[:, pair // 2, :],
                                               start=True, stop=True)
                    ins.then_inc(qk_ps, 1)
                    return
                for m in range(4):
                    if s[0] == "diff":
                        tt = s[2]
                        e, slot = m % 2, m // 2
                        h = 2 * s[1] + slot
                        q, k = qT[e * DH:(e + 1) * DH, h, tt * P:(tt + 1) * P], kT[e * DH:(e + 1) * DH, h, 0:n]
                        o = acc[:, b + e, slot * T:slot * T + n]
                    else:
                        tt, h = s[2], 4 * s[1] + m
                        e, slot = m % 2, m // 2
                        br = 0 if s[0] == "sel" else 4
                        q, k = qT[e * DH:(e + 1) * DH, h // 2, tt * P:(tt + 1) * P], \
                            kT[e * DH:(e + 1) * DH, br + s[1], 0:n]
                        o = acc[:, b + e, slot * T:slot * T + n]
                    ins = nc.tensor.matmul(o, q, k, start=True, stop=True)
                ins.then_inc(qk_ps, 1)

            def turn_probs(i):
                s = att_steps[i]
                b = i % 3
                n = nk(s)
                if s[0] == "cmp":
                    ins = nc.tensor.transpose(acc[0:8 * NCMP, 4, 0:P], sc[:, b, 0:8 * n], ident[:, :])
                else:
                    blocks = s[2] + 1
                    for m in range(2 if s[0] == "diff" else 4):
                        for kt in range(blocks):
                            at = (m + 2 * kt if s[0] == "diff" else m + 4 * kt) * P
                            ins = nc.tensor.transpose(acc[:, 4 + at // 512, at % 512:at % 512 + P],
                                                      sc[:, b, m * n + kt * P:m * n + (kt + 1) * P], ident[:, :])
                ins.then_inc(probs_turned, 1)

            def values(i):
                s = att_steps[i]
                b = i % 2
                O = acc[:, 6 + i % 2, :]
                if s[0] == "cmp":
                    pe.wait_ge(vblk_ready, 2)
                    ins = nc.tensor.matmul(O, pT[0:8 * NCMP, b, 0:P], vblk[:, s[1], :], start=True, stop=True)
                else:
                    blocks = s[2] + 1
                    diff = s[0] == "diff"
                    for m in range(2 if diff else 4):
                        for kt in range(blocks):
                            at = (m + 2 * kt if diff else m + 4 * kt) * P
                            if diff:
                                v = pd[:, kt, 2 * D + (2 * s[1] + m) * P:2 * D + (2 * s[1] + m + 1) * P]
                                o = O[:, m * P:(m + 1) * P]
                            else:
                                c0 = (1792 if s[0] == "sel" else 2304) + s[1] * DH
                                v = pj[:, kt, c0:c0 + DH]
                                o = O[:, m * DH:(m + 1) * DH]
                            ins = nc.tensor.matmul(o, pT[:, b, at:at + P], v, start=kt == 0, stop=kt == blocks - 1)
                ins.then_inc(pv_ps, 1)

            def attention(first, last):
                n_mixed = 0 if first == 0 else 4
                for i in range(first, last + 3):
                    if i < last:
                        if i >= first + 2:
                            pe.wait_ge(scored, i - 1)
                        scores(i)
                    if first + 2 <= i < last + 2:
                        j = i - 2
                        s = att_steps[j]
                        pe.wait_ge(probs, j + 1)
                        if s[0] in ("cmp", "diff"):
                            n_mixed += 1
                            pe.wait_ge(mixed, n_mixed)
                        if j > first:
                            pe.wait_ge(pT_act, j)
                        turn_probs(j)
                    if i >= first + 3:
                        j = i - 3
                        pe.wait_ge(pT_act, j + 1)
                        if j >= first + 2:
                            pe.wait_ge(combined, j - 1)
                        values(j)

            ffn(0, n_s)
            n_s += NPAIR
            turn(CONV_NSA)
            for n, c in enumerate(NSA_ORDER):
                w = w_at[("nsa", c)]
                chunk_ready(w)
                if n >= 4:
                    pe.wait_ge(proj_ready, n_proj + n - 3)
                tokens_by_cols(w, n % 4, NGATE if c == 10 else CC, first=CONV_NSA if n == 0 else None)
                if n == 3:
                    for kv in range(2):
                        pe.wait_ge(proj_ready, n_proj + kv + 1)
                        for h in range(HKV):
                            for tt in range(TT):
                                src = xn[:, tt, (4 * kv + h) * P:(4 * kv + h + 1) * P]
                                ins = nc.tensor.transpose(
                                    acc[:, 4 + 2 * kv + h // 2, (h % 2) * T + tt * P:(h % 2) * T + tt * P + P],
                                    src, ident[:, :])
                            if h % 2 == 1:
                                ins.then_inc(kc_ps, 1)
            n_proj += 11

            pe.wait_ge(cmpr_ready, 2)
            for kv in range(2):
                for half in range(2):
                    w = w_at[("cmp", kv, half)]
                    chunk_ready(w)
                    hi = whi[:, w % SPL, :].rearrange("p (k n) -> p k n", k=8)
                    lo = wlo[:, w % SPL, :].rearrange("p (k n) -> p k n", k=8)
                    o = acc[:, 4 + kv, 0:CMP_HIDDEN]
                    for k in range(8):
                        m = 8 * half + k
                        c0 = (CMP_TILES * kv + m) * HKV * NCMP
                        bh, bl = (v[:, c0:c0 + P] for v in cmp_flat)
                        nc.tensor.matmul(o, bh, hi[:, k, :], start=m == 0, stop=False)
                        nc.tensor.matmul(o, bh, lo[:, k, :], start=False, stop=False)
                        ins = nc.tensor.matmul(o, bl, hi[:, k, :], start=False, stop=m == 15)
                    ins.then_inc(chunk_used, 1)

            def turn_heads(src, bank, pair, tt):
                return nc.tensor.transpose(acc[:, bank, (pair % 2) * T + tt * P:(pair % 2) * T + tt * P + P], src,
                                           ident[:, :])

            pe.wait_ge(qn_ready, 6)
            pe.wait_ge(proj_ready, n_proj)
            for pair in range(8):
                for tt in range(TT):
                    ins = turn_heads(pj[:, tt, pair * P:(pair + 1) * P], pair // 2, pair, tt)
                if pair % 2 == 1:
                    ins.then_inc(qk_turned, 1)

            def turn_keys(b):
                for h in range(HKV):
                    k = 4 * b + h
                    if h % 2 == 0:
                        pe.wait_ge(qk_dve if (k // 2) % 2 else qk_act, k // 4 + 1)
                    for tt in range(TT):
                        ins = turn_heads(xn[:, tt, k * P:(k + 1) * P], k // 2, k, tt)
                    if h % 2 == 1:
                        ins.then_inc(qk_turned, 1)

            rows = HKV * NCMP
            pe.wait_ge(gelu_ready, 2)
            for kv in range(2):
                for ct in range(2):
                    ins = nc.tensor.transpose(acc[:, 6, (2 * kv + ct) * rows:(2 * kv + ct + 1) * rows],
                                              cmp_gt[:, kv, ct * P:(ct + 1) * P], ident[0:rows, 0:rows])
            ins.then_inc(g_turned, 1)
            turn_keys(0)
            pe.wait_ge(g_sb, 1)
            pe.wait_ge(wsmall_landed, 48)
            for kv, done in ((0, cmpk_ps), (1, cmpv_ps)):
                for ct in range(2):
                    ins = nc.tensor.matmul(acc[0:rows, 4 + kv, 0:DH], cmp_g[:, kv, ct, :], w2[:, kv, ct, :],
                                           start=ct == 0, stop=ct == 1)
                ins.then_inc(done, 1)
            turn_keys(1)
            pe.wait_ge(cmp_sb, 1)
            pe.wait_ge(bias_ready, 1)
            for f in range(2):
                ins = nc.tensor.matmul(acc[0:8 * NCMP, 7, f * DH:(f + 1) * DH], sel[:, f, :], v60, start=True,
                                       stop=True)
            ins.then_inc(vsel_ps, 1)
            pe.wait_ge(kcn_ready, 2)
            nc.tensor.transpose(acc[:, 4, P:P + rows], kcn.rearrange("p c d -> p (c d)"), ident[0:rows, 0:rows])\
              .then_inc(kcn_ps, 1)
            pe.wait_ge(qk_act, 4)
            pe.wait_ge(qk_dve, 4)
            attention(0, NS)
            turn(CONV_NSA_O)
            for n in range(4):
                w = w_at[("nsao", n)]
                chunk_ready(w)
                pe.wait_ge(feat_ready, 8 * CONV_NSA_O + 2 * n + 2)
                out_chunk(w, [2 * n, 2 * n + 1], n == 0, n == 3)
            ffn(1, n_s)
            n_s += NPAIR
            ffn(2, n_s)
            n_s += NPAIR
            turn(CONV_DIFF)
            for n in range(12):
                w = w_at[("diff", n)]
                chunk_ready(w)
                if n >= 4:
                    pe.wait_ge(proj_ready, n_proj + n - 3)
                tokens_by_cols(w, n % 4, first=CONV_DIFF if n == 0 else None)
            n_proj += 12
            pe.wait_ge(qn_ready, 8)
            for bank in DIFF_BANKS:
                if bank < 4:
                    pe.wait_ge(proj_ready, n_proj - 3 + bank)
                for pair in (2 * bank, 2 * bank + 1):
                    for tt in range(TT):
                        ins = turn_heads(pd[:, tt, pair * P:(pair + 1) * P], bank, pair, tt)
                ins.then_inc(qk_turned, 1)
            pe.wait_ge(qk_act, 8)
            pe.wait_ge(qk_dve, 8)
            attention(NS, NA)
            turn(CONV_DIFF_O)
            for n in range(4):
                w = w_at[("diffo", n)]
                chunk_ready(w)
                pe.wait_ge(feat_ready, 8 * CONV_DIFF_O + 2 * n + 2)
                out_chunk(w, [2 * n, 2 * n + 1], n == 0, n == 3)
            ffn(3, n_s)


N_PARAMS = 18


_USED = ["x", "c", "w_ada", "b_ada", "g_pre", "w_in", "w_conv", "w_pool", "pool_scale", "w_out", "g_post",
         "ffn1_norm_2", "ffn1_w_in_2", "ffn1_w_out_2", "mix_norm_2", "ffn2_norm_2", "ffn2_w_in_2", "ffn2_w_out_2",
         "nsa_w_in_2", "nsa_w_out_2", "nsa_q_norm_2", "nsa_k_norm_2", "nsa_cmp_pos_2", "nsa_cmp_w1_2",
         "nsa_cmp_w2_2", "diff_w_in_2", "diff_w_out_2", "diff_q_norm_2", "diff_k_norm_2", "diff_lambda_2",
         "diff_subln_2"]


def kernel(**inputs):
    import numpy as _np
    import concourse.bacc as _bacc
    from concourse import mybir as _mybir
    from concourse.bass_utils import run_bass_kernel_spmd as _run

    nc = _bacc.Bacc("TRN2", target_bir_lowering=False, num_devices=1)
    arrays, args = {}, {}
    for name in _USED:
        arr = _np.ascontiguousarray(inputs[name])
        arrays[f"in_{name}_dram"] = arr
        args[name] = nc.dram_tensor(f"in_{name}_dram", arr.shape, _mybir.dt.from_np(arr.dtype),
                                    kind="ExternalInput").ap()
    out = nc.dram_tensor("out_dram", (1, T, D), F32, kind="ExternalOutput").ap()
    two_blocks_kernel(nc, args, out)
    r = _run(nc, [arrays], core_ids=[0])
    return r.results[0]["out_dram"]
```
